# Optimizing a Trainium2 kernel written in Bass

```python
import jax
import jax.numpy as jnp
from jax import lax
import numpy as np

D_MODEL = 1024
BATCH = 1
SEQ = 1024
DEPTH = 1

BRANCH_WIDTH = D_MODEL // 2
N_BRANCHES = 3
GM_CHUNK = 128
GM_GROUPS = 8
GM_GROUP_DIM = BRANCH_WIDTH // GM_GROUPS
DN_HEADS = 4
DN_HEAD_DIM = BRANCH_WIDTH // DN_HEADS
DN_CHUNK = 64
CONV_WIDTH = 4
SB_HEADS = 8
SB_HEAD_DIM = BRANCH_WIDTH // SB_HEADS
SB_BLOCK = 128
D_FF = 4 * D_MODEL
NORM_EPS = 1e-6
PROJ_SIZES = (BRANCH_WIDTH, BRANCH_WIDTH, BRANCH_WIDTH, BRANCH_WIDTH, BRANCH_WIDTH, BRANCH_WIDTH, DN_HEADS, DN_HEADS, BRANCH_WIDTH, BRANCH_WIDTH, BRANCH_WIDTH, N_BRANCHES * D_MODEL)
P_IN = 9 * BRANCH_WIDTH + 2 * DN_HEADS + N_BRANCHES * D_MODEL

kernel_name = "hybrid_gated_gmlp_deltanet_stickbreaking"

def rms_norm(x, g):
    xf = x.astype(jnp.float32)
    y = xf * lax.rsqrt(jnp.mean(xf * xf, axis=-1, keepdims=True) + NORM_EPS)
    return (y * g.astype(jnp.float32)).astype(x.dtype)

def layer_norm(x, g, b):
    xf = x.astype(jnp.float32)
    xc = xf - jnp.mean(xf, axis=-1, keepdims=True)
    y = xc * lax.rsqrt(jnp.mean(xc * xc, axis=-1, keepdims=True) + NORM_EPS)
    return (y * g.astype(jnp.float32) + b.astype(jnp.float32)).astype(x.dtype)

def l2_normalize(x):
    xf = x.astype(jnp.float32)
    return xf * lax.rsqrt(jnp.sum(xf * xf, axis=-1, keepdims=True) + NORM_EPS)

def split_columns(p):
    idx = []
    off = 0
    for s in PROJ_SIZES[:-1]:
        off += s
        idx.append(off)
    return jnp.split(p, idx, axis=-1)

def chunked_spatial_gating(u, v, w_s, b_s):
    bsz, s, _ = u.shape
    n = s // GM_CHUNK
    vh = v.reshape(bsz, n, GM_CHUNK, GM_GROUPS, GM_GROUP_DIM)
    causal = jnp.tril(jnp.ones((GM_CHUNK, GM_CHUNK), dtype=bool))
    w = jnp.where(causal[None], w_s, 0).astype(v.dtype)
    mixed = jnp.einsum('gts,bnsgc->bntgc', w, vh) + b_s.T.astype(v.dtype)[:, :, None]
    return u * mixed.reshape(bsz, s, BRANCH_WIDTH)

def causal_depthwise_conv(x, w):
    c = x.shape[-1]
    return lax.conv_general_dilated(
        x, w.astype(x.dtype)[:, None, :], window_strides=(1,),
        padding=[(CONV_WIDTH - 1, 0)], dimension_numbers=('NWC', 'WIO', 'NWC'),
        feature_group_count=c)

def gated_delta_rule(q, k, v, beta, g):
    f32 = jnp.float32
    bsz, s, h, dk = q.shape
    dv = v.shape[-1]
    c = DN_CHUNK
    n = s // c
    q = q.astype(f32) * (dk ** -0.5)

    def to_chunks(t):
        return t.astype(f32).reshape(bsz, n, c, h, -1).transpose(0, 3, 1, 2, 4)

    qc, kc, vc = to_chunks(q), to_chunks(k), to_chunks(v)
    bc = beta.astype(f32).reshape(bsz, n, c, h).transpose(0, 3, 1, 2)
    gcum = lax.cumsum(g.astype(f32).reshape(bsz, n, c, h).transpose(0, 3, 1, 2), axis=3)
    tri = jnp.tril(jnp.ones((c, c), dtype=bool))
    strict = jnp.tril(jnp.ones((c, c), dtype=bool), -1)
    decay = jnp.exp(jnp.where(tri, gcum[..., :, None] - gcum[..., None, :], -jnp.inf))
    kk = jnp.einsum('bhnid,bhnjd->bhnij', kc, kc)
    a_strict = jnp.where(strict, bc[..., :, None] * kk * decay, 0.0)
    lhs = a_strict + jnp.eye(c, dtype=f32)
    rhs = jnp.concatenate([vc * bc[..., None], kc * (bc * jnp.exp(gcum))[..., None]], axis=-1)
    sol = lax.linalg.triangular_solve(lhs, rhs, left_side=True, lower=True, unit_diagonal=True)
    u_val, w_kd = sol[..., :dv], sol[..., dv:]
    qk = jnp.where(tri, jnp.einsum('bhnid,bhnjd->bhnij', qc, kc) * decay, 0.0)
    q_dec = qc * jnp.exp(gcum)[..., None]
    g_last = gcum[..., -1]
    k_tail = kc * jnp.exp(g_last[..., None] - gcum)[..., None]

    def step(state, inp):
        u_i, w_i, qd_i, qk_i, kt_i, gl_i = inp
        v_new = u_i - jnp.einsum('bhcd,bhde->bhce', w_i, state)
        o = jnp.einsum('bhcd,bhde->bhce', qd_i, state) + jnp.einsum('bhcj,bhje->bhce', qk_i, v_new)
        state = state * jnp.exp(gl_i)[..., None, None] + jnp.einsum('bhcd,bhce->bhde', kt_i, v_new)
        return state, o

    xs = tuple(jnp.moveaxis(t, 2, 0) for t in (u_val, w_kd, q_dec, qk, k_tail, g_last))
    s0 = jnp.zeros((bsz, h, dk, dv), f32)
    _, o = lax.scan(step, s0, xs)
    return o.transpose(1, 0, 3, 2, 4).reshape(bsz, s, h, dv)

def stick_breaking_attention(q, k, v):
    f32 = jnp.float32
    bsz, s, h, dh = q.shape
    nb = s // SB_BLOCK
    qb = q.astype(f32).reshape(bsz, nb, SB_BLOCK, h, dh).transpose(1, 0, 2, 3, 4)
    kf = k.astype(f32)
    vf = v.astype(f32)
    kpos = jnp.arange(s)
    scale = dh ** -0.5

    def block(args):
        qi, i = args
        z = jnp.einsum('bthd,bshd->bhts', qi, kf) * scale
        tpos = i * SB_BLOCK + jnp.arange(SB_BLOCK)
        causal = kpos[None, :] < tpos[:, None]
        log_keep = jnp.where(causal, jax.nn.log_sigmoid(-z), 0.0)
        later = lax.cumsum(log_keep, axis=3, reverse=True) - log_keep
        w = jnp.where(causal, jnp.exp(jax.nn.log_sigmoid(z) + later), 0.0)
        return jnp.einsum('bhts,bshd->bthd', w, vf)

    o = lax.map(block, (qb, jnp.arange(nb)))
    return o.transpose(1, 0, 2, 3, 4).reshape(bsz, s, h * dh).astype(q.dtype)

def setup_inputs(seed: int = 0) -> dict:
    key = jax.random.key(seed)
    ks = jax.random.split(key, 16)
    f32 = jnp.float32
    nrm = lambda k, shp: jax.random.normal(k, shp, f32)
    x = nrm(ks[0], (BATCH, SEQ, D_MODEL))
    norm_g = 1.0 + 0.05 * nrm(ks[1], (DEPTH, 4, D_MODEL))
    w_in = nrm(ks[2], (DEPTH, D_MODEL, P_IN)) * D_MODEL ** -0.5
    b_in = 0.01 * nrm(ks[3], (DEPTH, P_IN))
    sgu_ln_g = 1.0 + 0.05 * nrm(ks[4], (DEPTH, BRANCH_WIDTH))
    sgu_ln_b = 0.01 * nrm(ks[5], (DEPTH, BRANCH_WIDTH))
    w_spatial = nrm(ks[6], (DEPTH, GM_GROUPS, GM_CHUNK, GM_CHUNK)) * GM_CHUNK ** -0.5
    b_spatial = 1.0 + 0.05 * nrm(ks[7], (DEPTH, GM_GROUPS, GM_CHUNK))
    conv_w = nrm(ks[8], (DEPTH, CONV_WIDTH, 3 * BRANCH_WIDTH)) * CONV_WIDTH ** -0.5
    a_log = jnp.log(jax.random.uniform(ks[9], (DEPTH, DN_HEADS), f32, 1.0, 16.0))
    dt = jnp.exp(jax.random.uniform(ks[10], (DEPTH, DN_HEADS), f32, float(np.log(1e-3)), float(np.log(1e-1))))
    dt_bias = dt + jnp.log(-jnp.expm1(-dt))
    dn_norm_g = 1.0 + 0.05 * nrm(ks[11], (DEPTH, DN_HEAD_DIM))
    w_branch = nrm(ks[12], (DEPTH, N_BRANCHES, BRANCH_WIDTH, D_MODEL)) * BRANCH_WIDTH ** -0.5
    w_out = nrm(ks[13], (DEPTH, D_MODEL, D_MODEL)) * D_MODEL ** -0.5
    w_ff1 = nrm(ks[14], (DEPTH, D_MODEL, D_FF)) * D_MODEL ** -0.5
    w_ff2 = nrm(ks[15], (DEPTH, D_FF, D_MODEL)) * D_FF ** -0.5
    return {"x": x, "norm_g": norm_g, "w_in": w_in, "b_in": b_in,
            "sgu_ln_g": sgu_ln_g, "sgu_ln_b": sgu_ln_b, "w_spatial": w_spatial, "b_spatial": b_spatial,
            "conv_w": conv_w, "a_log": a_log, "dt_bias": dt_bias, "dn_norm_g": dn_norm_g,
            "w_branch": w_branch, "w_out": w_out, "w_ff1": w_ff1, "w_ff2": w_ff2}

def reference(x, norm_g, w_in, b_in, sgu_ln_g, sgu_ln_b, w_spatial, b_spatial, conv_w, a_log, dt_bias, dn_norm_g, w_branch, w_out, w_ff1, w_ff2):
    bsz, s, _ = x.shape
    for l in range(DEPTH):
        h = rms_norm(x, norm_g[l, 0])
        p = h @ w_in[l] + b_in[l]
        (a_u, a_v, b_q, b_k, b_v, b_z, b_beta, b_dec, c_q, c_k, c_v, gates) = split_columns(p)

        a_u = jax.nn.gelu(a_u, approximate=False)
        a_v = layer_norm(jax.nn.gelu(a_v, approximate=False), sgu_ln_g[l], sgu_ln_b[l])
        y_a = chunked_spatial_gating(a_u, a_v, w_spatial[l], b_spatial[l])

        qkv = jax.nn.silu(causal_depthwise_conv(jnp.concatenate([b_q, b_k, b_v], axis=-1), conv_w[l]))
        dq, dk_, dv_ = jnp.split(qkv, 3, axis=-1)
        dq = l2_normalize(dq.reshape(bsz, s, DN_HEADS, DN_HEAD_DIM))
        dk_ = l2_normalize(dk_.reshape(bsz, s, DN_HEADS, DN_HEAD_DIM))
        dv_ = dv_.reshape(bsz, s, DN_HEADS, DN_HEAD_DIM)
        beta = jax.nn.sigmoid(b_beta.astype(jnp.float32))
        g = -jnp.exp(a_log[l].astype(jnp.float32)) * jax.nn.softplus(b_dec.astype(jnp.float32) + dt_bias[l].astype(jnp.float32))
        o = gated_delta_rule(dq, dk_, dv_, beta, g).astype(x.dtype)
        o = rms_norm(o, dn_norm_g[l]) * jax.nn.silu(b_z.reshape(bsz, s, DN_HEADS, DN_HEAD_DIM))
        y_b = o.reshape(bsz, s, BRANCH_WIDTH)

        y_c = stick_breaking_attention(c_q.reshape(bsz, s, SB_HEADS, SB_HEAD_DIM),
                                       c_k.reshape(bsz, s, SB_HEADS, SB_HEAD_DIM),
                                       c_v.reshape(bsz, s, SB_HEADS, SB_HEAD_DIM))

        branches = jnp.stack([y_a, y_b, y_c], axis=0)
        proj = jnp.einsum('nbsw,nwd->bsnd', branches, w_branch[l])
        gate = jax.nn.sigmoid(gates.reshape(bsz, s, N_BRANCHES, D_MODEL))
        mixed = jnp.sum(gate * proj, axis=2) @ w_out[l]
        x = x + rms_norm(mixed, norm_g[l, 1])

        h = rms_norm(x, norm_g[l, 2])
        f = jnp.square(jax.nn.relu(h @ w_ff1[l])) @ w_ff2[l]
        x = x + rms_norm(f, norm_g[l, 3])
    return x


_drawn_inputs = setup_inputs


def setup_inputs(seed=0):
    import zlib

    import numpy as np

    out = dict(_drawn_inputs(seed))
    spreads = {}
    factors = {'b_in': 4.605, 'sgu_ln_g': 4.056, 'sgu_ln_b': 8.0, 'b_spatial': 2.834, 'dn_norm_g': 2.815}
    for name, (base, spread) in spreads.items():
        noise = np.random.default_rng([zlib.crc32(name.encode()), seed]).standard_normal(out[name].shape)
        drawn = base * np.exp(spread * noise) if base else spread * noise
        out[name] = jnp.asarray(drawn.astype(out[name].dtype))
    for name, factor in factors.items():
        out[name] = (out[name] * factor).astype(out[name].dtype)
    return out
```

```python
import concourse.bass as bass
from concourse import mybir
from contextlib import ExitStack
import numpy as np

P = 128
D = 1024
S = 1024
KT = D // P
HALF = 512
BW = 512
EPS = 1e-6
NCH = S // P

PAIR_DN, N_DN = 0, 8
PAIR_SB, N_SB = 8, 6
PAIR_MIX = 14
PAIR_GATE = 22
PAIR_BR = 30
PAIR_OUT = 36
PAIR_FF = 40
N_PAIRS = 72
ROW_DQ, ROW_DK, ROW_DV, ROW_DZ = 0, 4, 8, 12
ROW_SQ, ROW_SK, ROW_SV = 16, 20, 24
COL_AU, COL_AV, COL_DQ, COL_BETA, COL_SQ = 0, 512, 1024, 3072, 3080
COL_GATE = 4616

C_ID, C_ONE, C_UPI, C_UPS, C_LOI, C_LEV = 0, 1, 2, 3, 4, 5
N_LEV = 7
N_CONST = C_LEV + N_LEV

V_NORM = 0
V_BIN = V_NORM + 32
V_LNG = V_BIN + 60
V_LNB = V_LNG + 4
V_CONV = V_LNB + 4
V_DNG = V_CONV + 48
V_ALOG = V_DNG + 1
V_DTB = V_ALOG + 4
V_BBD = V_DTB + 4
V_BSP = V_BBD + 8
N_COLS = V_BSP + 4 * P


def gate_row(branch, pair):
    if branch == 0:
        return 2 * (PAIR_MIX + 1) + 4 * pair
    return 2 * PAIR_GATE + 8 * (branch - 1) + 2 * pair


def hybrid_decoder_layer(nc, xT, w_stream, w_bd, w_spT, cols_in, consts_in, outT):
    f32, f32r = mybir.dt.float32, mybir.dt.float32r
    ACT, ALU = mybir.ActivationFunctionType, mybir.AluOpType
    ds = bass.ds

    pT = nc.dram_tensor("projections", (60, P, S), f32, kind="Internal").ap()
    yT = nc.dram_tensor("branch_outputs", (12, P, S), f32, kind="Internal").ap()
    x1T = nc.dram_tensor("residual", (KT, P, S), f32, kind="Internal").ap()

    top = ExitStack()
    scope = [top]

    def sb(name, shape, dt=f32):
        return scope[0].enter_context(nc.sbuf_tensor(name, shape, dt))

    def sem(name):
        return top.enter_context(nc.semaphore(name))

    with top:
        consts = sb("consts", [P, N_CONST, P])
        cols = sb("cols", [P, N_COLS])
        ident, ones = consts[:, C_ID, :], consts[:, C_ONE, :]
        up_incl, up_strict, lo_incl = consts[:, C_UPI, :], consts[:, C_UPS, :], consts[:, C_LOI, :]
        w_raw = [sb(f"w_raw{s}", [P, KT * P]) for s in range(2)]
        w_hi = [sb(f"w_hi{s}", [P, KT, P], f32r) for s in range(2)]
        w_lo = [sb(f"w_lo{s}", [P, KT, P], f32r) for s in range(2)]
        act_hi = sb("act_hi", [P, KT, S], f32r)
        act_lo = sb("act_lo", [P, KT, S], f32r)
        bd_g = sb("bd_g", [P, 4, NCH])
        bd_beta = sb("bd_beta", [P, 4, NCH])
        bd_gc = sb("bd_gc", [P, 4, NCH])
        bd_egc = sb("bd_egc", [P, 4, NCH])

        scope[0] = ExitStack()
        with scope[0]:
            x_sb = sb("x_sb", [P, KT, S])
            sq0 = [sb(f"sq0_{s}", [P, S]) for s in range(2)]
            rstd0 = sb("rstd0", [P, S])
            hbuf = [sb(f"hbuf{s}", [P, S]) for s in range(2)]
            wbd = sb("wbd", [P, KT, 8])
            wbd_hi = sb("wbd_hi", [P, KT, 8], f32r)
            wbd_lo = sb("wbd_lo", [P, KT, 8], f32r)
            bd = sb("bd", [P, NCH, 8])
            bt = [sb(f"bt{s}", [P, 4, NCH]) for s in range(5)]

        scope[0] = ExitStack()
        with scope[0]:
            stage = [sb(f"stage{s}", [P, S]) for s in range(2)]
            d_in = [sb(f"d_in{s}", [P, 3 + S]) for s in range(3)]
            d_z = sb("d_z", [P, S])
            d_cv = [sb(f"d_cv{s}", [P, S]) for s in range(3)]
            d_gB = sb("d_gB", [P, NCH, P])
            d_bB = sb("d_bB", [P, NCH, P])
            d_eg = sb("d_eg", [P, NCH, P])
            d_dt = sb("d_dt", [P, NCH, P])
            d_at = sb("d_at", [P, NCH, P])
            d_qk = sb("d_qk", [P, NCH, P])
            d_kb = sb("d_kb", [P, NCH, P])
            d_kt = sb("d_kt", [P, NCH, P])
            d_vb = sb("d_vb", [P, NCH, P])
            d_TT = sb("d_TT", [P, NCH, P])
            d_T = sb("d_T", [P, NCH, P])
            d_wt = sb("d_wt", [P, NCH, P])
            d_tail = sb("d_tail", [P, NCH])
            d_S = sb("d_S", [P, P])
            d_vn = sb("d_vn", [P, P])
        d_X, d_B, d_r = d_gB, d_bB, d_eg
        d_o = d_cv[2]

        scope[0] = ExitStack()
        with scope[0]:
            _ = [sb(f"stage_keep{s}", [P, S]) for s in range(2)]
            a_q = sb("a_q", [P, S])
            a_k = sb("a_k", [P, 2, S])
            a_vT = sb("a_vT", [P, S])
            a_v = sb("a_v", [P, NCH, 2, P])
            a_z = [sb(f"a_z{s}", [P, HALF]) for s in range(2)]
            a_e = [sb(f"a_e{s}", [P, HALF]) for s in range(2)]
            a_sp = [sb(f"a_sp{s}", [P, HALF]) for s in range(2)]
            a_R = sb("a_R", [P, HALF])
            a_A = [sb(f"a_A{s}", [P, NCH, HALF]) for s in range(2)]
            a_y = [sb(f"a_y{s}", [P, HALF]) for s in range(2)]

        scope[0] = ExitStack()
        with scope[0]:
            g_w = sb("g_w", [P, 8, P])
            g_v = sb("g_v", [P, 4, S])
            g_u = sb("g_u", [P, 4, S])
            g_sq = [sb(f"g_sq{s}", [P, HALF]) for s in range(2)]
            g_mean = sb("g_mean", [P, S])
            g_rstd = sb("g_rstd", [P, S])
            g_vt = sb("g_vt", [P, NCH, P])
            g_n = sb("g_n", [P, S])
            g_y = [sb(f"g_y{s}", [P, S]) for s in range(2)]

        scope[0] = ExitStack()
        with scope[0]:
            y_hi = sb("y_hi", [P, 12, S], f32r)
            y_lo = sb("y_lo", [P, 12, S], f32r)
            m_acc = sb("m_acc", [P, 2, S])
            gate = [sb(f"gate{s}", [P, HALF]) for s in range(2)]
            m_t = sb("m_t", [P, HALF])

        outer = ExitStack()
        with outer:
            scope[0] = outer
            mixed = sb("mixed", [P, KT, S])
            scope[0] = ExitStack()
            with scope[0]:
                n_sq = [sb(f"n_sq{s}", [P, S]) for s in range(2)]
                n_rstd = sb("n_rstd", [P, S])
                n_x = [sb(f"n_x{s}", [P, S]) for s in range(2)]
                n_h = [sb(f"n_h{s}", [P, S]) for s in range(2)]
                x_fin = sb("x_fin", [P, KT, S])
            scope[0] = ExitStack()
            with scope[0]:
                f_hi = sb("f_hi", [P, KT, S], f32r)
                f_lo = sb("f_lo", [P, KT, S], f32r)
                f_t = [sb(f"f_t{s}", [P, HALF]) for s in range(2)]
        scope[0] = top

        def bank(name):
            return top.enter_context(nc.psum_tensor(name, [P, HALF], f32))

        g_bank = [bank("gemm0"), bank("gemm1")]
        z_bank = [bank("z0"), bank("z1")]
        c_bank = bank("cumsum")
        o_bank = bank("attn_out")
        d_bank = [bank("dn0"), bank("dn1")]

        loaded = sem("loaded")
        raw_loaded = [sem(f"raw_loaded{s}") for s in range(2)]
        hi_ready = [sem(f"hi_ready{s}") for s in range(2)]
        lo_ready = [sem(f"lo_ready{s}") for s in range(2)]
        blk_done = [sem(f"blk_done{s}") for s in range(2)]
        half_ready = sem("half_ready")
        bank_read = [sem(f"bank_read{s}") for s in range(2)]
        stored = [sem(f"stored{s}") for s in range(2)]
        staged = [sem(f"staged{s}") for s in range(2)]
        apart = sem("apart")
        phase = sem("phase")
        sq_ready, sq_used, ss_ready = sem("sq_ready"), sem("sq_used"), sem("ss_ready")
        ms_ready, root_ready, rstd_ready = sem("ms_ready"), sem("root_ready"), sem("rstd_ready")
        h_ready, hh_ready, hl_ready = sem("h_ready"), sem("hh_ready"), sem("hl_ready")
        ld = [sem(f"ld{s}") for s in range(2)]
        use = [sem(f"use{s}") for s in range(2)]
        small = sem("small")
        bd_mm = sem("bd_mm")
        dn_loaded, dn_conv, dn_silu, dn_sq = sem("dn_loaded"), sem("dn_conv"), sem("dn_silu"), sem("dn_sq")
        dn_chain = sem("dn_chain")
        dn_prod = [sem(f"dn_prod{g}") for g in range(2)]
        dn_taken = [sem(f"dn_taken{g}") for g in range(2)]
        dn_dve, dn_out = sem("dn_dve"), sem("dn_out")
        dn_eg, dn_min, dn_tt, dn_b = ([sem(f"{n}{g}") for g in range(2)] for n in ("dn_eg", "dn_min", "dn_tt", "dn_b"))
        dn_scan_mm, dn_scan_ev = sem("dn_scan_mm"), sem("dn_scan_ev")
        dn_o, dn_root, dn_yst = sem("dn_o"), sem("dn_root"), sem("dn_yst")
        dn_rcp = sem("dn_rcp")
        at_loaded, at_vt, at_v, at_iter = sem("at_loaded"), sem("at_vt"), sem("at_v"), sem("at_iter")
        z_ready, z_read, na_ready, e_ready, l_ready = (sem(n) for n in ("z_ready", "z_read", "na_ready", "e_ready", "l_ready"))
        sp_raw, sp_ready, r_ready, cum_ready, arg_ready, a_ready = (
            sem(n) for n in ("sp_raw", "sp_ready", "r_ready", "cum_ready", "arg_ready", "a_ready"))
        a_masked, av_done, av_out, av_read, y_stored = (sem(n) for n in ("a_masked", "av_done", "av_out", "av_read", "y_stored"))
        pad_zero = sem("pad_zero")
        g_load, g_chain, g_pe, g_act = sem("g_load"), sem("g_chain"), sem("g_pe"), sem("g_act")
        g_masked = sem("g_masked")
        g_out, g_store = sem("g_out"), [sem(f"g_store{s}") for s in range(2)]
        y_ld = [sem(f"y_ld{s}") for s in range(2)]
        yh_ready, yl_ready = sem("yh_ready"), sem("yl_ready")
        gate_ld = [sem(f"gate_ld{s}") for s in range(2)]
        gate_used = sem("gate_used")
        m_added, mh_ready, ml_ready = sem("m_added"), sem("mh_ready"), sem("ml_ready")
        mix_ready = sem("mix_ready")
        x_ld, x_used, x1_ready, x1_st = sem("x_ld"), sem("x_used"), sem("x1_ready"), sem("x1_st")
        n_chain = sem("n_chain")
        f_relu, f_sqr, f_hr, f_lr, f_acc = sem("f_relu"), sem("f_sqr"), sem("f_hr"), sem("f_lr"), sem("f_acc")
        out_ready, out_st = sem("out_ready"), sem("out_st")

        def tile_of(t, k):
            return t[:, ds(k, 1), :].rearrange("p k s -> p (k s)")

        def settle(eng):
            eng.sem_inc(apart, 1)

        def end_phase(eng, k):
            eng.drain().then_inc(phase, 1)
            eng.wait_ge(phase, 5 * k)

        def load_weights(sp, n, s, first=False):
            if not first:
                sp.wait_ge(lo_ready[s], n)
            sp.dma_start(w_raw[s][:], w_stream[n, s]).then_inc(raw_loaded[s], 16)

        def split_hi(act, n, s, first=False):
            act.wait_ge(raw_loaded[s], 16 * n + 16)
            if not first:
                act.wait_ge(blk_done[s], n)
            nc.scalar.activation(w_hi[s][:], w_raw[s][:].rearrange("p (k c) -> p k c", k=KT), ACT.Copy).then_inc(hi_ready[s], 1)

        def split_lo(dve, n, s):
            dve.wait_ge(hi_ready[s], n + 1)
            nc.vector.tensor_tensor(w_lo[s][:], w_raw[s][:].rearrange("p (k c) -> p k c", k=KT),
                                    w_hi[s][:].bitcast(f32), ALU.subtract).then_inc(lo_ready[s], 1)

        def product_step(pe, n, s, hf, k, a_hi, a_lo):
            if hf == 0 and k == 0:
                pe.wait_ge(lo_ready[s], n + 1)
            t = slice(HALF * hf, HALF * hf + HALF)
            nc.tensor.matmul(g_bank[hf][:], w_hi[s][:, k, :], a_hi[:, k, t], start=(k == 0), stop=False)
            nc.tensor.matmul(g_bank[hf][:], w_hi[s][:, k, :], a_lo[:, k, t], start=False, stop=False)
            last = nc.tensor.matmul(g_bank[hf][:], w_lo[s][:, k, :], a_hi[:, k, t], start=False, stop=(k == KT - 1))
            if k == KT - 1:
                last.then_inc(half_ready if hf == 0 else blk_done[s], 1)

        def product_half(pe, n, s, hf, a_hi, a_lo, fills):
            pe.wait_ge(bank_read[hf], 1 + fills)
            for k in range(KT):
                product_step(pe, n, s, hf, k, a_hi, a_lo)

        def wait_half(eng, n, s, hf, halves):
            if hf == 0:
                eng.wait_ge(half_ready, halves + 1)
            else:
                eng.wait_ge(blk_done[s], n + 1)

        def take_projection(act, n, s, hf, func):
            wait_half(act, n, s, hf, 2 * n + s)
            if hf == 0:
                act.wait_ge(stored[s], 1 + 16 * n)
            settle(act)
            nc.scalar.activation(stage[s][:, HALF * hf:HALF * hf + HALF], g_bank[hf][:], func,
                                 bias=cols[:, ds(V_BIN + 2 * n + s, 1)]).then_inc(bank_read[hf], 1)

        def store_projection(sp, n, s):
            sp.wait_ge(bank_read[0], 1 + 2 * n + s + 1)
            sp.wait_ge(bank_read[1], 1 + 2 * n + s + 1)
            sp.dma_start(pT[2 * n + s], stage[s][:]).then_inc(stored[s], 16)

        def sp_block(sp, n, s):
            load_weights(sp, n + 1, s)
            store_projection(sp, n, s)

        def act_block(act, n, s, func):
            take_projection(act, n, s, 0, func)
            take_projection(act, n, s, 1, func)
            split_hi(act, n + 1, s)

        def pe_block(pe, n, s, a_hi, a_lo, extra):
            for hf in range(2):
                product_half(pe, n, s, hf, a_hi, a_lo, 2 * n + s + extra)

        MIX_BRANCH = 12
        HALF_BRANCH = 24

        class Beside:

            def __init__(self, n0, slots):
                self.n0, self.slots, self.at = n0, slots, 0

            def steps(self, slot):
                end = 64 * (slot + 1) // self.slots
                out = range(self.at, end)
                self.at = end
                return out

        def pe_beside(pe, b, slot):
            for step in b.steps(slot):
                blk, r = divmod(step, 16)
                hf, k = divmod(r, 8)
                n, s = b.n0 + blk // 2, blk % 2
                if k == 0:
                    pe.wait_ge(bank_read[hf], 1 + 2 * n + s)
                product_step(pe, n, s, hf, k, act_hi, act_lo)

        def act_beside(act, b, slot, funcs):
            for step in b.steps(slot):
                blk, r = divmod(step, 16)
                n, s = b.n0 + blk // 2, blk % 2
                if r == 7:
                    take_projection(act, n, s, 0, funcs[blk // 2])
                if r == 15:
                    take_projection(act, n, s, 1, funcs[blk // 2])
                    split_hi(act, n + 1, s)

        def dve_beside(dve, b, slot):
            for step in b.steps(slot):
                blk, r = divmod(step, 16)
                if r == 15:
                    split_lo(dve, b.n0 + blk // 2 + 1, blk % 2)

        def norm_squares(act, i, src, buf, ready=None):
            for k in range(KT):
                if ready is not None:
                    act.wait_ge(*ready(k))
                if 8 * i + k >= 2:
                    act.wait_ge(sq_used, 8 * i + k - 1)
                nc.scalar.activation(buf[k % 2][:], src(k), ACT.Square).then_inc(sq_ready, 1)

        def norm_sums(pe, i, buf):
            for k in range(KT):
                pe.wait_ge(sq_ready, 8 * i + k + 1)
                for hf in range(2):
                    last = nc.tensor.matmul(d_bank[hf][:], ones, buf[k % 2][:, HALF * hf:HALF * hf + HALF],
                                            start=(k == 0), stop=(k == KT - 1))
                last.then_inc(sq_used, 1)

        def norm_rstd(dve, i, out):
            dve.wait_ge(sq_used, 8 * i + 8)
            for hf in range(2):
                t = slice(HALF * hf, HALF * hf + HALF)
                nc.vector.tensor_scalar(out[:, t], d_bank[hf][:], 1.0 / D, EPS, ALU.mult, ALU.add).then_inc(ms_ready, 1)
            dve.wait_ge(root_ready, i + 1)
            nc.vector.reciprocal(out[:], out[:]).then_inc(rstd_ready, 1)
            dve.wait_ge(rstd_ready, i + 1)

        def norm_root(act, i, out):
            act.wait_ge(ms_ready, 2 * i + 2)
            nc.scalar.activation(out[:], out[:], ACT.Sqrt).then_inc(root_ready, 1)

        block = top.enter_context(nc.Block())

        @block.sync
        def _(sp):
            sp.dma_start(x_sb[:], xT.rearrange("k p s -> p k s")).then_inc(loaded, 16)
            sp.dma_start(consts[:], consts_in).then_inc(loaded, 16)
            sp.dma_start(cols[:], cols_in).then_inc(loaded, 16)
            sp.dma_start(wbd[:], w_bd).then_inc(loaded, 16)
            for s in range(2):
                load_weights(sp, 0, s, first=True)
            for one in (*bank_read, *stored, dn_yst, *dn_taken, y_stored, at_iter, dn_chain, ml_ready, av_read, f_lr):
                sp.sem_inc(one, 1)
            end_phase(sp, 1)
            with sp.Fori(0, PAIR_MIX) as i:
                for s in range(2):
                    sp_block(sp, i, s)
            with sp.Fori(0, 4) as i:
                for s in range(2):
                    sp.wait_ge(stored[s], 1 + 16 * (PAIR_MIX))
                sp.wait_ge(dn_yst, 1 + 16 * i)
                for j, row in enumerate((ROW_DQ, ROW_DK, ROW_DV)):
                    sp.dma_start(d_in[j][:, 3:], pT[i + row]).then_inc(dn_loaded, 16)
                sp.dma_start(d_z[:], pT[i + ROW_DZ]).then_inc(dn_loaded, 16)
                for b in range(4):
                    sp_block(sp, PAIR_MIX + 2 * i + b // 2, b % 2)
                sp.wait_ge(dn_out, 2 * i + 2)
                sp.dma_start(yT[4 + i], d_o[:]).then_inc(dn_yst, 16)
            sp.wait_ge(dn_yst, 1 + 64)
            end_phase(sp, 2)
            with sp.Fori(0, 4) as i:
                sp.wait_ge(at_iter, 1 + i)
                sp.wait_ge(pad_zero, 2)
                sp.dma_start(a_q[:], pT[i + ROW_SQ]).then_inc(at_loaded, 16)
                for u in range(2):
                    sp.dma_start(a_k[64 * u:64 * u + 64, u, :], pT[i + ROW_SK, 64 * u:64 * u + 64]).then_inc(at_loaded, 16)
                sp.dma_start(a_vT[:], pT[i + ROW_SV]).then_inc(at_loaded, 16)
                for b in range(4):
                    sp_block(sp, PAIR_GATE + 2 * i + b // 2, b % 2)
                for T in range(2):
                    sp.wait_ge(av_read, 1 + 2 * i + T + 1)
                    sp.dma_start(yT[8 + i, :, HALF * T:HALF * T + HALF], a_y[T][:]).then_inc(y_stored, 16)
            sp.wait_ge(y_stored, 1 + 16 * 8)
            for s in range(2):
                sp.wait_ge(stored[s], 1 + 16 * PAIR_BR)
            end_phase(sp, 3)
            sp.dma_start(g_w[:], w_spT).then_inc(g_load, 16)
            for r in range(2):
                sp.dma_start(g_v[:, 2 * r:2 * r + 2, :], pT[2 * (PAIR_MIX + 4 + 2 * r):2 * (PAIR_MIX + 4 + 2 * r) + 2]
                             .rearrange("k p s -> p k s")).then_inc(g_load, 16)
            for r in range(2):
                sp.dma_start(g_u[:, 2 * r:2 * r + 2, :], pT[2 * (PAIR_MIX + 2 * r):2 * (PAIR_MIX + 2 * r) + 2]
                             .rearrange("k p s -> p k s")).then_inc(g_load, 16)
            for b in range(4):
                sp.wait_ge(g_out, b + 1)
                sp.dma_start(yT[b], g_y[b % 2][:]).then_inc(g_store[b % 2], 16)
            for s in range(2):
                sp.wait_ge(g_store[s], 32)
            end_phase(sp, 4)
            for k in range(12):
                if k >= 2:
                    sp.wait_ge(yl_ready, k - 1)
                sp.dma_start(m_acc[:, k % 2, :], yT[k]).then_inc(y_ld[k % 2], 16)
            with sp.Fori(0, 2) as i:
                for q in range(6):
                    n, s = PAIR_BR + 3 * i + q // 2, q % 2
                    load_weights(sp, n + 1, s)
                    for r in range(4):
                        dd, hf = divmod(r, 2)
                        row = gate_row(q % 3, 0) + (8 if q % 3 == 0 else 4) * i + (4 if q % 3 == 0 else 2) * (q // 3) + dd
                        sp.wait_ge(bank_read[hf], 1 + 2 * PAIR_BR + 12 * i + 2 * q + dd)
                        sp.dma_start(gate[r % 2][:], pT[row, :, HALF * hf:HALF * hf + HALF]).then_inc(gate_ld[r % 2], 16)
            end_phase(sp, 5)
            with sp.Fori(0, 4) as i:
                for s in range(2):
                    load_weights(sp, PAIR_OUT + i + 1, s)
            for k in range(KT):
                if k >= 2:
                    sp.wait_ge(x1_ready, k - 1)
                sp.dma_start(n_x[k % 2][:], xT[k]).then_inc(ld[k % 2], 16)
            for k in range(KT):
                sp.wait_ge(x1_ready, k + 1)
                sp.dma_start(x1T[k], mixed[:, k, :]).then_inc(x1_st, 16)
            sp.wait_ge(x1_st, 16 * KT)
            end_phase(sp, 6)
            with sp.Fori(PAIR_FF, N_PAIRS - 1) as n:
                for s in range(2):
                    load_weights(sp, n + 1, s)
            end_phase(sp, 7)
            sp.dma_start(x_fin[:], x1T.rearrange("k p s -> p k s")).then_inc(x_ld, 16)
            for k in range(KT):
                sp.wait_ge(out_ready, k + 1)
                sp.dma_start(outT[k], x_fin[:, k, :]).then_inc(out_st, 16)
            sp.wait_ge(out_st, 16 * KT)

        STEPS = [(T, u, j) for T in range(2) for u in range(2) for j in range(4 * T + 3, -1, -1)]
        NST = len(STEPS)

        def first_col(T, j):
            return max(0, P * j - HALF * T)

        def group_of(x):
            T, u, j = STEPS[x]
            return 2 * T + u, j == 4 * T + 3, j == 0

        def is_diag(T, j):
            return j >= 4 * T

        DIAGS = [sum(is_diag(STEPS[y][0], STEPS[y][2]) for y in range(x + 1)) for x in range(NST)]
        N_DIAG = DIAGS[-1]
        R_BEFORE = [sum(not group_of(y)[2] for y in range(x)) for x in range(NST)]
        N_R = NST - 4

        DN_STAGES = ["rowg", "rowb", "gram", "qk", "kT", "vT", "t0"]
        for lev in range(1, N_LEV):
            DN_STAGES += [f"x{lev}", f"y{lev}"] + ([f"t{lev}"] if lev < N_LEV - 1 else [])
        DN_STAGES += ["w"]
        NDS = len(DN_STAGES)
        DN_USES = NDS + 3
        DVE_CHAIN = 8
        DN_SLOTS = 2 + 2 * NDS + 2 * NCH + 2

        @block.scalar
        def _(act):
            act.wait_ge(loaded, 64)
            nc.scalar.activation(wbd_hi[:], wbd[:], ACT.Copy).then_inc(small, 1)
            for s in range(2):
                split_hi(act, 0, s, first=True)
            norm_squares(act, 0, lambda k: x_sb[:, k, :], sq0)
            norm_root(act, 0, rstd0)
            for k in range(KT):
                act.wait_ge(h_ready, k + 1)
                nc.scalar.activation(act_hi[:, k, :], hbuf[k % 2][:], ACT.Copy).then_inc(hh_ready, 1)
            act.wait_ge(small, 3)
            nc.scalar.activation(bd_beta[:], bd[:, :, 0:4].rearrange("p n h -> p h n"), ACT.Sigmoid).then_inc(small, 1)
            act.wait_ge(small, 6)
            nc.scalar.activation(bt[2][:], bt[1][:], ACT.Exp).then_inc(small, 1)
            act.wait_ge(small, 7)
            nc.scalar.activation(bt[2][:], bt[2][:], ACT.Ln, bias=1.0).then_inc(small, 1)
            for h in range(4):
                last = nc.scalar.activation(bt[3][:, h, :], cols[:, V_ALOG + h:V_ALOG + h + 1].broadcast_to([P, NCH]), ACT.Exp)
            last.then_inc(small, 1)
            act.wait_ge(small, 12)
            nc.scalar.activation(bt[4][:], bd_gc[:], ACT.Exp).then_inc(small, 1)
            end_phase(act, 1)
            with act.Fori(0, PAIR_MIX) as i:
                for s in range(2):
                    act_block(act, i, s, ACT.Identity)
            with act.Fori(0, 4) as i:
                b = Beside(PAIR_MIX + 2 * i, DN_SLOTS)
                funcs = (ACT.Gelu, ACT.Sigmoid)
                slot = [0]

                def beside():
                    act_beside(act, b, slot[0], funcs)
                    slot[0] += 1

                for j in range(3):
                    act.wait_ge(dn_conv, 12 * i + 4 * j + 4)
                    nc.scalar.activation(d_cv[j][:], d_cv[j][:], ACT.Silu).then_inc(dn_silu, 1)
                for j, sq in enumerate((d_eg, d_dt)):
                    act.wait_ge(dn_silu, 4 * i + j + 1)
                    nc.scalar.activation(sq[:].rearrange("p n c -> p (n c)"), d_cv[j][:], ACT.Square).then_inc(dn_sq, 1)
                for j in range(2):
                    for g in range(2):
                        act.wait_ge(dn_taken[g], 1 + DN_USES * i + j + 1)
                    nc.scalar.activation(d_wt[:], d_wt[:], ACT.Sqrt).then_inc(dn_root, 1)
                    beside()
                act.wait_ge(dn_loaded, 64 * i + 64)
                nc.scalar.activation(d_z[:], d_z[:], ACT.Silu).then_inc(dn_silu, 1)
                for x, name in enumerate(DN_STAGES):
                    for g in range(2):
                        c = slice(4 * g, 4 * g + 4)
                        p3 = d_bank[g][:].rearrange("p (n c) -> p n c", c=P)
                        if name == "rowg":
                            act.wait_ge(dn_prod[g], DN_USES * i + 3 + x)
                            act.wait_ge(dn_taken[g], 1 + DN_USES * i + 2 + x)
                            nc.scalar.activation(d_eg[:, c, :], p3, ACT.Exp).then_inc(dn_eg[g], 1)
                            act.wait_ge(dn_min[g], i + 1)
                            nc.scalar.activation(d_tail[:, c], d_tail[:, c], ACT.Exp).then_inc(dn_eg[g], 1)
                            nc.scalar.activation(d_dt[:, c, :], d_dt[:, c, :], ACT.Exp).then_inc(dn_eg[g], 1)
                        if name[0] in "xt" or name == "w":
                            act.wait_ge(dn_prod[g], DN_USES * i + 3 + x)
                            dst = d_X if name[0] == "x" else d_T if name[0] == "t" else d_wt
                            nc.scalar.activation(dst[:, c, :], p3, ACT.Copy, scale=-1.0 if name == "w" else 1.0).then_inc(dn_taken[g], 1)
                        beside()
                for n in range(NCH):
                    beside()
                    beside()
                    if n % 4 == 3:
                        act.wait_ge(dn_scan_mm, 16 * i + 2 * n + 2)
                        nc.scalar.activation(d_o[:, HALF * (n // 4):HALF * (n // 4) + HALF], d_bank[1][:], ACT.Copy).then_inc(dn_o, 1)
                act.wait_ge(dn_o, 2 * i + 2)
                nc.scalar.activation(d_X[:].rearrange("p n c -> p (n c)"), d_o[:], ACT.Square).then_inc(dn_sq, 1)
                for g in range(2):
                    beside()
                for g in range(2):
                    act.wait_ge(dn_taken[g], 1 + DN_USES * i + DN_USES)
                nc.scalar.activation(d_wt[:], d_wt[:], ACT.Sqrt).then_inc(dn_root, 1)
            end_phase(act, 2)
            with act.Fori(0, 4) as i:
                b = Beside(PAIR_GATE + 2 * i, NST)
                for hf in range(2):
                    act.wait_ge(at_vt, 2 * i + hf + 1)
                    src = z_bank[hf][:].rearrange("p (n c) -> p n c", c=P)
                    for u in range(2):
                        last = nc.scalar.activation(a_v[:, 4 * hf:4 * hf + 4, u, 64 * u:64 * u + 64], src[:, :, 64 * u:64 * u + 64], ACT.Copy)
                    last.then_inc(at_v, 1)

                def copy_z(x):
                    T, u, j = STEPS[x]
                    t = slice(first_col(T, j), HALF)
                    act.wait_ge(z_ready, NST * i + x + 1)
                    if x >= 2:
                        act.wait_ge(arg_ready, NST * i + x - 1)
                    nc.scalar.activation(a_z[x % 2][:, t], z_bank[x % 2][:, t], ACT.Copy, scale=0.125).then_inc(z_read, 1)

                def exp_arg(x):
                    T, u, j = STEPS[x]
                    act.wait_ge(arg_ready, NST * i + x + 1)
                    a = a_A[u][:, j, first_col(T, j):HALF]
                    nc.scalar.activation(a, a, ACT.Exp).then_inc(a_ready, 1)

                def out_av(T):
                    act.wait_ge(av_done, 4 * i + 2 * T + 2)
                    act.wait_ge(y_stored, 1 + 32 * i)
                    nc.scalar.activation(a_y[T][:], o_bank[:], ACT.Copy).then_inc(av_read, 1)

                copy_z(0)
                for x in range(NST):
                    T, u, j = STEPS[x]
                    t = slice(first_col(T, j), HALF)
                    if x + 1 < NST:
                        copy_z(x + 1)
                    act.wait_ge(na_ready, NST * i + x + 1)
                    nc.scalar.activation(a_e[x % 2][:, t], a_e[x % 2][:, t], ACT.Exp).then_inc(e_ready, 1)
                    act.wait_ge(e_ready, NST * i + x + 1)
                    nc.scalar.activation(a_e[x % 2][:, t], a_e[x % 2][:, t], ACT.Ln, bias=1.0).then_inc(l_ready, 1)
                    if x >= 1:
                        exp_arg(x - 1)
                    act_beside(act, b, x, (ACT.Sigmoid, ACT.Sigmoid))
                    if x >= 3 and group_of(x - 3)[2] and STEPS[x - 3][1] == 1:
                        out_av(STEPS[x - 3][0])
                exp_arg(NST - 1)
                out_av(1)
            end_phase(act, 3)
            act.wait_ge(g_load, 80)
            for b in range(4):
                for hf in range(2):
                    x = 2 * b + hf
                    act.wait_ge(g_chain, 2 + 8)
                    if x >= 2:
                        act.wait_ge(g_pe, 2 + x - 1)
                    nc.scalar.activation(g_sq[x % 2][:], g_v[:, b, HALF * hf:HALF * hf + HALF], ACT.Square).then_inc(g_act, 1)
            act.wait_ge(g_chain, 12)
            nc.scalar.activation(g_rstd[:], g_rstd[:], ACT.Sqrt).then_inc(g_chain, 1)
            for b in range(4):
                for hf in range(2):
                    act.wait_ge(g_pe, 10 + 4 * b + hf + 1)
                    if b:
                        act.wait_ge(g_pe, 10 + 4 * b)
                    nc.scalar.activation(g_vt[:, 4 * hf:4 * hf + 4, :], z_bank[hf][:].rearrange("p (n c) -> p n c", c=P), ACT.Copy).then_inc(g_act, 1)
            end_phase(act, 4)
            for k in range(12):
                act.wait_ge(y_ld[k % 2], 16 * (k // 2 + 1))
                nc.scalar.activation(y_hi[:, k, :], m_acc[:, k % 2, :], ACT.Copy).then_inc(yh_ready, 1)
            with act.Fori(0, 2) as i:
                for q in range(6):
                    n, s = PAIR_BR + 3 * i + q // 2, q % 2
                    split_hi(act, n + 1, s)
                    if q % 3 == 2:
                        for dd in range(2):
                            d = 4 * i + 2 * (q // 3) + dd
                            act.wait_ge(m_added, 16 * i + 8 * (q // 3) + 6 + 2 * dd)
                            settle(act)
                            nc.scalar.activation(tile_of(act_hi, d), m_acc[:, dd, :], ACT.Copy).then_inc(mh_ready, 1)
            end_phase(act, 5)
            with act.Fori(0, 4) as i:
                for s in range(2):
                    n = PAIR_OUT + i
                    for hf in range(2):
                        wait_half(act, n, s, hf, 2 * n + s + HALF_BRANCH)
                        settle(act)
                        nc.scalar.activation(tile_of(mixed, 2 * i + s)[:, HALF * hf:HALF * hf + HALF], g_bank[hf][:], ACT.Copy).then_inc(bank_read[hf], 1)
                    split_hi(act, n + 1, s)
            act.drain().then_inc(mix_ready, 1)
            act.wait_ge(mix_ready, 1)
            norm_squares(act, 1, lambda k: mixed[:, k, :], n_sq)
            norm_root(act, 1, n_rstd)
            norm_squares(act, 2, lambda k: mixed[:, k, :], n_sq, ready=lambda k: (x1_ready, k + 1))
            norm_root(act, 2, n_rstd)
            for k in range(KT):
                act.wait_ge(h_ready, KT + k + 1)
                nc.scalar.activation(act_hi[:, k, :], n_h[k % 2][:], ACT.Copy).then_inc(hh_ready, 1)
            end_phase(act, 6)
            def ff_hi(blk, hf, count):
                act.wait_ge(f_sqr, count)
                settle(act)
                nc.scalar.activation(tile_of(f_hi, blk)[:, HALF * hf:HALF * hf + HALF], f_t[hf][:], ACT.Copy).then_inc(f_hr, 1)

            def ff_group(g, last=False):
                with act.Fori(0, 4) as i:
                    for s in range(2):
                        n = PAIR_FF + 8 * g + i
                        for hf in range(2):
                            c = 16 * g + 4 * i + 2 * s + hf
                            wait_half(act, n, s, hf, 2 * n + s + HALF_BRANCH)
                            act.wait_ge(f_lr, 1 + 16 * g + 4 * i + 2 * s)
                            nc.scalar.activation(f_t[hf][:], g_bank[hf][:], ACT.Relu).then_inc(bank_read[hf], 1)
                            ff_hi(2 * i + s, hf, c + 1)
                        split_hi(act, n + 1, s)
                with act.Fori(0, 3 if last else 4) as i:
                    for s in range(2):
                        split_hi(act, PAIR_FF + 8 * g + 4 + i + 1, s)

            with act.Fori(0, 3) as g:
                ff_group(g)
            ff_group(3, last=True)
            end_phase(act, 7)
            norm_squares(act, 3, lambda k: mixed[:, k, :], n_sq)
            norm_root(act, 3, n_rstd)

        @block.tensor
        def _(pe):
            pe.wait_ge(loaded, 64)
            norm_sums(pe, 0, sq0)
            pe.wait_ge(hl_ready, KT)
            pe.wait_ge(small, 2)
            for n in range(NCH):
                for k in range(KT):
                    pos = slice(P * n, P * n + P)
                    nc.tensor.matmul(z_bank[0][:, 8 * n:8 * n + 8], act_hi[:, k, pos], wbd_hi[:, k, :], start=(k == 0), stop=False)
                    nc.tensor.matmul(z_bank[0][:, 8 * n:8 * n + 8], act_hi[:, k, pos], wbd_lo[:, k, :], start=False, stop=False)
                    last = nc.tensor.matmul(z_bank[0][:, 8 * n:8 * n + 8], act_lo[:, k, pos], wbd_hi[:, k, :], start=False, stop=(k == KT - 1))
            last.then_inc(bd_mm, 1)
            pe.wait_ge(small, 11)
            nc.tensor.matmul(z_bank[1][:, 0:32], up_incl, bd_g[:].rearrange("p h n -> p (h n)"), start=True, stop=True).then_inc(bd_mm, 1)
            end_phase(pe, 1)
            with pe.Fori(0, PAIR_MIX) as i:
                for s in range(2):
                    pe_block(pe, i, s, act_hi, act_lo, 0)
            with pe.Fori(0, 4) as i:
                b = Beside(PAIR_MIX + 2 * i, DN_SLOTS)
                slot = [0]

                def beside():
                    pe_beside(pe, b, slot[0])
                    slot[0] += 1

                def chunk(t, n):
                    return t[:, P * n:P * n + P]

                for j, sq in enumerate((d_eg, d_dt)):
                    pe.wait_ge(dn_sq, 3 * i + j + 1)
                    for g in range(2):
                        pe.wait_ge(dn_taken[g], 1 + DN_USES * i + j)
                        nc.tensor.matmul(d_bank[g][:], ones, sq[:].rearrange("p n c -> p (n c)")[:, HALF * g:HALF * g + HALF],
                                         start=True, stop=True).then_inc(dn_prod[g], 1)
                    beside()
                for x, name in enumerate(DN_STAGES):
                    for g in range(2):
                        pe.wait_ge(dn_taken[g], 1 + DN_USES * i + 2 + x)
                        if name == "rowg":
                            pe.wait_ge(dn_chain, 1 + 4 * i + 4)
                            pe.wait_ge(dn_silu, 4 * i + 3)
                        if name == "t0":
                            pe.wait_ge(dn_tt[g], i + 1)
                        if name[0] == "x":
                            pe.wait_ge(dn_b[g], (N_LEV - 1) * i + int(name[1:]))
                        for m in range(4):
                            n = 4 * g + m
                            o = d_bank[g][:, P * m:P * m + P]
                            if name == "rowg":
                                last = nc.tensor.matmul(o, d_gB[:, n, :], up_incl, start=True, stop=True)
                            elif name == "rowb":
                                last = nc.tensor.matmul(o, d_bB[:, n, :], ident, start=True, stop=True)
                            elif name == "gram":
                                last = nc.tensor.matmul(o, chunk(d_cv[1], n), chunk(d_cv[1], n), start=True, stop=True)
                            elif name == "qk":
                                last = nc.tensor.matmul(o, chunk(d_cv[1], n), chunk(d_cv[0], n), start=True, stop=True)
                            elif name == "kT":
                                last = nc.tensor.transpose(o, chunk(d_cv[1], n), ident)
                            elif name == "vT":
                                last = nc.tensor.transpose(o, chunk(d_cv[2], n), ident)
                            elif name[0] == "t":
                                last = nc.tensor.transpose(o, d_TT[:, n, :], ident)
                            elif name[0] == "x":
                                last = nc.tensor.matmul(o, d_B[:, n, :], d_T[:, n, :], start=True, stop=True)
                            elif name[0] == "y":
                                last = nc.tensor.matmul(o, d_X[:, n, :], d_TT[:, n, :], start=True, stop=True)
                            else:
                                last = nc.tensor.matmul(o, d_kb[:, n, :], d_TT[:, n, :], start=True, stop=True)
                        last.then_inc(dn_prod[g], 1)
                        beside()
                for g in range(2):
                    pe.wait_ge(dn_taken[g], 1 + DN_USES * i + 2 + NDS)
                for n in range(NCH):
                    if n == 4:
                        pe.wait_ge(dn_o, 2 * i + 1)
                    o = d_bank[1][:, P * (n % 4):P * (n % 4) + P]
                    pe.wait_ge(dn_scan_ev, 17 * i + 1 + 2 * n)
                    nc.tensor.matmul(o, d_S[:], d_cv[0][:, P * n:P * n + P], start=True, stop=False)
                    nc.tensor.matmul(d_bank[0][:, 0:P], d_TT[:, n, :], d_vb[:, n, :], start=True, stop=False)
                    nc.tensor.matmul(d_bank[0][:, 0:P], d_wt[:, n, :], d_S[:], start=False, stop=True).then_inc(dn_scan_mm, 1)
                    beside()
                    pe.wait_ge(dn_scan_ev, 17 * i + 2 + 2 * n)
                    nc.tensor.matmul(o, d_vn[:], d_qk[:, n, :], start=False, stop=True)
                    nc.tensor.matmul(d_bank[0][:, P:2 * P], d_kt[:, n, :], d_vn[:], start=True, stop=True).then_inc(dn_scan_mm, 1)
                    beside()
                pe.wait_ge(dn_sq, 3 * i + 3)
                pe.wait_ge(dn_scan_ev, 17 * i + 17)
                for g in range(2):
                    nc.tensor.matmul(d_bank[g][:], ones, d_X[:].rearrange("p n c -> p (n c)")[:, HALF * g:HALF * g + HALF],
                                     start=True, stop=True).then_inc(dn_prod[g], 1)
                    beside()
            end_phase(pe, 2)
            with pe.Fori(0, 4) as i:
                b = Beside(PAIR_GATE + 2 * i, NST)
                pe.wait_ge(at_loaded, 64 * i + 64)
                for hf in range(2):
                    for n in range(4):
                        last = nc.tensor.transpose(z_bank[hf][:, P * n:P * n + P], a_vT[:, P * (4 * hf + n):P * (4 * hf + n) + P], ident)
                    last.then_inc(at_vt, 1)

                def scores(x):
                    T, u, j = STEPS[x]
                    c = first_col(T, j)
                    if x < 2:
                        pe.wait_ge(at_v, 2 * i + x + 1)
                    else:
                        pe.wait_ge(z_read, NST * i + x - 1)
                    nc.tensor.matmul(z_bank[x % 2][:, c:HALF], a_k[:, u, P * j:P * j + P], a_q[:, HALF * T + c:HALF * T + HALF],
                                     start=True, stop=True).then_inc(z_ready, 1)

                def sums_above(x):
                    T, u, j = STEPS[x]
                    c = first_col(T, j)
                    _, first, _ = group_of(x)
                    pe.wait_ge(sp_ready, NST * i + x + 1)
                    if x:
                        pe.wait_ge(arg_ready, NST * i + x)
                    mm = nc.tensor.matmul(c_bank[:, c:HALF], lo_incl, a_sp[x % 2][:, c:HALF], start=True, stop=first)
                    if not first:
                        c1 = first_col(T, j + 1)
                        pe.wait_ge(r_ready, N_R * i + R_BEFORE[x])
                        mm = nc.tensor.matmul(c_bank[:, c1:HALF], ones, a_R[:, c1:HALF], start=False, stop=True)
                    mm.then_inc(cum_ready, 1)

                def weighted_values(x):
                    T, u, _ = STEPS[x]
                    pe.wait_ge(a_ready, NST * i + x + 1)
                    pe.wait_ge(a_masked, N_DIAG * i + DIAGS[x])
                    if u == 0:
                        pe.wait_ge(av_read, 1 + 2 * i + T)
                    for j in range(4 * T + 4):
                        c = first_col(T, j)
                        last = nc.tensor.matmul(o_bank[:, c:HALF], a_v[:, j, u, :], a_A[u][:, j, c:HALF],
                                                start=(u == 0 and j == 0), stop=(u == 1 and j == 4 * T + 3))
                    last.then_inc(av_done, 1)

                scores(0)
                for x in range(NST):
                    if x + 1 < NST:
                        scores(x + 1)
                    pe_beside(pe, b, x)
                    sums_above(x)
                    if x >= 2 and group_of(x - 2)[2]:
                        weighted_values(x - 2)
                weighted_values(NST - 1)
                pe.drain().then_inc(at_iter, 1)
            end_phase(pe, 3)
            pe.wait_ge(g_load, 80)
            pe.wait_ge(g_masked, 1)
            for hf in range(2):
                for b in range(4):
                    last = nc.tensor.matmul(d_bank[hf][:], ones, g_v[:, b, HALF * hf:HALF * hf + HALF], start=(b == 0), stop=(b == 3))
                last.then_inc(g_pe, 1)
            pe.wait_ge(g_chain, 2)
            for b in range(4):
                for hf in range(2):
                    pe.wait_ge(g_act, 2 * b + hf + 1)
                    nc.tensor.matmul(d_bank[hf][:], ones, g_sq[hf][:], start=(b == 0), stop=(b == 3)).then_inc(g_pe, 1)
            for b in range(4):
                pe.wait_ge(g_chain, 14 + 4 * b + 2)
                for hf in range(2):
                    if b:
                        pe.wait_ge(g_act, 8 + 2 * b)
                    for m in range(4):
                        n = 4 * hf + m
                        last = nc.tensor.transpose(z_bank[hf][:, P * m:P * m + P], g_n[:, P * n:P * n + P], ident)
                    last.then_inc(g_pe, 1)
                pe.wait_ge(g_act, 8 + 2 * b + 2)
                for hf in range(2):
                    if b:
                        pe.wait_ge(g_out, b)
                    for m in range(4):
                        for e in range(2):
                            last = nc.tensor.matmul(d_bank[hf][64 * e:64 * e + 64, P * m:P * m + P],
                                                    g_vt[:, 4 * hf + m, 64 * e:64 * e + 64], g_w[:, 2 * b + e, :], start=True, stop=True)
                    last.then_inc(g_pe, 1)
            end_phase(pe, 4)
            pe.wait_ge(yl_ready, 12)
            with pe.Fori(0, 2) as i:
                for q in range(6):
                    n, s = PAIR_BR + 3 * i + q // 2, q % 2
                    pe.wait_ge(lo_ready[s], n + 1)
                    for r in range(4):
                        dd, hf = divmod(r, 2)
                        t = slice(HALF * hf, HALF * hf + HALF)
                        pe.wait_ge(bank_read[hf], 1 + 2 * PAIR_BR + 12 * i + 2 * q + dd)
                        for k in range(4):
                            kk, y = 4 * dd + k, 4 * (q % 3) + k
                            nc.tensor.matmul(g_bank[hf][:], w_hi[s][:, kk, :], y_hi[:, y, t], start=(k == 0), stop=False)
                            nc.tensor.matmul(g_bank[hf][:], w_hi[s][:, kk, :], y_lo[:, y, t], start=False, stop=False)
                            last = nc.tensor.matmul(g_bank[hf][:], w_lo[s][:, kk, :], y_hi[:, y, t], start=False, stop=(k == 3))
                        last.then_inc(half_ready if r < 3 else blk_done[s], 1)
            end_phase(pe, 5)
            with pe.Fori(0, 4) as i:
                for s in range(2):
                    pe_block(pe, PAIR_OUT + i, s, act_hi, act_lo, MIX_BRANCH)
            norm_sums(pe, 1, n_sq)
            pe.wait_ge(rstd_ready, 2)
            norm_sums(pe, 2, n_sq)
            end_phase(pe, 6)

            def ff_group(g):
                with pe.Fori(0, 4) as i:
                    for s in range(2):
                        pe_block(pe, PAIR_FF + 8 * g + i, s, act_hi, act_lo, MIX_BRANCH)
                pe.wait_ge(f_lr, 1 + 16 * g + 16)
                settle(pe)
                with pe.Fori(0, 4) as i:
                    for s in range(2):
                        pe_block(pe, PAIR_FF + 8 * g + 4 + i, s, f_hi, f_lo, MIX_BRANCH)

            with pe.Fori(0, 4) as g:
                ff_group(g)
            end_phase(pe, 7)
            norm_sums(pe, 3, n_sq)

        @block.vector
        def _(dve):
            dve.wait_ge(loaded, 64)
            dve.wait_ge(small, 1)
            nc.vector.tensor_tensor(wbd_lo[:], wbd[:], wbd_hi[:].bitcast(f32), ALU.subtract).then_inc(small, 1)
            for s in range(2):
                split_lo(dve, 0, s)
            norm_rstd(dve, 0, rstd0)
            for k in range(KT):
                if k >= 2:
                    dve.wait_ge(hh_ready, k - 1)
                nc.vector.scalar_tensor_tensor(hbuf[k % 2][:], x_sb[:, k, :], cols[:, V_NORM + k:V_NORM + k + 1], rstd0[:],
                                               ALU.mult, ALU.mult).then_inc(h_ready, 1)
                dve.wait_ge(hh_ready, k + 1)
                nc.vector.tensor_tensor(act_lo[:, k, :], hbuf[k % 2][:], act_hi[:, k, :].bitcast(f32), ALU.subtract).then_inc(hl_ready, 1)
            dve.wait_ge(bd_mm, 1)
            nc.vector.tensor_tensor(bd[:], z_bank[0][:, 0:64].rearrange("p (n c) -> p n c", c=8),
                                    cols[:, None, V_BBD:V_BBD + 8].broadcast_to([P, NCH, 8]), ALU.add).then_inc(small, 1)
            dve.wait_ge(small, 4)
            nc.vector.tensor_tensor(bt[0][:], bd[:, :, 4:8].rearrange("p n h -> p h n"),
                                    cols[:, V_DTB:V_DTB + 4, None].broadcast_to([P, 4, NCH]), ALU.add).then_inc(small, 1)
            dve.wait_ge(small, 5)
            nc.vector.scalar_tensor_tensor(bt[1][:], bt[0][:], -1.0, bt[0][:], ALU.mult, ALU.min).then_inc(small, 1)
            dve.wait_ge(small, 9)
            nc.vector.scalar_tensor_tensor(bt[0][:], bt[0][:], 0.0, bt[2][:], ALU.max, ALU.add).then_inc(small, 1)
            dve.wait_ge(small, 10)
            nc.vector.scalar_tensor_tensor(bd_g[:], bt[0][:], -1.0, bt[3][:], ALU.mult, ALU.mult).then_inc(small, 1)
            dve.wait_ge(bd_mm, 2)
            nc.vector.tensor_copy(bd_gc[:].rearrange("p h n -> p (h n)"), z_bank[1][:, 0:32]).then_inc(small, 1)
            dve.wait_ge(small, 13)
            nc.vector.tensor_tensor(bd_egc[:], bt[4][:], bd_beta[:], ALU.mult).then_inc(small, 1)
            end_phase(dve, 1)
            with dve.Fori(0, PAIR_MIX) as i:
                for s in range(2):
                    split_lo(dve, i + 1, s)
            for j in range(3):
                nc.vector.memset(d_in[j][:, 0:3], 0.0).then_inc(dn_dve, 1)
            dve.wait_ge(dn_dve, 3)
            with dve.Fori(0, 4) as i:
                b = Beside(PAIR_MIX + 2 * i, DN_SLOTS)
                slot = [0]

                def beside():
                    dve_beside(dve, b, slot[0])
                    slot[0] += 1

                dve.wait_ge(dn_loaded, 64 * i + 64)
                for j in range(3):
                    w = V_CONV + 16 * j
                    nc.vector.tensor_scalar(d_cv[j][:], d_in[j][:, 3:3 + S], cols[:, ds(w + 4 * i + 3, 1)], None, ALU.mult).then_inc(dn_conv, 1)
                    for tap in range(2, -1, -1):
                        dve.wait_ge(dn_conv, 12 * i + 4 * j + 3 - tap)
                        nc.vector.scalar_tensor_tensor(d_cv[j][:], d_in[j][:, tap:tap + S], cols[:, ds(w + 4 * i + tap, 1)], d_cv[j][:],
                                                       ALU.mult, ALU.add).then_inc(dn_conv, 1)
                for j in range(2):
                    r = d_wt[:].rearrange("p n c -> p (n c)")
                    dve.wait_ge(dn_chain, 1 + 4 * i + j)
                    for g in range(2):
                        t = slice(HALF * g, HALF * g + HALF)
                        dve.wait_ge(dn_prod[g], DN_USES * i + j + 1)
                        nc.vector.tensor_scalar(r[:, t], d_bank[g][:], EPS, None, ALU.add).then_inc(dn_taken[g], 1)
                    dve.wait_ge(dn_root, 3 * i + j + 1)
                    nc.vector.reciprocal(r, r).then_inc(dn_rcp, 1)
                    dve.wait_ge(dn_rcp, 3 * i + j + 1)
                    nc.vector.scalar_tensor_tensor(d_cv[j][:], d_cv[j][:], P ** -0.5 if j == 0 else 1.0, r, ALU.mult, ALU.mult).then_inc(dn_chain, 1)
                    beside()
                nc.vector.tensor_copy(d_gB[:], bd_g[:, ds(i, 1), :].rearrange("p h n -> p (h n)")[:, :, None].broadcast_to([P, NCH, P])).then_inc(dn_chain, 1)
                nc.vector.tensor_copy(d_bB[:], bd_beta[:, ds(i, 1), :].rearrange("p h n -> p (h n)")[:, :, None].broadcast_to([P, NCH, P])).then_inc(dn_chain, 1)
                dve.wait_ge(dn_chain, 1 + 4 * i + 4)

                def per_row(t, c):
                    return t[:, ds(i, 1), c].rearrange("p h n -> p (h n)")[:, :, None].broadcast_to([P, 4, P])

                def mask(m):
                    return m[:, None, :].broadcast_to([P, 4, P])

                def chained(ins):
                    local[0] += 1
                    ins.then_inc(dn_dve, 1)
                    dve.wait_ge(dn_dve, 3 + DVE_CHAIN * i + local[0])

                local = [0]
                for x, name in enumerate(DN_STAGES):
                    for g in range(2):
                        c = slice(4 * g, 4 * g + 4)
                        p3 = d_bank[g][:].rearrange("p (n c) -> p n c", c=P)
                        if name in ("rowg", "rowb", "gram", "qk", "kT", "vT") or name[0] == "y":
                            dve.wait_ge(dn_prod[g], DN_USES * i + 3 + x)
                        taken = DN_USES * i + 3 + x
                        if name == "rowg":
                            dve.wait_ge(dn_eg[g], 3 * i + 1)
                            nc.vector.tensor_tensor(d_dt[:, c, :], p3, per_row(bd_gc, c), ALU.subtract).then_inc(dn_taken[g], 1)
                            dve.wait_ge(dn_taken[g], 1 + taken)
                            chained(nc.vector.tensor_copy(d_tail[:, c], d_dt[:, c, P - 1]))
                            nc.vector.tensor_scalar(d_dt[:, c, :], d_dt[:, c, :], 0.0, None, ALU.min).then_inc(dn_min[g], 1)
                        elif name == "rowb":
                            dve.wait_ge(dn_eg[g], 3 * i + 3)
                            chained(nc.vector.tensor_tensor(d_dt[:, c, :], d_dt[:, c, :], mask(up_incl), ALU.mult))
                            nc.vector.tensor_tensor(d_at[:, c, :], p3, d_dt[:, c, :], ALU.mult).then_inc(dn_taken[g], 1)
                            dve.wait_ge(dn_taken[g], 1 + taken)
                            chained(nc.vector.tensor_tensor(d_at[:, c, :], d_at[:, c, :], mask(up_strict), ALU.mult))
                        elif name == "gram":
                            nc.vector.tensor_tensor(d_at[:, c, :], p3, d_at[:, c, :], ALU.mult).then_inc(dn_taken[g], 1)
                        elif name == "qk":
                            nc.vector.tensor_tensor(d_qk[:, c, :], p3, d_dt[:, c, :], ALU.mult).then_inc(dn_taken[g], 1)
                        elif name == "kT":
                            nc.vector.tensor_tensor(d_kb[:, c, :], p3, per_row(bd_egc, c), ALU.mult)
                            nc.vector.tensor_tensor(d_kt[:, c, :], p3, d_tail[:, c, None].broadcast_to([P, 4, P]), ALU.mult).then_inc(dn_taken[g], 1)
                            q3 = d_cv[0][:, HALF * g:HALF * g + HALF].rearrange("p (n c) -> p n c", c=P)
                            nc.vector.tensor_tensor(q3, q3, d_eg[:, c, :], ALU.mult)
                        elif name == "vT":
                            nc.vector.tensor_tensor(d_vb[:, c, :], p3, per_row(bd_beta, c), ALU.mult).then_inc(dn_taken[g], 1)
                            chained(nc.vector.tensor_tensor(d_TT[:, c, :], d_at[:, c, :], mask(consts[:, C_LEV, :]), ALU.mult))
                            nc.vector.scalar_tensor_tensor(d_TT[:, c, :], d_TT[:, c, :], -1.0, mask(ident), ALU.mult, ALU.add).then_inc(dn_tt[g], 1)
                        if name == "t0" or (name[0] == "y" and name != f"y{N_LEV - 1}"):
                            lev = int(name[1:])
                            if lev:
                                nc.vector.tensor_tensor(d_TT[:, c, :], d_TT[:, c, :], p3, ALU.subtract).then_inc(dn_taken[g], 1)
                            nc.vector.tensor_tensor(d_B[:, c, :], d_at[:, c, :], mask(consts[:, C_LEV + lev + 1, :]), ALU.mult).then_inc(dn_b[g], 1)
                        elif name[0] == "y":
                            nc.vector.tensor_tensor(d_TT[:, c, :], d_TT[:, c, :], p3, ALU.subtract).then_inc(dn_taken[g], 1)
                        beside()
                assert local[0] == DVE_CHAIN
                nc.vector.memset(d_S[:], 0.0).then_inc(dn_scan_ev, 1)
                for n in range(NCH):
                    dve.wait_ge(dn_scan_mm, 16 * i + 2 * n + 1)
                    nc.vector.tensor_copy(d_vn[:], d_bank[0][:, 0:P]).then_inc(dn_scan_ev, 1)
                    beside()
                    dve.wait_ge(dn_scan_mm, 16 * i + 2 * n + 2)
                    dve.wait_ge(dn_scan_ev, 17 * i + 2 * n + 2)
                    nc.vector.scalar_tensor_tensor(d_S[:], d_S[:], d_eg[:, n, P - 1:P], d_bank[0][:, P:2 * P],
                                                   ALU.mult, ALU.add).then_inc(dn_scan_ev, 1)
                    beside()
                for g in range(2):
                    t = slice(HALF * g, HALF * g + HALF)
                    r = d_wt[:].rearrange("p n c -> p (n c)")
                    dve.wait_ge(dn_prod[g], DN_USES * i + DN_USES)
                    nc.vector.tensor_scalar(r[:, t], d_bank[g][:], 1.0 / P, EPS, ALU.mult, ALU.add).then_inc(dn_taken[g], 1)
                    beside()
                dve.wait_ge(dn_root, 3 * i + 3)
                nc.vector.reciprocal(r, r).then_inc(dn_rcp, 1)
                dve.wait_ge(dn_rcp, 3 * i + 3)
                nc.vector.scalar_tensor_tensor(d_o[:], d_o[:], cols[:, V_DNG:V_DNG + 1], r, ALU.mult, ALU.mult).then_inc(dn_out, 1)
                dve.wait_ge(dn_out, 2 * i + 1)
                dve.wait_ge(dn_silu, 4 * i + 4)
                nc.vector.tensor_tensor(d_o[:], d_o[:], d_z[:], ALU.mult).then_inc(dn_out, 1)
            end_phase(dve, 2)
            with dve.Fori(0, 4) as i:
                b = Beside(PAIR_GATE + 2 * i, NST)

                def minus_abs(x):
                    T, u, j = STEPS[x]
                    t = slice(first_col(T, j), HALF)
                    dve.wait_ge(z_read, NST * i + x + 1)
                    nc.vector.scalar_tensor_tensor(a_e[x % 2][:, t], a_z[x % 2][:, t], -1.0, a_z[x % 2][:, t], ALU.mult, ALU.min).then_inc(na_ready, 1)

                def softplus(x):
                    T, u, j = STEPS[x]
                    c = first_col(T, j)
                    t = slice(c, HALF)
                    dve.wait_ge(l_ready, NST * i + x + 1)
                    if x >= 2:
                        dve.wait_ge(cum_ready, NST * i + x - 1)
                    diag = is_diag(T, j)
                    nc.vector.scalar_tensor_tensor(a_sp[x % 2][:, t], a_z[x % 2][:, t], 0.0, a_e[x % 2][:, t],
                                                   ALU.max, ALU.add).then_inc(sp_raw if diag else sp_ready, 1)
                    if diag:
                        dve.wait_ge(sp_raw, N_DIAG * i + DIAGS[x])
                        nc.vector.tensor_tensor(a_sp[x % 2][:, c:c + P], a_sp[x % 2][:, c:c + P], up_strict, ALU.mult).then_inc(sp_ready, 1)

                def argument(x):
                    T, u, j = STEPS[x]
                    c = first_col(T, j)
                    t = slice(c, HALF)
                    _, first, last = group_of(x)
                    dve.wait_ge(cum_ready, NST * i + x + 1)
                    if first and T == 1:
                        dve.wait_ge(av_done, 4 * i + u + 1)
                    nc.vector.tensor_tensor(a_A[u][:, j, t], a_z[x % 2][:, t], c_bank[:, t], ALU.subtract).then_inc(arg_ready, 1)
                    if last:
                        return
                    if first:
                        if c:
                            nc.vector.memset(a_R[:, 0:c], 0.0)
                        nc.vector.tensor_copy(a_R[:, t], a_sp[x % 2][:, t]).then_inc(r_ready, 1)
                    else:
                        dve.wait_ge(r_ready, N_R * i + R_BEFORE[x])
                        nc.vector.tensor_tensor(a_R[:, t], a_R[:, t], a_sp[x % 2][:, t], ALU.add).then_inc(r_ready, 1)

                for x in range(NST):
                    minus_abs(x)
                    if x >= 1:
                        argument(x - 1)
                    softplus(x)
                    dve_beside(dve, b, x)
                argument(NST - 1)
            end_phase(dve, 3)
            for hf in range(2):
                dve.wait_ge(g_pe, hf + 1)
                nc.vector.tensor_scalar(g_mean[:, HALF * hf:HALF * hf + HALF], d_bank[hf][:], 1.0 / BW, None, ALU.mult).then_inc(g_chain, 1)
            dve.wait_ge(g_chain, 2)
            for b in range(4):
                for hf in range(2):
                    v = g_v[:, b, HALF * hf:HALF * hf + HALF]
                    nc.vector.tensor_tensor(v, v, g_mean[:, HALF * hf:HALF * hf + HALF], ALU.subtract).then_inc(g_chain, 1)
            dve.wait_ge(g_pe, 10)
            for hf in range(2):
                nc.vector.tensor_scalar(g_rstd[:, HALF * hf:HALF * hf + HALF], d_bank[hf][:], 1.0 / BW, EPS, ALU.mult, ALU.add).then_inc(g_chain, 1)
            dve.wait_ge(g_chain, 13)
            nc.vector.reciprocal(g_rstd[:], g_rstd[:]).then_inc(g_chain, 1)
            for b in range(4):
                dve.wait_ge(g_chain, 14 + 4 * b)
                nc.vector.scalar_tensor_tensor(g_n[:], g_v[:, b, :], cols[:, V_LNG + b:V_LNG + b + 1], g_rstd[:], ALU.mult, ALU.mult).then_inc(g_chain, 1)
                dve.wait_ge(g_chain, 15 + 4 * b)
                nc.vector.tensor_scalar(g_n[:], g_n[:], cols[:, V_LNB + b:V_LNB + b + 1], None, ALU.add).then_inc(g_chain, 1)
                y = g_y[b % 2]
                if b >= 2:
                    dve.wait_ge(g_store[b % 2], 16)
                for hf in range(2):
                    t = slice(HALF * hf, HALF * hf + HALF)
                    dve.wait_ge(g_pe, 10 + 4 * b + 2 + hf + 1)
                    bias = cols[:, None, V_BSP + P * b:V_BSP + P * b + P].broadcast_to([P, 4, P])
                    nc.vector.tensor_tensor(y[:, t].rearrange("p (n c) -> p n c", c=P), d_bank[hf][:].rearrange("p (n c) -> p n c", c=P),
                                            bias, ALU.add).then_inc(g_chain, 1)
                dve.wait_ge(g_chain, 18 + 4 * b)
                nc.vector.tensor_tensor(y[:], y[:], g_u[:, b, :], ALU.mult).then_inc(g_out, 1)
            end_phase(dve, 4)
            for k in range(12):
                dve.wait_ge(yh_ready, k + 1)
                nc.vector.tensor_tensor(y_lo[:, k, :], m_acc[:, k % 2, :], y_hi[:, k, :].bitcast(f32), ALU.subtract).then_inc(yl_ready, 1)
            with dve.Fori(0, 2) as i:
                for q in range(6):
                    n, s = PAIR_BR + 3 * i + q // 2, q % 2
                    for r in range(4):
                        dd, hf = divmod(r, 2)
                        acc = m_acc[:, dd, HALF * hf:HALF * hf + HALF]
                        if r < 3:
                            dve.wait_ge(half_ready, 2 * PAIR_BR + 18 * i + 3 * q + r + 1)
                        else:
                            dve.wait_ge(blk_done[s], n + 1)
                        uses = 12 * i + 2 * q + dd
                        dve.wait_ge(gate_ld[hf], 16 * uses + 16)
                        first = q % 3 == 0
                        added = 16 * i + 8 * (q // 3) + 4 * (q % 3 - 1) + r
                        if first:
                            dve.wait_ge(ml_ready, 1 + 4 * i + 2 * (q // 3))
                        else:
                            dve.wait_ge(m_added, added)
                        nc.vector.tensor_tensor(acc if first else m_t[:], g_bank[hf][:], gate[hf][:], ALU.mult).then_inc(bank_read[hf], 1)
                        if not first:
                            dve.wait_ge(bank_read[hf], 1 + 2 * PAIR_BR + uses + 1)
                            nc.vector.tensor_tensor(acc, acc, m_t[:], ALU.add).then_inc(m_added, 1)
                    split_lo(dve, n + 1, s)
                    if q % 3 == 2:
                        for dd in range(2):
                            d = 4 * i + 2 * (q // 3) + dd
                            dve.wait_ge(mh_ready, d + 1)
                            nc.vector.tensor_tensor(tile_of(act_lo, d), m_acc[:, dd, :], tile_of(act_hi, d).bitcast(f32), ALU.subtract).then_inc(ml_ready, 1)
            end_phase(dve, 5)
            with dve.Fori(0, 4) as i:
                for s in range(2):
                    split_lo(dve, PAIR_OUT + i + 1, s)
            norm_rstd(dve, 1, n_rstd)
            for k in range(KT):
                nc.vector.scalar_tensor_tensor(mixed[:, k, :], mixed[:, k, :], cols[:, V_NORM + 8 + k:V_NORM + 9 + k], n_rstd[:],
                                               ALU.mult, ALU.mult).then_inc(n_chain, 1)
                dve.wait_ge(n_chain, k + 1)
                dve.wait_ge(ld[k % 2], 16 * (k // 2 + 1))
                nc.vector.tensor_tensor(mixed[:, k, :], mixed[:, k, :], n_x[k % 2][:], ALU.add).then_inc(x1_ready, 1)
            norm_rstd(dve, 2, n_rstd)
            for k in range(KT):
                if k >= 2:
                    dve.wait_ge(hh_ready, KT + k - 1)
                nc.vector.scalar_tensor_tensor(n_h[k % 2][:], mixed[:, k, :], cols[:, V_NORM + 16 + k:V_NORM + 17 + k], n_rstd[:],
                                               ALU.mult, ALU.mult).then_inc(h_ready, 1)
                dve.wait_ge(hh_ready, KT + k + 1)
                nc.vector.tensor_tensor(act_lo[:, k, :], n_h[k % 2][:], act_hi[:, k, :].bitcast(f32), ALU.subtract).then_inc(hl_ready, 1)
            end_phase(dve, 6)

            def ff_group(g, first=False, last=False):
                with dve.Fori(0, 4) as i:
                    for s in range(2):
                        n = PAIR_FF + 8 * g + i
                        for hf in range(2):
                            c = 16 * g + 4 * i + 2 * s + hf
                            t = slice(HALF * hf, HALF * hf + HALF)
                            dve.wait_ge(bank_read[hf], 1 + 2 * n + s + 1 + MIX_BRANCH)
                            nc.vector.tensor_tensor(f_t[hf][:], f_t[hf][:], f_t[hf][:], ALU.mult).then_inc(f_sqr, 1)
                            dve.wait_ge(f_hr, c + 1)
                            nc.vector.tensor_tensor(tile_of(f_lo, 2 * i + s)[:, t], f_t[hf][:], tile_of(f_hi, 2 * i + s)[:, t].bitcast(f32),
                                                    ALU.subtract).then_inc(f_lr, 1)
                        split_lo(dve, n + 1, s)
                def add_pair(i, split):
                    for s in range(2):
                        n = PAIR_FF + 8 * g + 4 + i
                        for hf in range(2):
                            acc = tile_of(mixed, 2 * i + s)[:, HALF * hf:HALF * hf + HALF]
                            wait_half(dve, n, s, hf, 2 * n + s + HALF_BRANCH)
                            if first:
                                nc.vector.tensor_copy(acc, g_bank[hf][:]).then_inc(bank_read[hf], 1)
                            else:
                                nc.vector.tensor_tensor(acc, acc, g_bank[hf][:], ALU.add).then_inc(bank_read[hf], 1)
                        if split:
                            split_lo(dve, n + 1, s)

                with dve.Fori(0, 3 if last else 4) as i:
                    add_pair(i, True)
                if last:
                    add_pair(3, False)

            ff_group(0, first=True)
            with dve.Fori(1, 3) as g:
                ff_group(g)
            ff_group(3, last=True)
            end_phase(dve, 7)
            norm_rstd(dve, 3, n_rstd)
            for k in range(KT):
                nc.vector.scalar_tensor_tensor(mixed[:, k, :], mixed[:, k, :], cols[:, V_NORM + 24 + k:V_NORM + 25 + k], n_rstd[:],
                                               ALU.mult, ALU.mult).then_inc(n_chain, 1)
                dve.wait_ge(n_chain, KT + k + 1)
                dve.wait_ge(x_ld, 16)
                nc.vector.tensor_tensor(x_fin[:, k, :], x_fin[:, k, :], mixed[:, k, :], ALU.add).then_inc(out_ready, 1)

        @block.gpsimd
        def _(pool):
            end_phase(pool, 1)
            end_phase(pool, 2)
            nc.gpsimd.memset(a_k[:], 0.0).then_inc(pad_zero, 1)
            nc.gpsimd.memset(a_v[:], 0.0).then_inc(pad_zero, 1)
            with pool.Fori(0, 4) as i:
                for x, (T, u, j) in enumerate(STEPS):
                    if is_diag(T, j):
                        c = first_col(T, j)
                        pool.wait_ge(a_ready, NST * i + x + 1)
                        nc.gpsimd.tensor_tensor(a_A[u][:, j, c:c + P], a_A[u][:, j, c:c + P], up_strict, ALU.mult).then_inc(a_masked, 1)
            end_phase(pool, 3)
            pool.wait_ge(g_load, 80)
            nc.gpsimd.tensor_tensor(g_w[:], g_w[:], up_incl[:, None, :].broadcast_to([P, 8, P]), ALU.mult).then_inc(g_masked, 1)
            for k in range(4, 8):
                end_phase(pool, k)


def kernel(x, norm_g, w_in, b_in, sgu_ln_g, sgu_ln_b, w_spatial, b_spatial, conv_w, a_log, dt_bias, dn_norm_g,
           w_branch, w_out, w_ff1, w_ff2):
    import concourse.bacc as bacc
    from concourse.bass_utils import run_bass_kernel_spmd as run

    f = lambda a: np.asarray(a)
    x, w_in, b_in = f(x), f(w_in)[0], f(b_in)[0]
    w_branch, w_out, w_ff1, w_ff2 = f(w_branch)[0], f(w_out)[0], f(w_ff1)[0], f(w_ff2)[0]

    def tiles(w):
        r, c = w.shape
        return w.reshape(r // P, P, c // P, P).transpose(2, 1, 0, 3).reshape(c // P, P, r)

    starts = [c + P * t for c in (COL_DQ, COL_DQ + 512, COL_DQ + 1024, COL_DQ + 1536,
                                  COL_SQ, COL_SQ + 512, COL_SQ + 1024) for t in range(4)]
    for i in range(4):
        starts += [COL_AU + 256 * i, COL_AU + 256 * i + P, COL_GATE + 256 * i, COL_GATE + 256 * i + P]
    starts += [COL_GATE + 1024 + P * t for t in range(16)]
    stream = [tiles(w_in[:, c:c + P]) for c in starts]
    for i in range(2):
        for q in range(6):
            c = 512 * i + 256 * (q // 3)
            stream.append(tiles(w_branch[q % 3][:, c:c + 256]).transpose(1, 0, 2).reshape(1, P, KT * P))
    stream.append(tiles(w_out))
    for g in range(4):
        stream.append(tiles(w_ff1[:, 1024 * g:1024 * g + 1024]))
        stream.append(tiles(w_ff2[1024 * g:1024 * g + 1024]))
    w_stream = np.ascontiguousarray(np.concatenate(stream).reshape(N_PAIRS, 2, P, KT * P))

    def by_partition(a):
        return a.reshape(-1, P).T

    def on_all(a):
        return np.broadcast_to(a.reshape(1, -1), (P, a.size))

    bsp = np.repeat(f(b_spatial)[0].reshape(4, 2, P), 64, axis=1)
    cw = f(conv_w)[0].reshape(4, 12, P).transpose(2, 1, 0).reshape(P, 48)
    cols = np.concatenate([
        by_partition(f(norm_g)[0]), np.stack([b_in[c:c + P] for c in starts], 1),
        by_partition(f(sgu_ln_g)[0]), by_partition(f(sgu_ln_b)[0]), cw, by_partition(f(dn_norm_g)[0]),
        on_all(f(a_log)[0]), on_all(f(dt_bias)[0]), on_all(b_in[COL_BETA:COL_BETA + 8]),
        bsp.transpose(1, 0, 2).reshape(P, 4 * P)], axis=1)

    p, c = np.arange(P)[:, None], np.arange(P)[None, :]
    levels = [(c >> (v + 1) == p >> (v + 1)) & ((c >> v) % 2 == 1) & ((p >> v) % 2 == 0) for v in range(N_LEV)]
    consts = np.stack([p == c, p >= 0 * c, p <= c, p < c, p >= c, *levels], axis=1).astype(np.float32)

    arrays = {
        "xT": np.ascontiguousarray(x[0].T.reshape(KT, P, S)),
        "w_stream": w_stream,
        "w_bd": np.ascontiguousarray(w_in[:, COL_BETA:COL_BETA + 8].reshape(KT, P, 8).transpose(1, 0, 2)),
        "w_spT": np.ascontiguousarray(f(w_spatial)[0].transpose(2, 0, 1)),
        "cols_in": np.ascontiguousarray(cols),
        "consts_in": consts,
    }
    nc = bacc.Bacc("TRN2", target_bir_lowering=False, num_devices=1)
    f32 = mybir.dt.float32
    args = [nc.dram_tensor(n, a.shape, f32, kind="ExternalInput").ap() for n, a in arrays.items()]
    out = nc.dram_tensor("outT", (KT, P, S), f32, kind="ExternalOutput").ap()
    hybrid_decoder_layer(nc, *args, out)
    r = run(nc, [arrays], core_ids=[0])
    y = r.results[0]["outT"].reshape(D, S)
    return np.ascontiguousarray(y.T)[None]
```

```python
import concourse.bass as bass
from concourse import mybir
from contextlib import ExitStack
import numpy as np

P = 128
D = 1024
S = 1024
KT = D // P
HALF = 512
BW = 512
EPS = 1e-6
NCH = S // P

N_SB = 6
PAIR_AT = 6
PAIR_DN = 14
PAIR_SG = 26
PAIR_BR = 30
PAIR_OUT = 36
PAIR_FF = 40
N_PAIRS = 72
ROW_SQ, ROW_SK, ROW_SV = 0, 4, 8
ROW_DQ, ROW_DK, ROW_DV, ROW_DZ = 12, 16, 20, 24
ROW_U, ROW_V = (32, 38), (44, 50)
ROW_GATE01 = 28
ROW_GATE2 = 52
COL_AU, COL_AV, COL_DQ, COL_BETA, COL_SQ = 0, 512, 1024, 3072, 3080
COL_GATE = 4616

C_ID, C_ONE, C_UPI, C_UPS, C_LOI, C_LEV = 0, 1, 2, 3, 4, 5
N_LEV = 7
N_CONST = C_LEV + N_LEV

V_NORM = 0
V_BIN = V_NORM + 32
V_LNG = V_BIN + 60
V_LNB = V_LNG + 4
V_CONV = V_LNB + 4
V_DNG = V_CONV + 48
V_ALOG = V_DNG + 1
V_DTB = V_ALOG + 4
V_BBD = V_DTB + 4
V_BSP = V_BBD + 8
V_EPS = V_BSP + 4 * P
N_COLS = V_EPS + 1


def hybrid_decoder_layer(nc, xT, w_stream, w_bd, w_spT, cols_in, consts_in, outT):
    f32, f32r = mybir.dt.float32, mybir.dt.float32r
    ACT, ALU = mybir.ActivationFunctionType, mybir.AluOpType
    ds = bass.ds

    pT = nc.dram_tensor("projections", (60, P, S), f32, kind="Internal").ap()
    yT = nc.dram_tensor("branch_outputs", (12, P, S), f32, kind="Internal").ap()
    x1T = nc.dram_tensor("residual", (KT, P, S), f32, kind="Internal").ap()

    top = ExitStack()
    scope = [top]

    def sb(name, shape, dt=f32):
        return scope[0].enter_context(nc.sbuf_tensor(name, shape, dt))

    def sem(name):
        return top.enter_context(nc.semaphore(name))

    with top:
        consts = sb("consts", [P, N_CONST, P])
        cols = sb("cols", [P, N_COLS])
        ident, ones = consts[:, C_ID, :], consts[:, C_ONE, :]
        eps = cols[:, V_EPS:V_EPS + 1]
        up_incl, up_strict, lo_incl = consts[:, C_UPI, :], consts[:, C_UPS, :], consts[:, C_LOI, :]
        w_raw = [sb(f"w_raw{s}", [P, KT * P]) for s in range(2)]
        w_hi = [sb(f"w_hi{s}", [P, KT, P], f32r) for s in range(2)]
        w_lo = [sb(f"w_lo{s}", [P, KT, P], f32r) for s in range(2)]
        act_hi = sb("act_hi", [P, KT, S], f32r)
        act_lo = sb("act_lo", [P, KT, S], f32r)
        bd_g = sb("bd_g", [P, 4, NCH])
        bd_beta = sb("bd_beta", [P, 4, NCH])
        bd_gc = sb("bd_gc", [P, 4, NCH])
        bd_egc = sb("bd_egc", [P, 4, NCH])

        early = ExitStack()
        early.__enter__()
        scope[0] = early
        stage = [sb(f"stage{s}", [P, S]) for s in range(2)]

        scope[0] = ExitStack()
        with scope[0]:
            x_sb = sb("x_sb", [P, KT, S])
            sq0 = [sb(f"sq0_{s}", [P, S]) for s in range(3)]
            ss0 = sb("ss0", [P, S])
            rstd0 = sb("rstd0", [P, S])
            hbuf = [sb(f"hbuf{s}", [P, S]) for s in range(2)]
            wbd = sb("wbd", [P, KT, 8])
            wbd_parts = sb("wbd_parts", [P, KT, P], f32r)
            bdT = sb("bdT", [16, S])
            bd = sb("bd", [P, NCH, 8])
            bt = [sb(f"bt{s}", [P, 4, NCH]) for s in range(5)]

        scope[0] = ExitStack()
        with scope[0]:
            d_in = [sb(f"d_in{s}", [P, 3 + S]) for s in range(3)]
            d_z = sb("d_z", [P, S])
            d_cv = [sb(f"d_cv{s}", [P, S]) for s in range(3)]
            d_gB = sb("d_gB", [P, NCH, P])
            d_bB = sb("d_bB", [P, NCH, P])
            d_eg = sb("d_eg", [P, NCH, P])
            d_dt = sb("d_dt", [P, NCH, P])
            d_at = sb("d_at", [P, NCH, P])
            d_qk = sb("d_qk", [P, NCH, P])
            d_kb = sb("d_kb", [P, NCH, P])
            d_kt = sb("d_kt", [P, NCH, P])
            d_vb = sb("d_vb", [P, NCH, P])
            d_TT = sb("d_TT", [P, NCH, P])
            d_T = sb("d_T", [P, NCH, P])
            d_wt = sb("d_wt", [P, NCH, P])
            d_tail = sb("d_tail", [P, NCH])
            d_S = sb("d_S", [P, P])
            d_vn = sb("d_vn", [P, P])
        d_X, d_B, d_r = d_gB, d_bB, d_eg
        d_o = d_cv[2]

        scope[0] = ExitStack()
        with scope[0]:
            a_q = sb("a_q", [P, S])
            a_k = sb("a_k", [P, 2, S])
            a_vT = sb("a_vT", [P, S])
            a_v = sb("a_v", [P, NCH, 2, P])
            a_z = [sb(f"a_z{s}", [P, HALF]) for s in range(4)]
            a_e = [sb(f"a_e{s}", [P, HALF]) for s in range(3)]
            a_sp = [sb(f"a_sp{s}", [P, HALF]) for s in range(3)]
            a_sp_hi = [sb(f"a_sp_hi{s}", [P, HALF], f32r) for s in range(2)]
            a_sp_lo = [sb(f"a_sp_lo{s}", [P, HALF], f32r) for s in range(2)]
            a_from = sb("a_from", [P, P], f32r)
            a_ones = sb("a_ones", [P, P], f32r)
            a_R = [sb(f"a_R{s}", [P, HALF]) for s in range(2)]
            a_R_hi = [sb(f"a_R_hi{s}", [P, HALF], f32r) for s in range(2)]
            a_R_lo = [sb(f"a_R_lo{s}", [P, HALF], f32r) for s in range(2)]
            a_A = [sb(f"a_A{s}", [P, NCH, HALF]) for s in range(2)]
            a_y = [sb(f"a_y{s}", [P, HALF]) for s in range(2)]

        scope[0] = ExitStack()
        with scope[0]:
            g_w = sb("g_w", [P, 8, P])
            g_v = sb("g_v", [P, 4, S])
            g_u = sb("g_u", [P, 4, S])
            g_sq = [sb(f"g_sq{s}", [P, HALF]) for s in range(2)]
            g_mean = sb("g_mean", [P, S])
            g_rstd = sb("g_rstd", [P, S])
            g_vt = sb("g_vt", [P, NCH, P])
            g_n = sb("g_n", [P, S])
            g_y = [sb(f"g_y{s}", [P, S]) for s in range(2)]

        early.close()

        scope[0] = ExitStack()
        with scope[0]:
            y_hi = sb("y_hi", [P, 12, S], f32r)
            y_lo = sb("y_lo", [P, 12, S], f32r)
            m_acc = sb("m_acc", [P, 2, S])
            gate = [sb(f"gate{s}", [P, HALF]) for s in range(2)]
            m_t = sb("m_t", [P, HALF])

        outer = ExitStack()
        with outer:
            scope[0] = outer
            mixed = sb("mixed", [P, KT, S])
            scope[0] = ExitStack()
            with scope[0]:
                n_sq = [sb(f"n_sq{s}", [P, S]) for s in range(3)]
                n_ss = sb("n_ss", [P, S])
                n_rstd = sb("n_rstd", [P, S])
                n_x = [sb(f"n_x{s}", [P, S]) for s in range(2)]
                n_h = [sb(f"n_h{s}", [P, S]) for s in range(2)]
                x_fin = sb("x_fin", [P, KT, S])
            scope[0] = ExitStack()
            with scope[0]:
                f_hi = sb("f_hi", [P, KT, S], f32r)
                f_lo = sb("f_lo", [P, KT, S], f32r)
                f_t = [sb(f"f_t{s}", [P, HALF]) for s in range(2)]
        scope[0] = top

        def bank(name):
            return top.enter_context(nc.psum_tensor(name, [P, HALF], f32))

        g_bank = [bank("gemm0"), bank("gemm1")]
        z_bank = [bank("z0"), bank("z1")]
        c_bank = bank("cumsum")
        o_bank = bank("attn_out")
        d_bank = [bank("dn0"), bank("dn1")]
        cum_bank = [c_bank, d_bank[0]]

        loaded = sem("loaded")
        raw_loaded = [sem(f"raw_loaded{s}") for s in range(2)]
        hi_ready = [sem(f"hi_ready{s}") for s in range(2)]
        lo_ready = [sem(f"lo_ready{s}") for s in range(2)]
        blk_done = [sem(f"blk_done{s}") for s in range(2)]
        half_ready = sem("half_ready")
        bank_read = [sem(f"bank_read{s}") for s in range(2)]
        stored = [sem(f"stored{s}") for s in range(2)]
        staged = [sem(f"staged{s}") for s in range(2)]
        apart = sem("apart")
        phase = sem("phase")
        sq_ready, sq_added, ss_ready = sem("sq_ready"), sem("sq_added"), sem("ss_ready")
        ln_ready, rstd_ready = sem("ln_ready"), sem("rstd_ready")
        h_ready, hh_ready, hl_ready = sem("h_ready"), sem("hh_ready"), sem("hl_ready")
        x_in = [sem(f"x_in{r}") for r in range(4)]
        gw_load, gu_load = sem("gw_load"), sem("gu_load")
        ld = [sem(f"ld{s}") for s in range(2)]
        use = [sem(f"use{s}") for s in range(2)]
        small = sem("small")
        bd_mm, wbd_zero, bdT_ready = sem("bd_mm"), sem("wbd_zero"), sem("bdT_ready")
        w_sq, w_added = sem("w_sq"), sem("w_added")
        dn_loaded, dn_conv, dn_silu, dn_sq = sem("dn_loaded"), sem("dn_conv"), sem("dn_silu"), sem("dn_sq")
        dn_chain = sem("dn_chain")
        dn_prod = [sem(f"dn_prod{g}") for g in range(2)]
        dn_taken = [sem(f"dn_taken{g}") for g in range(2)]
        dn_dve, dn_out = sem("dn_dve"), sem("dn_out")
        dn_eg, dn_min, dn_tt, dn_b = ([sem(f"{n}{g}") for g in range(2)] for n in ("dn_eg", "dn_min", "dn_tt", "dn_b"))
        dn_scan_mm, dn_scan_ev = sem("dn_scan_mm"), sem("dn_scan_ev")
        dn_o, dn_root, dn_yst = sem("dn_o"), sem("dn_root"), sem("dn_yst")
        dn_z = sem("dn_z")
        at_loaded, at_vt, at_v = sem("at_loaded"), sem("at_vt"), sem("at_v")
        z_ready, z_read, na_ready, e_ready, l_ready = (sem(n) for n in ("z_ready", "z_read", "na_ready", "e_ready", "l_ready"))
        sp_raw, sp_ready, sp_hi_ready, sp_lo_ready, r_sum, r_hi, r_ready, tri_ready, cum_ready, arg_ready, a_ready = (
            sem(n) for n in ("sp_raw", "sp_ready", "sp_hi_ready", "sp_lo_ready", "r_sum", "r_hi", "r_ready", "tri_ready", "cum_ready", "arg_ready", "a_ready"))
        a_masked, av_done, av_read = (sem(n) for n in ("a_masked", "av_done", "av_read"))
        y_stored = [sem(f"y_stored{T}") for T in range(2)]
        pad_zero = sem("pad_zero")
        g_load, g_chain, g_pe, g_act = sem("g_load"), sem("g_chain"), sem("g_pe"), sem("g_act")
        g_masked = sem("g_masked")
        g_out, g_store = sem("g_out"), [sem(f"g_store{s}") for s in range(2)]
        y_ld = [sem(f"y_ld{b}") for b in range(3)]
        yh_ready, yl_ready = sem("yh_ready"), sem("yl_ready")
        gate_ld = [sem(f"gate_ld{s}") for s in range(2)]
        gate_sig = [sem(f"gate_sig{s}") for s in range(2)]
        m_added, mh_ready, ml_ready = sem("m_added"), sem("mh_ready"), sem("ml_ready")
        x_ld, x_used, x1_ready, x1_st = sem("x_ld"), sem("x_used"), sem("x1_ready"), sem("x1_st")
        n_chain = sem("n_chain")
        f_relu, f_sqr, f_hr, f_lr, f_acc = sem("f_relu"), sem("f_sqr"), sem("f_hr"), sem("f_lr"), sem("f_acc")
        out_ready, out_st = sem("out_ready"), sem("out_st")

        def tile_of(t, k):
            return t[:, ds(k, 1), :].rearrange("p k s -> p (k s)")

        def settle(eng):
            eng.sem_inc(apart, 1)

        def end_phase(eng, k):
            eng.drain().then_inc(phase, 1)
            eng.wait_ge(phase, 5 * k)

        def load_weights(sp, n, s, first=False):
            if not first:
                sp.wait_ge(lo_ready[s], n)
            sp.dma_start(w_raw[s][:], w_stream[n, s]).then_inc(raw_loaded[s], 16)

        def split_hi(act, n, s, first=False):
            act.wait_ge(raw_loaded[s], 16 * n + 16)
            if not first:
                act.wait_ge(blk_done[s], n)
            nc.scalar.activation(w_hi[s][:], w_raw[s][:].rearrange("p (k c) -> p k c", k=KT), ACT.Copy).then_inc(hi_ready[s], 1)

        def split_lo(dve, n, s):
            dve.wait_ge(hi_ready[s], n + 1)
            nc.vector.tensor_tensor(w_lo[s][:], w_raw[s][:].rearrange("p (k c) -> p k c", k=KT),
                                    w_hi[s][:].bitcast(f32), ALU.subtract).then_inc(lo_ready[s], 1)

        def product_step(pe, n, s, hf, k, a_hi, a_lo):
            if hf == 0 and k == 0:
                pe.wait_ge(lo_ready[s], n + 1)
            t = slice(HALF * hf, HALF * hf + HALF)
            nc.tensor.matmul(g_bank[hf][:], w_hi[s][:, k, :], a_hi[:, k, t], start=(k == 0), stop=False)
            nc.tensor.matmul(g_bank[hf][:], w_hi[s][:, k, :], a_lo[:, k, t], start=False, stop=False)
            last = nc.tensor.matmul(g_bank[hf][:], w_lo[s][:, k, :], a_hi[:, k, t], start=False, stop=(k == KT - 1))
            if k == KT - 1:
                last.then_inc(half_ready if hf == 0 else blk_done[s], 1)

        def product_half(pe, n, s, hf, a_hi, a_lo, fills, ready=None):
            pe.wait_ge(bank_read[hf], 1 + fills)
            for k in range(KT):
                if ready is not None and hf == 0:
                    pe.wait_ge(*ready(k))
                product_step(pe, n, s, hf, k, a_hi, a_lo)

        def wait_half(eng, n, s, hf, halves):
            if hf == 0:
                eng.wait_ge(half_ready, halves + 1)
            else:
                eng.wait_ge(blk_done[s], n + 1)

        def take_projection(act, n, s, hf, func):
            wait_half(act, n, s, hf, 2 * n + s)
            if hf == 0:
                act.wait_ge(stored[s], 1 + 16 * n)
            settle(act)
            nc.scalar.activation(stage[s][:, HALF * hf:HALF * hf + HALF], g_bank[hf][:], func,
                                 bias=cols[:, ds(V_BIN + 2 * n + s, 1)]).then_inc(bank_read[hf], 1)

        def store_projection(sp, n, s):
            sp.wait_ge(bank_read[0], 1 + 2 * n + s + 1)
            sp.wait_ge(bank_read[1], 1 + 2 * n + s + 1)
            sp.dma_start(pT[2 * n + s], stage[s][:]).then_inc(stored[s], 16)

        def exp_ln_tables():
            nc.scalar.preload_act_table_set("natural_log_exp_and_others")

        def sp_block(sp, n, s):
            load_weights(sp, n + 1, s)
            store_projection(sp, n, s)

        def act_block(act, n, s, func):
            take_projection(act, n, s, 0, func)
            take_projection(act, n, s, 1, func)
            split_hi(act, n + 1, s)

        def pe_block(pe, n, s, a_hi, a_lo, extra):
            for hf in range(2):
                product_half(pe, n, s, hf, a_hi, a_lo, 2 * n + s + extra)

        MIX_BRANCH = 12
        HALF_BRANCH = 24

        class Beside:

            def __init__(self, n0, weights, funcs):
                self.n0, self.funcs, self.slot, self.at, self.sum = n0, funcs, 0, 0, 0.0
                self.weights, self.total = weights, 32 * len(funcs)

            def steps(self):
                self.sum += self.weights[self.slot]
                self.slot += 1
                end = self.total if self.slot == len(self.weights) else int(self.total * self.sum / sum(self.weights))
                out = range(self.at, end)
                self.at = end
                return out

        def pe_beside(pe, b):
            for step in b.steps():
                blk, r = divmod(step, 16)
                hf, k = divmod(r, 8)
                n, s = b.n0 + blk // 2, blk % 2
                if k == 0:
                    pe.wait_ge(bank_read[hf], 1 + 2 * n + s)
                product_step(pe, n, s, hf, k, act_hi, act_lo)

        def act_beside(act, b):
            for step in b.steps():
                blk, r = divmod(step, 16)
                n, s = b.n0 + blk // 2, blk % 2
                if r == 7:
                    take_projection(act, n, s, 0, b.funcs[blk // 2])
                if r == 15:
                    take_projection(act, n, s, 1, b.funcs[blk // 2])
                    if b.funcs[blk // 2] == ACT.Gelu and s == 1:
                        exp_ln_tables()
                    split_hi(act, n + 1, s)

        def dve_beside(dve, b):
            for step in b.steps():
                blk, r = divmod(step, 16)
                if r == 15:
                    split_lo(dve, b.n0 + blk // 2 + 1, blk % 2)

        def norm_squares(act, i, src, buf, ready=None):
            for k in range(KT):
                if ready is not None:
                    act.wait_ge(*ready(k))
                if k >= 3:
                    act.wait_ge(sq_added, 7 * max(0, i - 1) + k - 2)
                elif i:
                    act.wait_ge(ss_ready, i)
                nc.scalar.activation(buf[k % 3][:], src(k), ACT.Square).then_inc(sq_ready, 1)

        def norm_add(dve, i, buf, acc):
            for k in range(1, KT):
                dve.wait_ge(sq_ready, 8 * max(0, i - 1) + k + 1)
                if k > 1:
                    dve.wait_ge(sq_added, 7 * max(0, i - 1) + k - 1)
                elif i:
                    dve.wait_ge(ss_ready, i)
                nc.vector.tensor_tensor(acc[:], buf[0][:] if k == 1 else acc[:], buf[k % 3][:], ALU.add).then_inc(sq_added, 1)

        def normalised(dve, i, src, gain, rstd, buf):
            base = KT * min(i, 1)
            for k in range(KT + 1):
                if k < KT:
                    if k >= 2:
                        dve.wait_ge(hh_ready, base + k - 1)
                        dve.wait_ge(hl_ready, base + k - 1)
                    nc.vector.scalar_tensor_tensor(buf[k % 2][:], src[:, k, :], cols[:, gain + k:gain + k + 1], rstd[:],
                                                   ALU.mult, ALU.mult).then_inc(h_ready, 1)
                if k:
                    dve.wait_ge(hh_ready, base + k)
                    nc.vector.tensor_tensor(act_lo[:, k - 1, :], buf[(k - 1) % 2][:], act_hi[:, k - 1, :].bitcast(f32), ALU.subtract).then_inc(hl_ready, 1)

        def norm_sums(pe, i, acc):
            if i == 1:
                pe.wait_ge(w_added, 10)
            else:
                pe.wait_ge(sq_added, 7 * max(0, i - 1) + 7)
            for hf in range(2):
                if i:
                    pe.wait_ge(ln_ready, 2 * i)
                last = nc.tensor.matmul(d_bank[hf][:], ones, acc[:, HALF * hf:HALF * hf + HALF], start=True, stop=True)
            last.then_inc(ss_ready, 1)

        def norm_root(act, i, out, scale=1.0 / D):
            act.wait_ge(ss_ready, i + 1)
            for hf in range(2):
                nc.scalar.activation(out[:, HALF * hf:HALF * hf + HALF], d_bank[hf][:], ACT.Ln, scale=scale, bias=eps).then_inc(ln_ready, 1)
            act.wait_ge(ln_ready, 2 * i + 2)
            nc.scalar.activation(out[:], out[:], ACT.Exp, scale=-0.5).then_inc(rstd_ready, 1)

        STEPS = [(T, u, j) for T in range(2) for u in range(2) for j in range(4 * T + 3, -1, -1)]
        NST = len(STEPS)

        def first_col(T, j):
            return max(0, P * j - HALF * T)

        def group_of(x):
            T, u, j = STEPS[x]
            return 2 * T + u, j == 4 * T + 3, j == 0

        def is_diag(T, j):
            return j >= 4 * T

        DIAGS = [sum(is_diag(STEPS[y][0], STEPS[y][2]) for y in range(x + 1)) for x in range(NST)]
        N_DIAG = DIAGS[-1]
        R_BEFORE = [sum(not group_of(y)[2] for y in range(x)) for x in range(NST)]
        N_R = NST - 4
        LAG = 3

        DN_STAGES = ["rowg", "rowb", "gram", "qk", "kT", "vT", "t0"]
        for lev in range(1, N_LEV):
            DN_STAGES += [f"x{lev}", f"y{lev}"] + ([f"t{lev}"] if lev < N_LEV - 1 else [])
        DN_STAGES += ["w"]
        NDS = len(DN_STAGES)
        DN_USES = NDS + 3
        DVE_CHAIN = 8
        DN_FUNCS = (ACT.Identity, ACT.Identity, ACT.Gelu)
        DN_SLOTS = [8.0] * 4 + [5.0] * 2 + [1.6] * 12 + [0.35] * (2 * NDS - 12) + [1.5] * (2 * NCH) + [4.0] * 2
        SG_SLOTS = [16, 12] + [3] * 8 + [8] + [8.5] * 8
        AT_SLOTS = [1.5] + [1] * (NST + LAG)

        block = top.enter_context(nc.Block())

        @block.sync
        def _(sp):
            for r in range(4):
                sp.dma_start(x_sb[:, 2 * r:2 * r + 2, :], xT[2 * r:2 * r + 2].rearrange("k p s -> p k s")).then_inc(x_in[r], 16)
            sp.dma_start(cols[:], cols_in).then_inc(loaded, 16)
            sp.dma_start(consts[:], consts_in).then_inc(loaded, 16)
            sp.dma_start(wbd[:], w_bd).then_inc(loaded, 16)
            for s in range(2):
                load_weights(sp, 0, s, first=True)
            for one in (*bank_read, *stored, dn_yst, w_added, *dn_taken, *y_stored, z_ready, dn_chain, ml_ready, av_read, f_lr):
                sp.sem_inc(one, 1)
            with sp.Fori(0, N_SB) as i:
                for s in range(2):
                    sp_block(sp, i, s)
            for s in range(2):
                sp.wait_ge(stored[s], 1 + 16 * N_SB)
            end_phase(sp, 1)
            with sp.Fori(0, 4) as i:
                sp.wait_ge(z_ready, 1 + NST * i)
                sp.wait_ge(pad_zero, 2)
                sp.dma_start(a_q[:], pT[i + ROW_SQ]).then_inc(at_loaded, 16)
                for u in range(2):
                    sp.dma_start(a_k[64 * u:64 * u + 64, u, :], pT[i + ROW_SK, 64 * u:64 * u + 64]).then_inc(at_loaded, 16)
                sp.dma_start(a_vT[:], pT[i + ROW_SV]).then_inc(at_loaded, 16)
                for b in range(4):
                    sp_block(sp, PAIR_AT + 2 * i + b // 2, b % 2)
            for T in range(2):
                sp.wait_ge(y_stored[T], 1 + 16 * 4)
            for s in range(2):
                sp.wait_ge(stored[s], 1 + 16 * PAIR_DN)
            end_phase(sp, 2)
            for j, row in enumerate((ROW_DQ, ROW_DK, ROW_DV)):
                sp.dma_start(d_in[j][:, 3:], pT[row]).then_inc(dn_loaded, 16)
            with sp.Fori(0, 4) as i:
                sp.wait_ge(dn_yst, 1 + 16 * i)
                sp.dma_start(d_z[:], pT[i + ROW_DZ]).then_inc(dn_z, 16)
                sp_block(sp, PAIR_DN + 3 * i, 0)
                sp.wait_ge(dn_conv, 12 * i + 12)
                for j, row in enumerate((ROW_DQ, ROW_DK, ROW_DV)):
                    sp.dma_start(d_in[j][:, 3:], pT[i + 1 + row]).then_inc(dn_loaded, 16)
                for b in range(1, 6):
                    sp_block(sp, PAIR_DN + 3 * i + b // 2, b % 2)
                sp.wait_ge(dn_out, 2 * i + 2)
                sp.dma_start(yT[4 + i], d_o[:]).then_inc(dn_yst, 16)
            sp.wait_ge(dn_yst, 1 + 64)
            sp.wait_ge(dn_loaded, 48 * 5)
            for s in range(2):
                sp.wait_ge(stored[s], 1 + 16 * PAIR_SG)
            end_phase(sp, 3)
            for r in range(2):
                sp.dma_start(g_v[:, 2 * r:2 * r + 2, :], pT[ROW_V[r]:ROW_V[r] + 2].rearrange("k p s -> p k s")).then_inc(g_load, 16)
            sp.dma_start(g_w[:], w_spT).then_inc(gw_load, 16)
            for r in range(2):
                sp.dma_start(g_u[:, 2 * r:2 * r + 2, :], pT[ROW_U[r]:ROW_U[r] + 2].rearrange("k p s -> p k s")).then_inc(gu_load, 16)
            for b in range(8):
                sp_block(sp, PAIR_SG + b // 2, b % 2)
                if b >= 4:
                    sp.wait_ge(g_out, b - 3)
                    sp.dma_start(yT[b - 4], g_y[b % 2][:]).then_inc(g_store[b % 2], 16)
            for s in range(2):
                sp.wait_ge(g_store[s], 32)
            for s in range(2):
                sp.wait_ge(stored[s], 1 + 16 * PAIR_BR)
            end_phase(sp, 4)
            for b in range(3):
                sp.dma_start(y_lo[:, 4 * b:4 * b + 4, :].bitcast(f32), yT[4 * b:4 * b + 4].rearrange("k p s -> p k s")).then_inc(y_ld[b], 16)
            with sp.Fori(0, 2) as i:
                for q in range(6):
                    n, s = PAIR_BR + 3 * i + q // 2, q % 2
                    load_weights(sp, n + 1, s)
                    for r in range(4):
                        dd, hf = divmod(r, 2)
                        j, branch = divmod(q, 3)
                        row = ROW_GATE2 + 4 * i + 2 * j + dd if branch == 2 else ROW_GATE01 + 12 * i + 6 * j + 2 * branch + dd
                        sp.wait_ge(bank_read[hf], 1 + 2 * PAIR_BR + 12 * i + 2 * q + dd)
                        sp.dma_start(gate[r % 2][:], pT[row, :, HALF * hf:HALF * hf + HALF]).then_inc(gate_ld[r % 2], 16)
            end_phase(sp, 5)
            with sp.Fori(0, 4) as i:
                for s in range(2):
                    load_weights(sp, PAIR_OUT + i + 1, s)
            for k in range(KT):
                if k >= 2:
                    sp.wait_ge(x1_ready, k - 1)
                sp.dma_start(n_x[k % 2][:], xT[k]).then_inc(ld[k % 2], 16)
            for k in range(KT):
                sp.wait_ge(x1_ready, k + 1)
                sp.dma_start(x1T[k], mixed[:, k, :]).then_inc(x1_st, 16)
            sp.wait_ge(x1_st, 16 * KT)
            end_phase(sp, 6)
            with sp.Fori(PAIR_FF, N_PAIRS - 1) as n:
                for s in range(2):
                    load_weights(sp, n + 1, s)
            end_phase(sp, 7)
            sp.dma_start(x_fin[:], x1T.rearrange("k p s -> p k s")).then_inc(x_ld, 16)
            for k in range(KT):
                sp.wait_ge(out_ready, k + 1)
                sp.dma_start(outT[k], x_fin[:, k, :]).then_inc(out_st, 16)
            sp.wait_ge(out_st, 16 * KT)

        @block.scalar
        def _(act):
            exp_ln_tables()
            norm_squares(act, 0, lambda k: x_sb[:, k, :], sq0, ready=lambda k: (x_in[k // 2], 16))
            for s in range(2):
                split_hi(act, 0, s, first=True)
            act.wait_ge(loaded, 48)
            nc.scalar.activation(wbd_parts[:], ident[:, None, :].broadcast_to([P, KT, P]), ACT.Copy, scale=0.0).then_inc(wbd_zero, 1)
            act.wait_ge(wbd_zero, 1)
            nc.scalar.activation(wbd_parts[:, :, 0:8], wbd[:], ACT.Copy).then_inc(small, 1)
            norm_root(act, 0, rstd0)
            for k in range(KT):
                act.wait_ge(h_ready, k + 1)
                nc.scalar.activation(act_hi[:, k, :], hbuf[k % 2][:], ACT.Copy).then_inc(hh_ready, 1)
            with act.Fori(0, N_SB - 1) as i:
                for s in range(2):
                    act_block(act, i, s, ACT.Identity)
            act.wait_ge(small, 3)
            nc.scalar.activation(bd_beta[:], bd[:, :, 0:4].rearrange("p n h -> p h n"), ACT.Sigmoid).then_inc(small, 1)
            act.wait_ge(small, 6)
            nc.scalar.activation(bt[2][:], bt[1][:], ACT.Exp).then_inc(small, 1)
            act.wait_ge(small, 7)
            nc.scalar.activation(bt[2][:], bt[2][:], ACT.Ln, bias=1.0).then_inc(small, 1)
            for h in range(4):
                last = nc.scalar.activation(bt[3][:, h, :], cols[:, V_ALOG + h:V_ALOG + h + 1].broadcast_to([P, NCH]), ACT.Exp)
            last.then_inc(small, 1)
            act_block(act, N_SB - 1, 0, ACT.Identity)
            act.wait_ge(small, 12)
            nc.scalar.activation(bt[4][:], bd_gc[:], ACT.Exp).then_inc(small, 1)
            act_block(act, N_SB - 1, 1, ACT.Identity)
            end_phase(act, 1)
            for tri, c in ((a_from, lo_incl), (a_ones, ones)):
                last = nc.scalar.activation(tri[:], c, ACT.Copy)
            last.then_inc(tri_ready, 1)
            exp_ln_tables()
            with act.Fori(0, 4) as i:
                b = Beside(PAIR_AT + 2 * i, AT_SLOTS, (ACT.Identity,) * 2)
                act_beside(act, b)
                for hf in range(2):
                    act.wait_ge(at_vt, 2 * i + hf + 1)
                    src = z_bank[hf][:].rearrange("p (n c) -> p n c", c=P)
                    for u in range(2):
                        last = nc.scalar.activation(a_v[:, 4 * hf:4 * hf + 4, u, 64 * u:64 * u + 64], src[:, :, 64 * u:64 * u + 64], ACT.Copy)
                    last.then_inc(at_v, 1)

                def cols_of(x):
                    return slice(first_col(STEPS[x][0], STEPS[x][2]), HALF)

                def copy_z(x):
                    act.wait_ge(z_ready, 1 + NST * i + x + 1)
                    if x >= 4:
                        act.wait_ge(arg_ready, NST * i + x - 3)
                    nc.scalar.activation(a_z[x % 4][:, cols_of(x)], z_bank[x % 2][:, cols_of(x)], ACT.Copy, scale=0.125).then_inc(z_read, 1)

                def exp_arg(x):
                    T, u, j = STEPS[x]
                    act.wait_ge(arg_ready, NST * i + x + 1)
                    a = a_A[u][:, j, cols_of(x)]
                    nc.scalar.activation(a, a, ACT.Exp).then_inc(a_ready, 1)

                def exp_z(x):
                    e = a_e[x % 3][:, cols_of(x)]
                    act.wait_ge(na_ready, NST * i + x + 1)
                    nc.scalar.activation(e, e, ACT.Exp).then_inc(e_ready, 1)

                def ln_z(x):
                    e = a_e[x % 3][:, cols_of(x)]
                    act.wait_ge(e_ready, NST * i + x + 1)
                    nc.scalar.activation(e, e, ACT.Ln, bias=1.0).then_inc(l_ready, 1)

                def upper_sp(x):
                    act.wait_ge(sp_ready, NST * i + x + 1)
                    if x >= 2:
                        act.wait_ge(cum_ready, NST * i + x - 1)
                    nc.scalar.activation(a_sp_hi[x % 2][:, cols_of(x)], a_sp[x % 3][:, cols_of(x)], ACT.Copy).then_inc(sp_hi_ready, 1)

                def upper_R(x):
                    c = first_col(STEPS[x][0], STEPS[x][2])
                    act.wait_ge(r_sum, N_R * i + R_BEFORE[x] + 1)
                    if x >= 2:
                        act.wait_ge(cum_ready, NST * i + x)
                    nc.scalar.activation(a_R_hi[x % 2][:, c:HALF], a_R[x % 2][:, c:HALF], ACT.Copy).then_inc(r_hi, 1)

                def out_av(T):
                    act.wait_ge(av_done, 4 * i + 2 * T + 2)
                    act.wait_ge(y_stored[T], 1 + 16 * i)
                    nc.scalar.activation(a_y[T][:], o_bank[:], ACT.Copy).then_inc(av_read, 1)
                    act.wait_ge(av_read, 1 + 2 * i + T + 1)
                    act.dma_start(yT[8 + i, :, HALF * T:HALF * T + HALF], a_y[T][:]).then_inc(y_stored[T], 16)

                copy_z(0)
                for x in range(NST + LAG):
                    if 1 <= x < NST + 1:
                        upper_sp(x - 1)
                    if x < NST:
                        exp_z(x)
                    if x + 1 < NST:
                        copy_z(x + 1)
                    if x < NST:
                        ln_z(x)
                    if 1 <= x < NST and not group_of(x - 1)[2]:
                        upper_R(x - 1)
                    if 2 <= x < NST + 2:
                        exp_arg(x - 2)
                    act_beside(act, b)
                    if x >= 4 and group_of(x - 4)[2] and STEPS[x - 4][1] == 1:
                        out_av(STEPS[x - 4][0])
                out_av(1)
            end_phase(act, 2)
            with act.Fori(0, 4) as i:
                b = Beside(PAIR_DN + 3 * i, DN_SLOTS, DN_FUNCS)

                def beside():
                    act_beside(act, b)

                beside()
                for j in range(3):
                    act.wait_ge(dn_conv, 12 * i + 4 * j + 4)
                    nc.scalar.activation(d_cv[j][:], d_cv[j][:], ACT.Silu).then_inc(dn_silu, 1)
                    beside()
                act.wait_ge(dn_z, 16 * i + 16)
                nc.scalar.activation(d_z[:], d_z[:], ACT.Silu).then_inc(dn_silu, 1)
                exp_ln_tables()
                for j, sq in enumerate((d_eg, d_dt)):
                    act.wait_ge(dn_silu, 4 * i + j + 1)
                    nc.scalar.activation(sq[:].rearrange("p n c -> p (n c)"), d_cv[j][:], ACT.Square).then_inc(dn_sq, 1)
                r = d_wt[:].rearrange("p n c -> p (n c)")

                def inverse_root(use, scale):
                    for g in range(2):
                        act.wait_ge(dn_prod[g], DN_USES * i + use)
                        nc.scalar.activation(r[:, HALF * g:HALF * g + HALF], d_bank[g][:], ACT.Ln, scale=scale, bias=eps).then_inc(dn_taken[g], 1)
                    for g in range(2):
                        act.wait_ge(dn_taken[g], 1 + DN_USES * i + use)
                    nc.scalar.activation(r, r, ACT.Exp, scale=-0.5).then_inc(dn_root, 1)

                for j in range(2):
                    act.wait_ge(dn_chain, 1 + 4 * i + j)
                    inverse_root(j + 1, 1.0)
                    beside()
                for x, name in enumerate(DN_STAGES):
                    for g in range(2):
                        c = slice(4 * g, 4 * g + 4)
                        p3 = d_bank[g][:].rearrange("p (n c) -> p n c", c=P)
                        if name == "rowg":
                            act.wait_ge(dn_prod[g], DN_USES * i + 3 + x)
                            act.wait_ge(dn_taken[g], 1 + DN_USES * i + 2 + x)
                            nc.scalar.activation(d_eg[:, c, :], p3, ACT.Exp).then_inc(dn_eg[g], 1)
                            act.wait_ge(dn_min[g], i + 1)
                            nc.scalar.activation(d_tail[:, c], d_tail[:, c], ACT.Exp).then_inc(dn_eg[g], 1)
                            nc.scalar.activation(d_dt[:, c, :], d_dt[:, c, :], ACT.Exp).then_inc(dn_eg[g], 1)
                        if name[0] in "xt" or name == "w":
                            act.wait_ge(dn_prod[g], DN_USES * i + 3 + x)
                            dst = d_X if name[0] == "x" else d_T if name[0] == "t" else d_wt
                            nc.scalar.activation(dst[:, c, :], p3, ACT.Copy, scale=-1.0 if name == "w" else 1.0).then_inc(dn_taken[g], 1)
                        beside()
                for n in range(NCH):
                    beside()
                    beside()
                    if n % 4 == 3:
                        act.wait_ge(dn_scan_mm, 16 * i + 2 * n + 2)
                        nc.scalar.activation(d_o[:, HALF * (n // 4):HALF * (n // 4) + HALF], d_bank[1][:], ACT.Copy).then_inc(dn_o, 1)
                act.wait_ge(dn_o, 2 * i + 2)
                nc.scalar.activation(d_X[:].rearrange("p n c -> p (n c)"), d_o[:], ACT.Square).then_inc(dn_sq, 1)
                for g in range(2):
                    beside()
                inverse_root(DN_USES, 1.0 / P)
            end_phase(act, 3)
            b8 = Beside(PAIR_SG, SG_SLOTS, (ACT.Identity,) * 4)
            act_beside(act, b8)
            act_beside(act, b8)
            for b in range(4):
                for hf in range(2):
                    x = 2 * b + hf
                    act.wait_ge(g_chain, 2 + x + 1)
                    if x >= 2:
                        act.wait_ge(g_pe, 2 + x - 1)
                    nc.scalar.activation(g_sq[x % 2][:], g_v[:, b, HALF * hf:HALF * hf + HALF], ACT.Square).then_inc(g_act, 1)
                    act_beside(act, b8)
            act.wait_ge(g_pe, 10)
            for hf in range(2):
                nc.scalar.activation(g_rstd[:, HALF * hf:HALF * hf + HALF], d_bank[hf][:], ACT.Ln, scale=1.0 / BW, bias=eps).then_inc(g_chain, 1)
            act.wait_ge(g_chain, 12)
            nc.scalar.activation(g_rstd[:], g_rstd[:], ACT.Exp, scale=-0.5).then_inc(g_chain, 1)
            act_beside(act, b8)
            for b in range(4):
                for hf in range(2):
                    act.wait_ge(g_pe, 10 + 4 * b + hf + 1)
                    if b:
                        act.wait_ge(g_pe, 10 + 4 * b)
                    nc.scalar.activation(g_vt[:, 4 * hf:4 * hf + 4, :], z_bank[hf][:].rearrange("p (n c) -> p n c", c=P), ACT.Copy).then_inc(g_act, 1)
                act_beside(act, b8)
                act_beside(act, b8)
            end_phase(act, 4)
            for k in range(12):
                act.wait_ge(y_ld[k // 4], 16)
                nc.scalar.activation(y_hi[:, k, :], y_lo[:, k, :].bitcast(f32), ACT.Copy).then_inc(yh_ready, 1)
            with act.Fori(0, 2) as i:
                for q in range(6):
                    n, s = PAIR_BR + 3 * i + q // 2, q % 2
                    for r in range(4):
                        dd, hf = divmod(r, 2)
                        act.wait_ge(gate_ld[hf], 16 * (12 * i + 2 * q + dd) + 16)
                        nc.scalar.activation(gate[hf][:], gate[hf][:], ACT.Sigmoid).then_inc(gate_sig[hf], 1)
                    split_hi(act, n + 1, s)
                    if q % 3 == 2:
                        for dd in range(2):
                            d = 4 * i + 2 * (q // 3) + dd
                            act.wait_ge(m_added, 16 * i + 8 * (q // 3) + 6 + 2 * dd)
                            settle(act)
                            nc.scalar.activation(tile_of(act_hi, d), m_acc[:, dd, :], ACT.Copy).then_inc(mh_ready, 1)
            end_phase(act, 5)
            exp_ln_tables()
            with act.Fori(0, 4) as i:
                for s in range(2):
                    n = PAIR_OUT + i
                    for hf in range(2):
                        wait_half(act, n, s, hf, 2 * n + s + HALF_BRANCH)
                        settle(act)
                        nc.scalar.activation(tile_of(mixed, 2 * i + s)[:, HALF * hf:HALF * hf + HALF], g_bank[hf][:], ACT.Copy).then_inc(bank_read[hf], 1)
                    split_hi(act, n + 1, s)
                    act.wait_ge(w_added, 2 * i + s + 1)
                    for hf in range(2):
                        act.wait_ge(bank_read[hf], 1 + 2 * n + s + 1 + MIX_BRANCH)
                    settle(act)
                    nc.scalar.activation(n_sq[s][:], tile_of(mixed, 2 * i + s), ACT.Square).then_inc(w_sq, 1)
            norm_root(act, 1, n_rstd)
            norm_squares(act, 2, lambda k: mixed[:, k, :], n_sq, ready=lambda k: (x1_ready, k + 1))
            norm_root(act, 2, n_rstd)
            for k in range(KT):
                act.wait_ge(h_ready, KT + k + 1)
                nc.scalar.activation(act_hi[:, k, :], n_h[k % 2][:], ACT.Copy).then_inc(hh_ready, 1)
            end_phase(act, 6)
            def ff_hi(blk, hf, count):
                act.wait_ge(f_sqr, count)
                settle(act)
                nc.scalar.activation(tile_of(f_hi, blk)[:, HALF * hf:HALF * hf + HALF], f_t[hf][:], ACT.Copy).then_inc(f_hr, 1)

            def ff_group(g, last=False):
                with act.Fori(0, 4) as i:
                    for s in range(2):
                        n = PAIR_FF + 8 * g + i
                        for hf in range(2):
                            c = 16 * g + 4 * i + 2 * s + hf
                            wait_half(act, n, s, hf, 2 * n + s + HALF_BRANCH)
                            act.wait_ge(f_lr, 1 + 16 * g + 4 * i + 2 * s)
                            nc.scalar.activation(f_t[hf][:], g_bank[hf][:], ACT.Relu).then_inc(bank_read[hf], 1)
                            ff_hi(2 * i + s, hf, c + 1)
                        split_hi(act, n + 1, s)
                with act.Fori(0, 3 if last else 4) as i:
                    for s in range(2):
                        split_hi(act, PAIR_FF + 8 * g + 4 + i + 1, s)

            with act.Fori(0, 3) as g:
                ff_group(g)
            ff_group(3, last=True)
            end_phase(act, 7)
            norm_squares(act, 3, lambda k: mixed[:, k, :], n_sq)
            norm_root(act, 3, n_rstd)

        @block.tensor
        def _(pe):
            pe.wait_ge(loaded, 48)
            norm_sums(pe, 0, ss0)
            for hf in range(2):
                product_half(pe, 0, 0, hf, act_hi, act_lo, 0, ready=lambda k: (hl_ready, k + 1))
            pe_block(pe, 0, 1, act_hi, act_lo, 0)
            with pe.Fori(1, N_SB - 2) as i:
                for s in range(2):
                    pe_block(pe, i, s, act_hi, act_lo, 0)
            pe.wait_ge(small, 2)
            for hf in range(2):
                t = slice(HALF * hf, HALF * hf + HALF)
                for k in range(KT):
                    nc.tensor.matmul(z_bank[hf][:], wbd_parts[:, k, :], act_hi[:, k, t], start=(k == 0), stop=False)
                    last = nc.tensor.matmul(z_bank[hf][:], wbd_parts[:, k, :], act_lo[:, k, t], start=False, stop=(k == KT - 1))
                last.then_inc(bd_mm, 1)
            for s in range(2):
                pe_block(pe, N_SB - 2, s, act_hi, act_lo, 0)
            pe.wait_ge(bdT_ready, 2)
            for n in range(NCH):
                for part in range(2):
                    last = nc.tensor.matmul(c_bank[:, 8 * n:8 * n + 8], bdT[:, P * n:P * n + P], ident[0:16, 8 * part:8 * part + 8],
                                            start=(part == 0), stop=(part == 1))
            last.then_inc(bd_mm, 1)
            pe_block(pe, N_SB - 1, 0, act_hi, act_lo, 0)
            pe.wait_ge(small, 11)
            nc.tensor.matmul(z_bank[1][:, 0:32], up_incl, bd_g[:].rearrange("p h n -> p (h n)"), start=True, stop=True).then_inc(bd_mm, 1)
            pe_block(pe, N_SB - 1, 1, act_hi, act_lo, 0)
            end_phase(pe, 1)
            pe.wait_ge(tri_ready, 1)
            with pe.Fori(0, 4) as i:
                b = Beside(PAIR_AT + 2 * i, AT_SLOTS, (ACT.Identity,) * 2)
                pe_beside(pe, b)
                pe.wait_ge(at_loaded, 64 * i + 64)
                for hf in range(2):
                    for n in range(4):
                        last = nc.tensor.transpose(z_bank[hf][:, P * n:P * n + P], a_vT[:, P * (4 * hf + n):P * (4 * hf + n) + P], ident)
                    last.then_inc(at_vt, 1)

                def scores(x):
                    T, u, j = STEPS[x]
                    c = first_col(T, j)
                    if x < 2:
                        pe.wait_ge(at_v, 2 * i + x + 1)
                    else:
                        pe.wait_ge(z_read, NST * i + x - 1)
                    nc.tensor.matmul(z_bank[x % 2][:, c:HALF], a_k[:, u, P * j:P * j + P], a_q[:, HALF * T + c:HALF * T + HALF],
                                     start=True, stop=True).then_inc(z_ready, 1)

                def sums_above(x):
                    T, u, j = STEPS[x]
                    c, c1 = first_col(T, j), first_col(T, j + 1)
                    first = group_of(x)[1]
                    pe.wait_ge(sp_lo_ready, NST * i + x + 1)
                    if x >= 2:
                        pe.wait_ge(arg_ready, NST * i + x - 1)
                    nc.tensor.matmul(cum_bank[x % 2][:, c:HALF], a_from[:], a_sp_hi[x % 2][:, c:HALF], start=True, stop=False)
                    mm = nc.tensor.matmul(cum_bank[x % 2][:, c:HALF], a_from[:], a_sp_lo[x % 2][:, c:HALF], start=False, stop=first)
                    if not first:
                        pe.wait_ge(r_ready, N_R * i + R_BEFORE[x])
                        nc.tensor.matmul(cum_bank[x % 2][:, c1:HALF], a_ones[:], a_R_hi[(x - 1) % 2][:, c1:HALF], start=False, stop=False)
                        mm = nc.tensor.matmul(cum_bank[x % 2][:, c1:HALF], a_ones[:], a_R_lo[(x - 1) % 2][:, c1:HALF], start=False, stop=True)
                    mm.then_inc(cum_ready, 1)

                def weighted_values(x):
                    T, u, _ = STEPS[x]
                    pe.wait_ge(a_ready, NST * i + x + 1)
                    pe.wait_ge(a_masked, N_DIAG * i + DIAGS[x])
                    if u == 0:
                        pe.wait_ge(av_read, 1 + 2 * i + T)
                    for j in range(4 * T + 4):
                        c = first_col(T, j)
                        last = nc.tensor.matmul(o_bank[:, c:HALF], a_v[:, j, u, :], a_A[u][:, j, c:HALF],
                                                start=(u == 0 and j == 0), stop=(u == 1 and j == 4 * T + 3))
                    last.then_inc(av_done, 1)

                scores(0)
                scores(1)
                for x in range(NST + LAG):
                    if x + 2 < NST:
                        scores(x + 2)
                    pe_beside(pe, b)
                    if 1 <= x < NST + 1:
                        sums_above(x - 1)
                    if x >= 3 and group_of(x - 3)[2]:
                        weighted_values(x - 3)
            end_phase(pe, 2)
            with pe.Fori(0, 4) as i:
                b = Beside(PAIR_DN + 3 * i, DN_SLOTS, DN_FUNCS)

                def beside():
                    pe_beside(pe, b)

                def chunk(t, n):
                    return t[:, P * n:P * n + P]

                for j in range(4):
                    beside()
                for j, sq in enumerate((d_eg, d_dt)):
                    pe.wait_ge(dn_sq, 3 * i + j + 1)
                    for g in range(2):
                        pe.wait_ge(dn_taken[g], 1 + DN_USES * i + j)
                        nc.tensor.matmul(d_bank[g][:], ones, sq[:].rearrange("p n c -> p (n c)")[:, HALF * g:HALF * g + HALF],
                                         start=True, stop=True).then_inc(dn_prod[g], 1)
                    beside()
                for x, name in enumerate(DN_STAGES):
                    for g in range(2):
                        pe.wait_ge(dn_taken[g], 1 + DN_USES * i + 2 + x)
                        if name == "rowg":
                            pe.wait_ge(dn_chain, 1 + 4 * i + 4)
                            pe.wait_ge(dn_silu, 4 * i + 3)
                        if name == "t0":
                            pe.wait_ge(dn_tt[g], i + 1)
                        if name[0] == "x":
                            pe.wait_ge(dn_b[g], (N_LEV - 1) * i + int(name[1:]))
                        for m in range(4):
                            n = 4 * g + m
                            o = d_bank[g][:, P * m:P * m + P]
                            if name == "rowg":
                                last = nc.tensor.matmul(o, d_gB[:, n, :], up_incl, start=True, stop=True)
                            elif name == "rowb":
                                last = nc.tensor.matmul(o, d_bB[:, n, :], ident, start=True, stop=True)
                            elif name == "gram":
                                last = nc.tensor.matmul(o, chunk(d_cv[1], n), chunk(d_cv[1], n), start=True, stop=True)
                            elif name == "qk":
                                last = nc.tensor.matmul(o, chunk(d_cv[1], n), chunk(d_cv[0], n), start=True, stop=True)
                            elif name == "kT":
                                last = nc.tensor.transpose(o, chunk(d_cv[1], n), ident)
                            elif name == "vT":
                                last = nc.tensor.transpose(o, chunk(d_cv[2], n), ident)
                            elif name[0] == "t":
                                last = nc.tensor.transpose(o, d_TT[:, n, :], ident)
                            elif name[0] == "x":
                                last = nc.tensor.matmul(o, d_B[:, n, :], d_T[:, n, :], start=True, stop=True)
                            elif name[0] == "y":
                                last = nc.tensor.matmul(o, d_X[:, n, :], d_TT[:, n, :], start=True, stop=True)
                            else:
                                last = nc.tensor.matmul(o, d_kb[:, n, :], d_TT[:, n, :], start=True, stop=True)
                        last.then_inc(dn_prod[g], 1)
                        beside()
                for g in range(2):
                    pe.wait_ge(dn_taken[g], 1 + DN_USES * i + 2 + NDS)
                for n in range(NCH):
                    if n == 4:
                        pe.wait_ge(dn_o, 2 * i + 1)
                    o = d_bank[1][:, P * (n % 4):P * (n % 4) + P]
                    pe.wait_ge(dn_scan_ev, 17 * i + 1 + 2 * n)
                    nc.tensor.matmul(o, d_S[:], d_cv[0][:, P * n:P * n + P], start=True, stop=False)
                    nc.tensor.matmul(d_bank[0][:, 0:P], d_TT[:, n, :], d_vb[:, n, :], start=True, stop=False)
                    nc.tensor.matmul(d_bank[0][:, 0:P], d_wt[:, n, :], d_S[:], start=False, stop=True).then_inc(dn_scan_mm, 1)
                    beside()
                    pe.wait_ge(dn_scan_ev, 17 * i + 2 + 2 * n)
                    nc.tensor.matmul(o, d_vn[:], d_qk[:, n, :], start=False, stop=True)
                    nc.tensor.matmul(d_bank[0][:, P:2 * P], d_kt[:, n, :], d_vn[:], start=True, stop=True).then_inc(dn_scan_mm, 1)
                    beside()
                pe.wait_ge(dn_sq, 3 * i + 3)
                pe.wait_ge(dn_scan_ev, 17 * i + 17)
                for g in range(2):
                    nc.tensor.matmul(d_bank[g][:], ones, d_X[:].rearrange("p n c -> p (n c)")[:, HALF * g:HALF * g + HALF],
                                     start=True, stop=True).then_inc(dn_prod[g], 1)
                    beside()
            end_phase(pe, 3)
            b8 = Beside(PAIR_SG, SG_SLOTS, (ACT.Identity,) * 4)
            pe_beside(pe, b8)
            pe.wait_ge(g_load, 32)
            for hf in range(2):
                for b in range(4):
                    last = nc.tensor.matmul(d_bank[hf][:], ones, g_v[:, b, HALF * hf:HALF * hf + HALF], start=(b == 0), stop=(b == 3))
                last.then_inc(g_pe, 1)
            pe_beside(pe, b8)
            pe.wait_ge(g_chain, 2)
            for b in range(4):
                for hf in range(2):
                    pe.wait_ge(g_act, 2 * b + hf + 1)
                    nc.tensor.matmul(d_bank[hf][:], ones, g_sq[hf][:], start=(b == 0), stop=(b == 3)).then_inc(g_pe, 1)
                    pe_beside(pe, b8)
            pe_beside(pe, b8)
            pe.wait_ge(g_masked, 1)
            for b in range(4):
                pe.wait_ge(g_chain, 13 + 4 * b + 2)
                for hf in range(2):
                    if b:
                        pe.wait_ge(g_act, 8 + 2 * b)
                    for m in range(4):
                        n = 4 * hf + m
                        last = nc.tensor.transpose(z_bank[hf][:, P * m:P * m + P], g_n[:, P * n:P * n + P], ident)
                    last.then_inc(g_pe, 1)
                pe_beside(pe, b8)
                pe.wait_ge(g_act, 8 + 2 * b + 2)
                for hf in range(2):
                    if b:
                        pe.wait_ge(g_out, b)
                    for m in range(4):
                        for e in range(2):
                            last = nc.tensor.matmul(d_bank[hf][64 * e:64 * e + 64, P * m:P * m + P],
                                                    g_vt[:, 4 * hf + m, 64 * e:64 * e + 64], g_w[:, 2 * b + e, :], start=True, stop=True)
                    last.then_inc(g_pe, 1)
                pe_beside(pe, b8)
            end_phase(pe, 4)
            with pe.Fori(0, 2) as i:
                for q in range(6):
                    n, s = PAIR_BR + 3 * i + q // 2, q % 2
                    pe.wait_ge(lo_ready[s], n + 1)
                    pe.wait_ge(yl_ready, 4 * (q % 3) + 4)
                    for r in range(4):
                        dd, hf = divmod(r, 2)
                        t = slice(HALF * hf, HALF * hf + HALF)
                        pe.wait_ge(bank_read[hf], 1 + 2 * PAIR_BR + 12 * i + 2 * q + dd)
                        for k in range(4):
                            kk, y = 4 * dd + k, 4 * (q % 3) + k
                            nc.tensor.matmul(g_bank[hf][:], w_hi[s][:, kk, :], y_hi[:, y, t], start=(k == 0), stop=False)
                            nc.tensor.matmul(g_bank[hf][:], w_hi[s][:, kk, :], y_lo[:, y, t], start=False, stop=False)
                            last = nc.tensor.matmul(g_bank[hf][:], w_lo[s][:, kk, :], y_hi[:, y, t], start=False, stop=(k == 3))
                        last.then_inc(half_ready if r < 3 else blk_done[s], 1)
            end_phase(pe, 5)
            with pe.Fori(0, 4) as i:
                for s in range(2):
                    pe_block(pe, PAIR_OUT + i, s, act_hi, act_lo, MIX_BRANCH)
            norm_sums(pe, 1, n_ss)
            norm_sums(pe, 2, n_ss)
            end_phase(pe, 6)

            def ff_group(g):
                with pe.Fori(0, 4) as i:
                    for s in range(2):
                        pe_block(pe, PAIR_FF + 8 * g + i, s, act_hi, act_lo, MIX_BRANCH)
                pe.wait_ge(f_lr, 1 + 16 * g + 16)
                settle(pe)
                with pe.Fori(0, 4) as i:
                    for s in range(2):
                        pe_block(pe, PAIR_FF + 8 * g + 4 + i, s, f_hi, f_lo, MIX_BRANCH)

            with pe.Fori(0, 4) as g:
                ff_group(g)
            end_phase(pe, 7)
            norm_sums(pe, 3, n_ss)

        @block.vector
        def _(dve):
            norm_add(dve, 0, sq0, ss0)
            for s in range(2):
                split_lo(dve, 0, s)
            dve.wait_ge(loaded, 48)
            dve.wait_ge(small, 1)
            nc.vector.tensor_tensor(wbd_parts[:, :, 8:16], wbd[:], wbd_parts[:, :, 0:8].bitcast(f32), ALU.subtract).then_inc(small, 1)
            dve.wait_ge(rstd_ready, 1)
            normalised(dve, 0, x_sb, V_NORM, rstd0, hbuf)
            with dve.Fori(0, N_SB - 2) as i:
                for s in range(2):
                    split_lo(dve, i + 1, s)
            for hf in range(2):
                dve.wait_ge(bd_mm, hf + 1)
                nc.vector.tensor_copy(bdT[:, HALF * hf:HALF * hf + HALF], z_bank[hf][0:16, :]).then_inc(bdT_ready, 1)
            for s in range(2):
                split_lo(dve, N_SB - 1, s)
            dve.wait_ge(bd_mm, 3)
            nc.vector.tensor_tensor(bd[:], c_bank[:, 0:64].rearrange("p (n c) -> p n c", c=8),
                                    cols[:, None, V_BBD:V_BBD + 8].broadcast_to([P, NCH, 8]), ALU.add).then_inc(small, 1)
            dve.wait_ge(small, 4)
            nc.vector.tensor_tensor(bt[0][:], bd[:, :, 4:8].rearrange("p n h -> p h n"),
                                    cols[:, V_DTB:V_DTB + 4, None].broadcast_to([P, 4, NCH]), ALU.add).then_inc(small, 1)
            dve.wait_ge(small, 5)
            nc.vector.scalar_tensor_tensor(bt[1][:], bt[0][:], -1.0, bt[0][:], ALU.mult, ALU.min).then_inc(small, 1)
            dve.wait_ge(small, 9)
            nc.vector.scalar_tensor_tensor(bt[0][:], bt[0][:], 0.0, bt[2][:], ALU.max, ALU.add).then_inc(small, 1)
            dve.wait_ge(small, 10)
            nc.vector.scalar_tensor_tensor(bd_g[:], bt[0][:], -1.0, bt[3][:], ALU.mult, ALU.mult).then_inc(small, 1)
            split_lo(dve, N_SB, 0)
            dve.wait_ge(bd_mm, 4)
            nc.vector.tensor_copy(bd_gc[:].rearrange("p h n -> p (h n)"), z_bank[1][:, 0:32]).then_inc(small, 1)
            dve.wait_ge(small, 13)
            nc.vector.tensor_tensor(bd_egc[:], bt[4][:], bd_beta[:], ALU.mult).then_inc(small, 1)
            split_lo(dve, N_SB, 1)
            end_phase(dve, 1)
            with dve.Fori(0, 4) as i:
                b = Beside(PAIR_AT + 2 * i, AT_SLOTS, (ACT.Identity,) * 2)

                def cols_of(x):
                    return slice(first_col(STEPS[x][0], STEPS[x][2]), HALF)

                def minus_abs(x):
                    t, z = cols_of(x), a_z[x % 4]
                    dve.wait_ge(z_read, NST * i + x + 1)
                    nc.vector.scalar_tensor_tensor(a_e[x % 3][:, t], z[:, t], -1.0, z[:, t], ALU.mult, ALU.min).then_inc(na_ready, 1)

                def softplus(x):
                    T, u, j = STEPS[x]
                    c, t, sp = first_col(T, j), cols_of(x), a_sp[x % 3]
                    dve.wait_ge(l_ready, NST * i + x + 1)
                    if x >= 3:
                        dve.wait_ge(sp_lo_ready, NST * i + x - 2)
                        dve.wait_ge(r_ready, N_R * i + R_BEFORE[x - 2])
                    diag = is_diag(T, j)
                    nc.vector.scalar_tensor_tensor(sp[:, t], a_z[x % 4][:, t], 0.0, a_e[x % 3][:, t],
                                                   ALU.max, ALU.add).then_inc(sp_raw if diag else sp_ready, 1)
                    if diag:
                        dve.wait_ge(sp_raw, N_DIAG * i + DIAGS[x])
                        nc.vector.tensor_tensor(sp[:, c:c + P], sp[:, c:c + P], up_strict, ALU.mult).then_inc(sp_ready, 1)

                def lower_sp(x):
                    t = cols_of(x)
                    dve.wait_ge(sp_hi_ready, NST * i + x + 1)
                    if x >= 2:
                        dve.wait_ge(cum_ready, NST * i + x - 1)
                    nc.vector.tensor_tensor(a_sp_lo[x % 2][:, t], a_sp[x % 3][:, t], a_sp_hi[x % 2][:, t].bitcast(f32),
                                            ALU.subtract).then_inc(sp_lo_ready, 1)

                def argument(x):
                    T, u, j = STEPS[x]
                    t = cols_of(x)
                    dve.wait_ge(cum_ready, NST * i + x + 1)
                    if group_of(x)[1] and T == 1:
                        dve.wait_ge(av_done, 4 * i + u + 1)
                    nc.vector.tensor_tensor(a_A[u][:, j, t], a_z[x % 4][:, t], cum_bank[x % 2][:, t], ALU.subtract).then_inc(arg_ready, 1)

                dve_beside(dve, b)
                minus_abs(0)
                for x in range(NST + LAG):
                    if 1 <= x < NST + 1:
                        lower_sp(x - 1)
                    if 2 <= x < NST + 2:
                        argument(x - 2)
                    if x + 1 < NST:
                        minus_abs(x + 1)
                    if x < NST:
                        softplus(x)
                    dve_beside(dve, b)
            end_phase(dve, 2)
            for j in range(3):
                nc.vector.memset(d_in[j][:, 0:3], 0.0).then_inc(dn_dve, 1)
            dve.wait_ge(dn_dve, 3)
            with dve.Fori(0, 4) as i:
                b = Beside(PAIR_DN + 3 * i, DN_SLOTS, DN_FUNCS)

                def beside():
                    dve_beside(dve, b)

                beside()
                dve.wait_ge(dn_loaded, 48 * i + 48)
                for j in range(3):
                    w = V_CONV + 16 * j
                    if j == 2:
                        dve.wait_ge(dn_yst, 1 + 16 * i)
                    nc.vector.tensor_scalar(d_cv[j][:], d_in[j][:, 3:3 + S], cols[:, ds(w + 4 * i + 3, 1)], None, ALU.mult).then_inc(dn_conv, 1)
                    for tap in range(2, -1, -1):
                        dve.wait_ge(dn_conv, 12 * i + 4 * j + 3 - tap)
                        nc.vector.scalar_tensor_tensor(d_cv[j][:], d_in[j][:, tap:tap + S], cols[:, ds(w + 4 * i + tap, 1)], d_cv[j][:],
                                                       ALU.mult, ALU.add).then_inc(dn_conv, 1)
                    beside()
                r = d_wt[:].rearrange("p n c -> p (n c)")
                for j in range(2):
                    dve.wait_ge(dn_root, 3 * i + j + 1)
                    nc.vector.scalar_tensor_tensor(d_cv[j][:], d_cv[j][:], P ** -0.5 if j == 0 else 1.0, r, ALU.mult, ALU.mult).then_inc(dn_chain, 1)
                    beside()
                nc.vector.tensor_copy(d_gB[:], bd_g[:, ds(i, 1), :].rearrange("p h n -> p (h n)")[:, :, None].broadcast_to([P, NCH, P])).then_inc(dn_chain, 1)
                nc.vector.tensor_copy(d_bB[:], bd_beta[:, ds(i, 1), :].rearrange("p h n -> p (h n)")[:, :, None].broadcast_to([P, NCH, P])).then_inc(dn_chain, 1)
                dve.wait_ge(dn_chain, 1 + 4 * i + 4)

                def per_row(t, c):
                    return t[:, ds(i, 1), c].rearrange("p h n -> p (h n)")[:, :, None].broadcast_to([P, 4, P])

                def mask(m):
                    return m[:, None, :].broadcast_to([P, 4, P])

                def chained(ins):
                    local[0] += 1
                    ins.then_inc(dn_dve, 1)
                    dve.wait_ge(dn_dve, 3 + DVE_CHAIN * i + local[0])

                local = [0]
                for x, name in enumerate(DN_STAGES):
                    for g in range(2):
                        c = slice(4 * g, 4 * g + 4)
                        p3 = d_bank[g][:].rearrange("p (n c) -> p n c", c=P)
                        if name in ("rowg", "rowb", "gram", "qk", "kT", "vT") or name[0] == "y":
                            dve.wait_ge(dn_prod[g], DN_USES * i + 3 + x)
                        taken = DN_USES * i + 3 + x
                        if name == "rowg":
                            dve.wait_ge(dn_eg[g], 3 * i + 1)
                            nc.vector.tensor_tensor(d_dt[:, c, :], p3, per_row(bd_gc, c), ALU.subtract).then_inc(dn_taken[g], 1)
                            dve.wait_ge(dn_taken[g], 1 + taken)
                            chained(nc.vector.tensor_copy(d_tail[:, c], d_dt[:, c, P - 1]))
                            nc.vector.tensor_scalar(d_dt[:, c, :], d_dt[:, c, :], 0.0, None, ALU.min).then_inc(dn_min[g], 1)
                        elif name == "rowb":
                            dve.wait_ge(dn_eg[g], 3 * i + 3)
                            chained(nc.vector.tensor_tensor(d_dt[:, c, :], d_dt[:, c, :], mask(up_incl), ALU.mult))
                            nc.vector.tensor_tensor(d_at[:, c, :], p3, d_dt[:, c, :], ALU.mult).then_inc(dn_taken[g], 1)
                            dve.wait_ge(dn_taken[g], 1 + taken)
                            chained(nc.vector.tensor_tensor(d_at[:, c, :], d_at[:, c, :], mask(up_strict), ALU.mult))
                        elif name == "gram":
                            nc.vector.tensor_tensor(d_at[:, c, :], p3, d_at[:, c, :], ALU.mult).then_inc(dn_taken[g], 1)
                        elif name == "qk":
                            nc.vector.tensor_tensor(d_qk[:, c, :], p3, d_dt[:, c, :], ALU.mult).then_inc(dn_taken[g], 1)
                        elif name == "kT":
                            nc.vector.tensor_tensor(d_kb[:, c, :], p3, per_row(bd_egc, c), ALU.mult)
                            nc.vector.tensor_tensor(d_kt[:, c, :], p3, d_tail[:, c, None].broadcast_to([P, 4, P]), ALU.mult).then_inc(dn_taken[g], 1)
                            q3 = d_cv[0][:, HALF * g:HALF * g + HALF].rearrange("p (n c) -> p n c", c=P)
                            nc.vector.tensor_tensor(q3, q3, d_eg[:, c, :], ALU.mult)
                        elif name == "vT":
                            nc.vector.tensor_tensor(d_vb[:, c, :], p3, per_row(bd_beta, c), ALU.mult).then_inc(dn_taken[g], 1)
                            chained(nc.vector.tensor_tensor(d_TT[:, c, :], d_at[:, c, :], mask(consts[:, C_LEV, :]), ALU.mult))
                            nc.vector.scalar_tensor_tensor(d_TT[:, c, :], d_TT[:, c, :], -1.0, mask(ident), ALU.mult, ALU.add).then_inc(dn_tt[g], 1)
                        if name == "t0" or (name[0] == "y" and name != f"y{N_LEV - 1}"):
                            lev = int(name[1:])
                            if lev:
                                nc.vector.tensor_tensor(d_TT[:, c, :], d_TT[:, c, :], p3, ALU.subtract).then_inc(dn_taken[g], 1)
                            nc.vector.tensor_tensor(d_B[:, c, :], d_at[:, c, :], mask(consts[:, C_LEV + lev + 1, :]), ALU.mult).then_inc(dn_b[g], 1)
                        elif name[0] == "y":
                            nc.vector.tensor_tensor(d_TT[:, c, :], d_TT[:, c, :], p3, ALU.subtract).then_inc(dn_taken[g], 1)
                        beside()
                assert local[0] == DVE_CHAIN
                nc.vector.memset(d_S[:], 0.0).then_inc(dn_scan_ev, 1)
                for n in range(NCH):
                    dve.wait_ge(dn_scan_mm, 16 * i + 2 * n + 1)
                    nc.vector.tensor_copy(d_vn[:], d_bank[0][:, 0:P]).then_inc(dn_scan_ev, 1)
                    beside()
                    dve.wait_ge(dn_scan_mm, 16 * i + 2 * n + 2)
                    dve.wait_ge(dn_scan_ev, 17 * i + 2 * n + 2)
                    nc.vector.scalar_tensor_tensor(d_S[:], d_S[:], d_eg[:, n, P - 1:P], d_bank[0][:, P:2 * P],
                                                   ALU.mult, ALU.add).then_inc(dn_scan_ev, 1)
                    beside()
                for g in range(2):
                    beside()
                dve.wait_ge(dn_root, 3 * i + 3)
                nc.vector.scalar_tensor_tensor(d_o[:], d_o[:], cols[:, V_DNG:V_DNG + 1], r, ALU.mult, ALU.mult).then_inc(dn_out, 1)
                dve.wait_ge(dn_out, 2 * i + 1)
                dve.wait_ge(dn_silu, 4 * i + 4)
                nc.vector.tensor_tensor(d_o[:], d_o[:], d_z[:], ALU.mult).then_inc(dn_out, 1)
            end_phase(dve, 3)
            b8 = Beside(PAIR_SG, SG_SLOTS, (ACT.Identity,) * 4)
            dve_beside(dve, b8)
            for hf in range(2):
                dve.wait_ge(g_pe, hf + 1)
                nc.vector.tensor_scalar(g_mean[:, HALF * hf:HALF * hf + HALF], d_bank[hf][:], 1.0 / BW, None, ALU.mult).then_inc(g_chain, 1)
            dve_beside(dve, b8)
            dve.wait_ge(g_chain, 2)
            for b in range(4):
                for hf in range(2):
                    v = g_v[:, b, HALF * hf:HALF * hf + HALF]
                    nc.vector.tensor_tensor(v, v, g_mean[:, HALF * hf:HALF * hf + HALF], ALU.subtract).then_inc(g_chain, 1)
                    dve_beside(dve, b8)
            dve_beside(dve, b8)
            dve.wait_ge(gu_load, 32)
            for b in range(4):
                dve.wait_ge(g_chain, 13 + 4 * b)
                nc.vector.scalar_tensor_tensor(g_n[:], g_v[:, b, :], cols[:, V_LNG + b:V_LNG + b + 1], g_rstd[:], ALU.mult, ALU.mult).then_inc(g_chain, 1)
                dve.wait_ge(g_chain, 14 + 4 * b)
                nc.vector.tensor_scalar(g_n[:], g_n[:], cols[:, V_LNB + b:V_LNB + b + 1], None, ALU.add).then_inc(g_chain, 1)
                dve_beside(dve, b8)
                y = g_y[b % 2]
                if b >= 2:
                    dve.wait_ge(g_store[b % 2], 16)
                for hf in range(2):
                    t = slice(HALF * hf, HALF * hf + HALF)
                    dve.wait_ge(g_pe, 10 + 4 * b + 2 + hf + 1)
                    bias = cols[:, None, V_BSP + P * b:V_BSP + P * b + P].broadcast_to([P, 4, P])
                    nc.vector.tensor_tensor(y[:, t].rearrange("p (n c) -> p n c", c=P), d_bank[hf][:].rearrange("p (n c) -> p n c", c=P),
                                            bias, ALU.add).then_inc(g_chain, 1)
                dve.wait_ge(g_chain, 17 + 4 * b)
                nc.vector.tensor_tensor(y[:], y[:], g_u[:, b, :], ALU.mult).then_inc(g_out, 1)
                dve_beside(dve, b8)
            end_phase(dve, 4)
            for k in range(12):
                dve.wait_ge(yh_ready, k + 1)
                nc.vector.tensor_tensor(y_lo[:, k, :], y_lo[:, k, :].bitcast(f32), y_hi[:, k, :].bitcast(f32), ALU.subtract).then_inc(yl_ready, 1)
            with dve.Fori(0, 2) as i:
                for q in range(6):
                    n, s = PAIR_BR + 3 * i + q // 2, q % 2
                    for r in range(4):
                        dd, hf = divmod(r, 2)
                        acc = m_acc[:, dd, HALF * hf:HALF * hf + HALF]
                        if r < 3:
                            dve.wait_ge(half_ready, 2 * PAIR_BR + 18 * i + 3 * q + r + 1)
                        else:
                            dve.wait_ge(blk_done[s], n + 1)
                        uses = 12 * i + 2 * q + dd
                        dve.wait_ge(gate_sig[hf], uses + 1)
                        first = q % 3 == 0
                        added = 16 * i + 8 * (q // 3) + 4 * (q % 3 - 1) + r
                        if first:
                            dve.wait_ge(ml_ready, 1 + 4 * i + 2 * (q // 3))
                        else:
                            dve.wait_ge(m_added, added)
                        nc.vector.tensor_tensor(acc if first else m_t[:], g_bank[hf][:], gate[hf][:], ALU.mult).then_inc(bank_read[hf], 1)
                        if not first:
                            dve.wait_ge(bank_read[hf], 1 + 2 * PAIR_BR + uses + 1)
                            nc.vector.tensor_tensor(acc, acc, m_t[:], ALU.add).then_inc(m_added, 1)
                    split_lo(dve, n + 1, s)
                    if q % 3 == 2:
                        for dd in range(2):
                            d = 4 * i + 2 * (q // 3) + dd
                            dve.wait_ge(mh_ready, d + 1)
                            nc.vector.tensor_tensor(tile_of(act_lo, d), m_acc[:, dd, :], tile_of(act_hi, d).bitcast(f32), ALU.subtract).then_inc(ml_ready, 1)
            end_phase(dve, 5)
            nc.vector.memset(n_ss[:], 0.0).then_inc(w_added, 1)
            with dve.Fori(0, 4) as i:
                for s in range(2):
                    split_lo(dve, PAIR_OUT + i + 1, s)
                    dve.wait_ge(w_sq, 2 * i + s + 1)
                    dve.wait_ge(w_added, 2 * i + s + 2)
                    nc.vector.tensor_tensor(n_ss[:], n_ss[:], n_sq[s][:], ALU.add).then_inc(w_added, 1)
            dve.wait_ge(rstd_ready, 2)
            for k in range(KT):
                nc.vector.scalar_tensor_tensor(mixed[:, k, :], mixed[:, k, :], cols[:, V_NORM + 8 + k:V_NORM + 9 + k], n_rstd[:],
                                               ALU.mult, ALU.mult).then_inc(n_chain, 1)
                dve.wait_ge(n_chain, k + 1)
                dve.wait_ge(ld[k % 2], 16 * (k // 2 + 1))
                nc.vector.tensor_tensor(mixed[:, k, :], mixed[:, k, :], n_x[k % 2][:], ALU.add).then_inc(x1_ready, 1)
            norm_add(dve, 2, n_sq, n_ss)
            dve.wait_ge(rstd_ready, 3)
            normalised(dve, 2, mixed, V_NORM + 16, n_rstd, n_h)
            end_phase(dve, 6)

            def ff_group(g, first=False, last=False):
                with dve.Fori(0, 4) as i:
                    for s in range(2):
                        n = PAIR_FF + 8 * g + i
                        for hf in range(2):
                            c = 16 * g + 4 * i + 2 * s + hf
                            t = slice(HALF * hf, HALF * hf + HALF)
                            dve.wait_ge(bank_read[hf], 1 + 2 * n + s + 1 + MIX_BRANCH)
                            nc.vector.tensor_tensor(f_t[hf][:], f_t[hf][:], f_t[hf][:], ALU.mult).then_inc(f_sqr, 1)
                            dve.wait_ge(f_hr, c + 1)
                            nc.vector.tensor_tensor(tile_of(f_lo, 2 * i + s)[:, t], f_t[hf][:], tile_of(f_hi, 2 * i + s)[:, t].bitcast(f32),
                                                    ALU.subtract).then_inc(f_lr, 1)
                        split_lo(dve, n + 1, s)
                def add_pair(i, split):
                    for s in range(2):
                        n = PAIR_FF + 8 * g + 4 + i
                        for hf in range(2):
                            acc = tile_of(mixed, 2 * i + s)[:, HALF * hf:HALF * hf + HALF]
                            wait_half(dve, n, s, hf, 2 * n + s + HALF_BRANCH)
                            if first:
                                nc.vector.tensor_copy(acc, g_bank[hf][:]).then_inc(bank_read[hf], 1)
                            else:
                                nc.vector.tensor_tensor(acc, acc, g_bank[hf][:], ALU.add).then_inc(bank_read[hf], 1)
                        if split:
                            split_lo(dve, n + 1, s)

                with dve.Fori(0, 3 if last else 4) as i:
                    add_pair(i, True)
                if last:
                    add_pair(3, False)

            ff_group(0, first=True)
            with dve.Fori(1, 3) as g:
                ff_group(g)
            ff_group(3, last=True)
            end_phase(dve, 7)
            norm_add(dve, 3, n_sq, n_ss)
            dve.wait_ge(rstd_ready, 4)
            for k in range(KT):
                nc.vector.scalar_tensor_tensor(mixed[:, k, :], mixed[:, k, :], cols[:, V_NORM + 24 + k:V_NORM + 25 + k], n_rstd[:],
                                               ALU.mult, ALU.mult).then_inc(n_chain, 1)
                dve.wait_ge(n_chain, KT + k + 1)
                dve.wait_ge(x_ld, 16)
                nc.vector.tensor_tensor(x_fin[:, k, :], x_fin[:, k, :], mixed[:, k, :], ALU.add).then_inc(out_ready, 1)

        @block.gpsimd
        def _(pool):
            end_phase(pool, 1)
            nc.gpsimd.memset(a_k[:], 0.0).then_inc(pad_zero, 1)
            nc.gpsimd.memset(a_v[:], 0.0).then_inc(pad_zero, 1)
            with pool.Fori(0, 4) as i:
                for x in range(NST + 2):
                    if x >= 2 and is_diag(STEPS[x - 2][0], STEPS[x - 2][2]):
                        T, u, j = STEPS[x - 2]
                        c = first_col(T, j)
                        pool.wait_ge(a_ready, NST * i + x - 1)
                        nc.gpsimd.tensor_tensor(a_A[u][:, j, c:c + P], a_A[u][:, j, c:c + P], up_strict, ALU.mult).then_inc(a_masked, 1)
                    if 1 <= x < NST and not group_of(x - 1)[2]:
                        c = first_col(STEPS[x - 1][0], STEPS[x - 1][2])
                        pool.wait_ge(r_hi, N_R * i + R_BEFORE[x])
                        if x >= 3:
                            pool.wait_ge(cum_ready, NST * i + x - 1)
                        nc.gpsimd.tensor_tensor(a_R_lo[(x - 1) % 2][:, c:HALF], a_R[(x - 1) % 2][:, c:HALF],
                                                a_R_hi[(x - 1) % 2][:, c:HALF].bitcast(f32), ALU.subtract).then_inc(r_ready, 1)
                    if x < NST and not group_of(x)[2]:
                        c = first_col(STEPS[x][0], STEPS[x][2])
                        pool.wait_ge(sp_ready, NST * i + x + 1)
                        if group_of(x)[1]:
                            if x:
                                pool.wait_ge(r_ready, N_R * i + R_BEFORE[x])
                            settle(pool)
                            for R in a_R:
                                nc.gpsimd.memset(R[:, 0:c], 0.0)
                            nc.gpsimd.tensor_copy(a_R[x % 2][:, c:HALF], a_sp[x % 3][:, c:HALF]).then_inc(r_sum, 1)
                        else:
                            pool.wait_ge(r_sum, N_R * i + R_BEFORE[x])
                            if R_BEFORE[x] >= 2:
                                pool.wait_ge(r_ready, N_R * i + R_BEFORE[x] - 1)
                            nc.gpsimd.tensor_tensor(a_R[x % 2][:, c:HALF], a_R[(x - 1) % 2][:, c:HALF], a_sp[x % 3][:, c:HALF], ALU.add).then_inc(r_sum, 1)
            end_phase(pool, 2)
            end_phase(pool, 3)
            pool.wait_ge(gw_load, 16)
            nc.gpsimd.tensor_tensor(g_w[:], g_w[:], up_incl[:, None, :].broadcast_to([P, 8, P]), ALU.mult).then_inc(g_masked, 1)
            for k in range(4, 8):
                end_phase(pool, k)


def kernel(x, norm_g, w_in, b_in, sgu_ln_g, sgu_ln_b, w_spatial, b_spatial, conv_w, a_log, dt_bias, dn_norm_g,
           w_branch, w_out, w_ff1, w_ff2):
    import concourse.bacc as bacc
    from concourse.bass_utils import run_bass_kernel_spmd as run

    f = lambda a: np.asarray(a)
    x, w_in, b_in = f(x), f(w_in)[0], f(b_in)[0]
    w_branch, w_out, w_ff1, w_ff2 = f(w_branch)[0], f(w_out)[0], f(w_ff1)[0], f(w_ff2)[0]

    def tiles(w):
        r, c = w.shape
        return w.reshape(r // P, P, c // P, P).transpose(2, 1, 0, 3).reshape(c // P, P, r)

    starts = [c + P * t for c in (COL_SQ, COL_SQ + 512, COL_SQ + 1024,
                                  COL_DQ, COL_DQ + 512, COL_DQ + 1024, COL_DQ + 1536) for t in range(4)]
    for h in range(4):
        starts += [c + 256 * h + P * t for c in (COL_GATE, COL_GATE + 1024, COL_AU) for t in range(2)]
    starts += [COL_GATE + 2048 + P * t for t in range(8)]
    stream = [tiles(w_in[:, c:c + P]) for c in starts]
    for i in range(2):
        for q in range(6):
            c = 512 * i + 256 * (q // 3)
            stream.append(tiles(w_branch[q % 3][:, c:c + 256]).transpose(1, 0, 2).reshape(1, P, KT * P))
    stream.append(tiles(w_out))
    for g in range(4):
        stream.append(tiles(w_ff1[:, 1024 * g:1024 * g + 1024]))
        stream.append(tiles(w_ff2[1024 * g:1024 * g + 1024]))
    w_stream = np.ascontiguousarray(np.concatenate(stream).reshape(N_PAIRS, 2, P, KT * P))

    def by_partition(a):
        return a.reshape(-1, P).T

    def on_all(a):
        return np.broadcast_to(a.reshape(1, -1), (P, a.size))

    bsp = np.repeat(f(b_spatial)[0].reshape(4, 2, P), 64, axis=1)
    cw = f(conv_w)[0].reshape(4, 12, P).transpose(2, 1, 0).reshape(P, 48)
    cols = np.concatenate([
        by_partition(f(norm_g)[0]), np.stack([b_in[c:c + P] for c in starts], 1),
        by_partition(f(sgu_ln_g)[0]), by_partition(f(sgu_ln_b)[0]), cw, by_partition(f(dn_norm_g)[0]),
        on_all(f(a_log)[0]), on_all(f(dt_bias)[0]), on_all(b_in[COL_BETA:COL_BETA + 8]),
        bsp.transpose(1, 0, 2).reshape(P, 4 * P), np.full((P, 1), EPS, np.float32)], axis=1)

    p, c = np.arange(P)[:, None], np.arange(P)[None, :]
    levels = [(c >> (v + 1) == p >> (v + 1)) & ((c >> v) % 2 == 1) & ((p >> v) % 2 == 0) for v in range(N_LEV)]
    consts = np.stack([p == c, p >= 0 * c, p <= c, p < c, p >= c, *levels], axis=1).astype(np.float32)

    arrays = {
        "xT": np.ascontiguousarray(x[0].T.reshape(KT, P, S)),
        "w_stream": w_stream,
        "w_bd": np.ascontiguousarray(w_in[:, COL_BETA:COL_BETA + 8].reshape(KT, P, 8).transpose(1, 0, 2)),
        "w_spT": np.ascontiguousarray(f(w_spatial)[0].transpose(2, 0, 1)),
        "cols_in": np.ascontiguousarray(cols),
        "consts_in": consts,
    }
    nc = bacc.Bacc("TRN2", target_bir_lowering=False, num_devices=1)
    f32 = mybir.dt.float32
    args = [nc.dram_tensor(n, a.shape, f32, kind="ExternalInput").ap() for n, a in arrays.items()]
    out = nc.dram_tensor("outT", (KT, P, S), f32, kind="ExternalOutput").ap()
    hybrid_decoder_layer(nc, *args, out)
    r = run(nc, [arrays], core_ids=[0])
    y = r.results[0]["outT"].reshape(D, S)
    return np.ascontiguousarray(y.T)[None]
```

```python
import concourse.bass as bass
from concourse import mybir
from contextlib import ExitStack
import numpy as np

P = 128
D = 1024
S = 1024
KT = D // P
HALF = 512
BW = 512
EPS = 1e-6
NCH = S // P

N_SB = 6
PAIR_AT = 6
PAIR_DN = 14
PAIR_SG = 26
PAIR_BR = 30
PAIR_OUT = 36
PAIR_FF = 40
N_PAIRS = 72
ROW_SQ, ROW_SK, ROW_SV = 0, 4, 8
ROW_DQ, ROW_DK, ROW_DV, ROW_DZ = 12, 16, 20, 24
ROW_U, ROW_V = (32, 38), (44, 50)
ROW_GATE01 = 28
ROW_GATE2 = 52
BRANCHES = (1, 0, 2)
COL_AU, COL_AV, COL_DQ, COL_BETA, COL_SQ = 0, 512, 1024, 3072, 3080
COL_GATE = 4616

C_ID, C_UPI, C_UPS, C_LOI, C_LEV = 0, 1, 2, 3, 4
N_LEV = 7
N_CONST = C_LEV + N_LEV

V_NORM = 0
V_BIN = V_NORM + 32
V_LNG = V_BIN + 60
V_LNB = V_LNG + 4
V_CONV = V_LNB + 4
V_DNG = V_CONV + 48
V_ALOG = V_DNG + 1
V_DTB = V_ALOG + 4
V_BBD = V_DTB + 4
V_BSP = V_BBD + 8
N_COLS = V_BSP + 4 * P


def hybrid_decoder_layer(nc, xT, w_stream, w_bd, w_spT, cols_in, consts_in, outT):
    f32, f32r = mybir.dt.float32, mybir.dt.float32r
    ACT, ALU = mybir.ActivationFunctionType, mybir.AluOpType
    ds = bass.ds

    pT = nc.dram_tensor("projections", (60, P, S), f32, kind="Internal").ap()
    yT = nc.dram_tensor("branch_outputs", (12, P, S), f32, kind="Internal").ap()
    x1T = nc.dram_tensor("residual", (KT, P, S), f32, kind="Internal").ap()

    top = ExitStack()
    scope = [top]

    def sb(name, shape, dt=f32):
        return scope[0].enter_context(nc.sbuf_tensor(name, shape, dt))

    def sem(name):
        return top.enter_context(nc.semaphore(name))

    with top:
        consts = sb("consts", [P, N_CONST, P])
        cols = sb("cols", [P, N_COLS])
        ident = consts[:, C_ID, :]
        ones = sb("ones", [P, P])
        eps_tile = sb("eps", [P, 1])
        eps = eps_tile[:]
        up_incl, up_strict, lo_incl = consts[:, C_UPI, :], consts[:, C_UPS, :], consts[:, C_LOI, :]
        w_raw = [sb(f"w_raw{s}", [P, KT * P]) for s in range(2)]
        w_hi = [sb(f"w_hi{s}", [P, KT, P], f32r) for s in range(2)]
        w_lo = [sb(f"w_lo{s}", [P, KT, P], f32r) for s in range(2)]
        act_hi = sb("act_hi", [P, KT, S], f32r)
        act_lo = sb("act_lo", [P, KT, S], f32r)
        bd_g = sb("bd_g", [P, 4, NCH])
        bd_beta = sb("bd_beta", [P, 4, NCH])
        bd_gc = sb("bd_gc", [P, 4, NCH])
        bd_egc = sb("bd_egc", [P, 4, NCH])

        early = ExitStack()
        early.__enter__()
        scope[0] = early
        stage = [sb(f"stage{s}", [P, S]) for s in range(2)]

        scope[0] = ExitStack()
        with scope[0]:
            x_sb = sb("x_sb", [P, KT, S])
            sq0 = [sb(f"sq0_{s}", [P, S]) for s in range(3)]
            rstd0 = sb("rstd0", [P, S])
            hbuf = [sb(f"hbuf{s}", [P, S]) for s in range(4)]
            wbd = sb("wbd", [P, KT, 8])
            wbd_parts = sb("wbd_parts", [P, KT, P], f32r)
            bdT = sb("bdT", [16, S])
            bd = sb("bd", [P, NCH, 8])
            bt = [sb(f"bt{s}", [P, 4, NCH]) for s in range(5)]

        scope[0] = ExitStack()
        with scope[0]:
            d_in = [sb(f"d_in{s}", [P, 3 + S]) for s in range(3)]
            d_z = sb("d_z", [P, S])
            d_cv = [sb(f"d_cv{s}", [P, S]) for s in range(3)]
            d_gB = sb("d_gB", [P, NCH, P])
            d_bB = sb("d_bB", [P, NCH, P])
            d_eg = sb("d_eg", [P, NCH, P])
            d_dt = sb("d_dt", [P, NCH, P])
            d_at = sb("d_at", [P, NCH, P])
            d_qk = sb("d_qk", [P, NCH, P])
            d_kb = sb("d_kb", [P, NCH, P])
            d_kt = sb("d_kt", [P, NCH, P])
            d_vb = sb("d_vb", [P, NCH, P])
            d_TT = sb("d_TT", [P, NCH, P])
            d_T = sb("d_T", [P, NCH, P])
            d_wt = sb("d_wt", [P, NCH, P])
            d_tail = sb("d_tail", [P, NCH])
            d_S = sb("d_S", [P, P])
            d_vn = sb("d_vn", [P, P])
        d_X, d_B, d_r = d_gB, d_bB, d_eg
        d_o = d_cv[2]

        scope[0] = ExitStack()
        with scope[0]:
            a_q = sb("a_q", [P, S])
            a_k = sb("a_k", [P, 2, S])
            a_vT = sb("a_vT", [P, S])
            a_v = sb("a_v", [P, NCH, 2, P])
            a_z = [sb(f"a_z{s}", [P, HALF]) for s in range(4)]
            a_e = [sb(f"a_e{s}", [P, HALF]) for s in range(3)]
            a_sp = [sb(f"a_sp{s}", [P, HALF]) for s in range(3)]
            a_sp_hi = [sb(f"a_sp_hi{s}", [P, HALF], f32r) for s in range(2)]
            a_sp_lo = [sb(f"a_sp_lo{s}", [P, HALF], f32r) for s in range(2)]
            a_from = sb("a_from", [P, P], f32r)
            a_ones = sb("a_ones", [P, P], f32r)
            a_R = [sb(f"a_R{s}", [P, HALF]) for s in range(2)]
            a_R_hi = [sb(f"a_R_hi{s}", [P, HALF], f32r) for s in range(2)]
            a_R_lo = [sb(f"a_R_lo{s}", [P, HALF], f32r) for s in range(2)]
            a_A = [sb(f"a_A{s}", [P, NCH, HALF]) for s in range(2)]
            a_y = [sb(f"a_y{s}", [P, HALF]) for s in range(2)]

        scope[0] = ExitStack()
        with scope[0]:
            g_w = sb("g_w", [P, 8, P])
            g_v = sb("g_v", [P, 4, S])
            g_u = sb("g_u", [P, 4, S])
            g_sq = [sb(f"g_sq{s}", [P, HALF]) for s in range(2)]
            g_mean = sb("g_mean", [P, S])
            g_rstd = sb("g_rstd", [P, S])
            g_vt = sb("g_vt", [P, NCH, P])
            g_n = sb("g_n", [P, S])
            g_y = [sb(f"g_y{s}", [P, S]) for s in range(2)]

        early.close()

        scope[0] = ExitStack()
        with scope[0]:
            y_hi = sb("y_hi", [P, 8, S], f32r)
            y_lo = sb("y_lo", [P, 8, S], f32r)
            m_acc = sb("m_acc", [P, 2, S])
            y1_hi = sb("y1_hi", [P, 4, S], f32r)
            y1_lo = sb("y1_lo", [P, 4, S], f32r)
            gate = [sb(f"gate{s}", [P, HALF]) for s in range(2)]
            m_t = sb("m_t", [P, HALF])

        outer = ExitStack()
        with outer:
            scope[0] = outer
            mixed = sb("mixed", [P, KT, S])
            sum_sq = sb("sum_sq", [P, S])
            scope[0] = ExitStack()
            with scope[0]:
                n_sq = [sb(f"n_sq{s}", [P, S]) for s in range(3)]
                n_rstd = sb("n_rstd", [P, S])
                n_h = [sb(f"n_h{s}", [P, S]) for s in range(4)]
                x_fin = sb("x_fin", [P, KT, S])
            scope[0] = ExitStack()
            with scope[0]:
                f_hi = sb("f_hi", [P, KT, S], f32r)
                f_lo = sb("f_lo", [P, KT, S], f32r)
                f_t = [sb(f"f_t{s}", [P, HALF]) for s in range(2)]
                f_sq = [sb(f"f_sq{s}", [P, HALF]) for s in range(2)]
        scope[0] = top

        def bank(name):
            return top.enter_context(nc.psum_tensor(name, [P, HALF], f32))

        g_bank = [bank("gemm0"), bank("gemm1")]
        z_bank = [bank("z0"), bank("z1")]
        c_bank = bank("cumsum")
        o_bank = bank("attn_out")
        d_bank = [bank("dn0"), bank("dn1")]
        cum_bank = [c_bank, d_bank[0]]

        ones_set, cols_loaded = sem("ones_set"), sem("cols_loaded")
        loaded = sem("loaded")
        raw_loaded = [sem(f"raw_loaded{s}") for s in range(2)]
        hi_ready = [sem(f"hi_ready{s}") for s in range(2)]
        lo_ready = [sem(f"lo_ready{s}") for s in range(2)]
        blk_done = [sem(f"blk_done{s}") for s in range(2)]
        half_ready = sem("half_ready")
        bank_read = [sem(f"bank_read{s}") for s in range(2)]
        stored = [sem(f"stored{s}") for s in range(2)]
        staged = [sem(f"staged{s}") for s in range(2)]
        apart = sem("apart")
        phase = sem("phase")
        sq_ready, sq_used, ss_ready = sem("sq_ready"), sem("sq_used"), sem("ss_ready")
        ln_ready, rstd_ready = sem("ln_ready"), sem("rstd_ready")
        h_ready, hh_ready = sem("h_ready"), sem("hh_ready")
        hl_ready = [sem(f"hl_ready{q}") for q in ("_even", "_odd")]
        x_in = [sem(f"x_in{r}") for r in range(4)]
        gw_load, gu_load = sem("gw_load"), sem("gu_load")
        small = sem("small")
        bd_mm, wbd_zero, bdT_ready = sem("bd_mm"), sem("wbd_zero"), sem("bdT_ready")
        w_sq, w_added = sem("w_sq"), sem("w_added")
        dn_loaded, dn_conv, dn_silu, dn_sq = sem("dn_loaded"), sem("dn_conv"), sem("dn_silu"), sem("dn_sq")
        dn_chain = sem("dn_chain")
        dn_prod = [sem(f"dn_prod{g}") for g in range(2)]
        dn_taken = [sem(f"dn_taken{g}") for g in range(2)]
        dn_dve, dn_out = sem("dn_dve"), sem("dn_out")
        dn_eg, dn_min, dn_tt, dn_b = ([sem(f"{n}{g}") for g in range(2)] for n in ("dn_eg", "dn_min", "dn_tt", "dn_b"))
        dn_scan_mm, dn_scan_ev = sem("dn_scan_mm"), sem("dn_scan_ev")
        dn_o, dn_root, dn_yst = sem("dn_o"), sem("dn_root"), sem("dn_yst")
        dn_z, dn_q = sem("dn_z"), sem("dn_q")
        vT_loaded, at_loaded, at_vt, at_v = sem("vT_loaded"), sem("at_loaded"), sem("at_vt"), sem("at_v")
        z_ready, z_read, na_ready, e_ready, l_ready = (sem(n) for n in ("z_ready", "z_read", "na_ready", "e_ready", "l_ready"))
        sp_raw, sp_ready, sp_hi_ready, sp_lo_ready, r_sum, r_hi, r_ready, tri_ready, cum_ready, arg_ready, a_ready = (
            sem(n) for n in ("sp_raw", "sp_ready", "sp_hi_ready", "sp_lo_ready", "r_sum", "r_hi", "r_ready", "tri_ready", "cum_ready", "arg_ready", "a_ready"))
        a_masked, av_done, av_read = (sem(n) for n in ("a_masked", "av_done", "av_read"))
        y_stored = [sem(f"y_stored{T}") for T in range(2)]
        pad_zero = sem("pad_zero")
        g_load, g_chain, g_pe, g_act = sem("g_load"), sem("g_chain"), sem("g_pe"), sem("g_act")
        g_masked = sem("g_masked")
        g_out, g_store = sem("g_out"), [sem(f"g_store{s}") for s in range(2)]
        y_ld = [sem(f"y_ld{r}") for r in range(6)]
        yh_ready, yl_ready = sem("yh_ready"), sem("yl_ready")
        gate_ld = [sem(f"gate_ld{s}") for s in range(2)]
        gate_sig = [sem(f"gate_sig{s}") for s in range(2)]
        m_added, mh_ready, ml_ready = sem("m_added"), sem("mh_ready"), sem("ml_ready")
        x_ld, x1_st = [sem(f"x_ld{r}") for r in range(4)], sem("x1_st")
        x1_ready = [sem(f"x1_ready{q}") for q in ("_even", "_odd")]
        n_chain = sem("n_chain")
        f_sqr, f_hr, f_lr = sem("f_sqr"), sem("f_hr"), sem("f_lr")
        out_st = sem("out_st")
        out_ready = [sem(f"out_ready{q}") for q in ("_even", "_odd")]

        def tile_of(t, k):
            return t[:, ds(k, 1), :].rearrange("p k s -> p (k s)")

        def settle(eng):
            eng.sem_inc(apart, 1)

        def end_phase(eng, k):
            eng.drain().then_inc(phase, 1)
            eng.wait_ge(phase, 5 * k)

        def leave_phase(pe):
            pe.drain().then_inc(phase, 1)

        def load_weights(sp, n, s, first=False):
            if not first:
                sp.wait_ge(lo_ready[s], n)
            sp.dma_start(w_raw[s][:], w_stream[n, s]).then_inc(raw_loaded[s], 16)

        def split_hi(act, n, s, first=False):
            act.wait_ge(raw_loaded[s], 16 * n + 16)
            if not first:
                act.wait_ge(blk_done[s], n)
            nc.scalar.activation(w_hi[s][:], w_raw[s][:].rearrange("p (k c) -> p k c", k=KT), ACT.Copy).then_inc(hi_ready[s], 1)

        def split_lo(dve, n, s):
            dve.wait_ge(hi_ready[s], n + 1)
            nc.vector.tensor_tensor(w_lo[s][:], w_raw[s][:].rearrange("p (k c) -> p k c", k=KT),
                                    w_hi[s][:].bitcast(f32), ALU.subtract).then_inc(lo_ready[s], 1)

        def product_step(pe, n, s, hf, k, a_hi, a_lo):
            if hf == 0 and k == 0:
                pe.wait_ge(lo_ready[s], n + 1)
            t = slice(HALF * hf, HALF * hf + HALF)
            nc.tensor.matmul(g_bank[hf][:], w_hi[s][:, k, :], a_hi[:, k, t], start=(k == 0), stop=False)
            nc.tensor.matmul(g_bank[hf][:], w_hi[s][:, k, :], a_lo[:, k, t], start=False, stop=False)
            last = nc.tensor.matmul(g_bank[hf][:], w_lo[s][:, k, :], a_hi[:, k, t], start=False, stop=(k == KT - 1))
            if k == KT - 1:
                last.then_inc(half_ready if hf == 0 else blk_done[s], 1)

        def product_half(pe, n, s, hf, a_hi, a_lo, fills, ready=None):
            pe.wait_ge(bank_read[hf], 1 + fills)
            for k in range(KT):
                if ready is not None and hf == 0:
                    pe.wait_ge(*ready(k))
                product_step(pe, n, s, hf, k, a_hi, a_lo)

        def wait_half(eng, n, s, hf, halves):
            if hf == 0:
                eng.wait_ge(half_ready, halves + 1)
            else:
                eng.wait_ge(blk_done[s], n + 1)

        def take_projection(act, n, s, hf, func):
            wait_half(act, n, s, hf, 2 * n + s)
            if hf == 0:
                act.wait_ge(stored[s], 1 + 16 * n)
            settle(act)
            nc.scalar.activation(stage[s][:, HALF * hf:HALF * hf + HALF], g_bank[hf][:], func,
                                 bias=cols[:, ds(V_BIN + 2 * n + s, 1)]).then_inc(bank_read[hf], 1)

        def store_projection(sp, n, s):
            sp.wait_ge(bank_read[0], 1 + 2 * n + s + 1)
            sp.wait_ge(bank_read[1], 1 + 2 * n + s + 1)
            sp.dma_start(pT[2 * n + s], stage[s][:]).then_inc(stored[s], 16)

        def exp_ln_tables():
            nc.scalar.preload_act_table_set("natural_log_exp_and_others")

        def sp_block(sp, n, s):
            load_weights(sp, n + 1, s)
            store_projection(sp, n, s)

        def act_block(act, n, s, func):
            take_projection(act, n, s, 0, func)
            take_projection(act, n, s, 1, func)
            split_hi(act, n + 1, s)

        def pe_block(pe, n, s, a_hi, a_lo, extra):
            for hf in range(2):
                product_half(pe, n, s, hf, a_hi, a_lo, 2 * n + s + extra)

        def y_upper(p):
            return y1_hi[:, p, :] if p < 4 else y_hi[:, p - 4, :]

        def y_lower(p):
            return y1_lo[:, p, :] if p < 4 else y_lo[:, p - 4, :]

        def split_y_hi(act, p):
            act.wait_ge(y_ld[p // 2], 16)
            nc.scalar.activation(y_upper(p), y_lower(p).bitcast(f32), ACT.Copy).then_inc(yh_ready, 1)

        def split_y_lo(dve, p):
            dve.wait_ge(yh_ready, p + 1)
            nc.vector.tensor_tensor(y_lower(p), y_lower(p).bitcast(f32), y_upper(p).bitcast(f32), ALU.subtract).then_inc(yl_ready, 1)

        def load_y(sp, r):
            dst = y1_lo[:, 2 * r:2 * r + 2, :] if r < 2 else y_lo[:, 2 * r - 4:2 * r - 2, :]
            row = 4 * BRANCHES[r // 2] + 2 * (r % 2)
            sp.dma_start(dst.bitcast(f32), yT[row:row + 2].rearrange("k p s -> p k s")).then_inc(y_ld[r], 16)

        def load_gate(sp, i, q, r):
            j, branch = q // 3, BRANCHES[q % 3]
            dd, hf = divmod(r, 2)
            row = ROW_GATE2 + 4 * i + 2 * j + dd if branch == 2 else ROW_GATE01 + 12 * i + 6 * j + 2 * branch + dd
            sp.dma_start(gate[hf][:], pT[row, :, HALF * hf:HALF * hf + HALF]).then_inc(gate_ld[hf], 16)

        def gate_sigmoid(act, uses, hf):
            act.wait_ge(gate_ld[hf], 16 * uses + 16)
            nc.scalar.activation(gate[hf][:], gate[hf][:], ACT.Sigmoid).then_inc(gate_sig[hf], 1)

        MIX_BRANCH = 12
        HALF_BRANCH = 24

        class Beside:

            def __init__(self, n0, weights, funcs):
                self.n0, self.funcs, self.slot, self.at, self.sum = n0, funcs, 0, 0, 0.0
                self.weights, self.total = weights, 32 * len(funcs)

            def steps(self):
                self.sum += self.weights[self.slot]
                self.slot += 1
                end = self.total if self.slot == len(self.weights) else int(self.total * self.sum / sum(self.weights))
                out = range(self.at, end)
                self.at = end
                return out

        def pe_beside(pe, b):
            for step in b.steps():
                blk, r = divmod(step, 16)
                hf, k = divmod(r, 8)
                n, s = b.n0 + blk // 2, blk % 2
                if k == 0:
                    pe.wait_ge(bank_read[hf], 1 + 2 * n + s)
                product_step(pe, n, s, hf, k, act_hi, act_lo)

        def act_beside(act, b):
            for step in b.steps():
                blk, r = divmod(step, 16)
                n, s = b.n0 + blk // 2, blk % 2
                if r == 7:
                    take_projection(act, n, s, 0, b.funcs[blk // 2])
                if r == 15:
                    take_projection(act, n, s, 1, b.funcs[blk // 2])
                    if b.funcs[blk // 2] == ACT.Gelu and s == 1:
                        exp_ln_tables()
                    split_hi(act, n + 1, s)

        def dve_beside(dve, b):
            for step in b.steps():
                blk, r = divmod(step, 16)
                if r == 15:
                    split_lo(dve, b.n0 + blk // 2 + 1, blk % 2)

        def norm_squares(act, i, src, buf, ready, after=lambda k: None):
            for k in range(KT):
                act.wait_ge(*ready(k))
                if k >= 3:
                    act.wait_ge(sq_used, 4 * i + k - 2)
                elif i:
                    act.wait_ge(ss_ready, i)
                nc.scalar.activation(buf[k % 3][:], src(k), ACT.Square).then_inc(sq_ready, 1)
                after(k)

        def norm_products(pe, i, buf):
            for hf in range(2):
                if i:
                    pe.wait_ge(ln_ready, 2 * i)
            for k in range(KT):
                pe.wait_ge(sq_ready, 4 * i + k + 1)
                for hf in range(2):
                    last = nc.tensor.matmul(d_bank[hf][:], ones[:], buf[k % 3][:, HALF * hf:HALF * hf + HALF], start=(k == 0), stop=(k == KT - 1))
                last.then_inc(sq_used if k < KT - 1 else ss_ready, 1)

        def loop_sums(pe, i, added):
            pe.wait_ge(w_added, added)
            pe.wait_ge(ln_ready, 2 * i)
            for hf in range(2):
                last = nc.tensor.matmul(d_bank[hf][:], ones[:], sum_sq[:, HALF * hf:HALF * hf + HALF], start=True, stop=True)
            last.then_inc(ss_ready, 1)

        def lower_part(ve, i, k, buf):
            ve.wait_ge(hh_ready, KT * min(i, 1) + k + 1)
            ve.tensor_tensor(act_lo[:, k, :], buf[k % 4][:], act_hi[:, k, :].bitcast(f32), ALU.subtract).then_inc(hl_ready[k % 2], 1)

        def normalised(dve, i, src, gain, rstd, buf):
            for k in range(KT + 1):
                if k < KT:
                    if k >= 4:
                        dve.wait_ge(hl_ready[k % 2], 4 * min(i, 1) + k // 2 - 1)
                    nc.vector.scalar_tensor_tensor(buf[k % 4][:], src[:, k, :], cols[:, gain + k:gain + k + 1], rstd[:],
                                                   ALU.mult, ALU.mult).then_inc(h_ready, 1)
                if k % 2:
                    lower_part(nc.vector, i, k - 1, buf)

        def norm_root(act, i, out, scale=1.0 / D):
            act.wait_ge(ss_ready, i + 1)
            for hf in range(2):
                nc.scalar.activation(out[:, HALF * hf:HALF * hf + HALF], d_bank[hf][:], ACT.Ln, scale=scale, bias=eps).then_inc(ln_ready, 1)
            act.wait_ge(ln_ready, 2 * i + 2)
            nc.scalar.activation(out[:], out[:], ACT.Exp, scale=-0.5).then_inc(rstd_ready, 1)

        STEPS = [(T, u, j) for T in range(2) for u in range(2) for j in range(4 * T + 3, -1, -1)]
        NST = len(STEPS)

        def first_col(T, j):
            return max(0, P * j - HALF * T)

        def group_of(x):
            T, u, j = STEPS[x]
            return 2 * T + u, j == 4 * T + 3, j == 0

        def is_diag(T, j):
            return j >= 4 * T

        DIAGS = [sum(is_diag(STEPS[y][0], STEPS[y][2]) for y in range(x + 1)) for x in range(NST)]
        N_DIAG = DIAGS[-1]
        R_BEFORE = [sum(not group_of(y)[2] for y in range(x)) for x in range(NST)]
        N_R = NST - 4
        LAG = 3

        DN_STAGES = ["rowg", "rowb", "gram", "qk", "kT", "vT", "t0"]
        for lev in range(1, N_LEV):
            DN_STAGES += [f"x{lev}", f"y{lev}"] + ([f"t{lev}"] if lev < N_LEV - 1 else [])
        DN_STAGES += ["w"]
        NDS = len(DN_STAGES)
        DN_USES = NDS + 3
        DVE_CHAIN = 8
        DN_FUNCS = (ACT.Identity, ACT.Identity, ACT.Gelu)
        DN_SLOTS = [9.0] * 4 + [7.0] * 2 + [2.0] * 12 + [0.25] * (2 * NDS - 12) + [1.4] * (2 * NCH) + [4.0] * 2
        SG_SLOTS = [16, 8] + [3] * 8 + [8] + [9] * 8
        AT_SLOTS = [0.5] + [1] * NST + [1.5] * LAG

        def add_residual(ve, k):
            ve.wait_ge(n_chain, k + 1)
            ve.wait_ge(x_ld[k // 2], 16)
            ve.tensor_tensor(mixed[:, k, :], mixed[:, k, :], x_fin[:, k, :], ALU.add).then_inc(x1_ready[k % 2], 1)

        def add_output(ve, k):
            ve.wait_ge(n_chain, KT + k + 1)
            ve.wait_ge(x_ld[k // 2], 32)
            ve.tensor_tensor(x_fin[:, k, :], x_fin[:, k, :], mixed[:, k, :], ALU.add).then_inc(out_ready[k % 2], 1)

        block = top.enter_context(nc.Block())

        @block.sync
        def _(sp):
            for r in range(4):
                sp.dma_start(x_sb[:, 2 * r:2 * r + 2, :], xT[2 * r:2 * r + 2].rearrange("k p s -> p k s")).then_inc(x_in[r], 16)
                if r in (1, 2):
                    load_weights(sp, 0, r - 1, first=True)
            sp.dma_start(cols[:], cols_in).then_inc(cols_loaded, 16)
            sp.dma_start(wbd[:], w_bd).then_inc(loaded, 16)
            sp.dma_start(consts[:], consts_in).then_inc(loaded, 16)
            for one in (*bank_read, *stored, dn_yst, w_added, *dn_taken, *y_stored, z_ready, dn_chain, ml_ready, av_read, f_lr):
                sp.sem_inc(one, 1)
            with sp.Fori(0, N_SB) as i:
                for s in range(2):
                    sp_block(sp, i, s)
            for s in range(2):
                sp.wait_ge(stored[s], 1 + 16 * N_SB)
            end_phase(sp, 1)
            with sp.Fori(0, 4) as i:
                sp.wait_ge(z_ready, 1 + NST * i)
                sp.dma_start(a_vT[:], pT[i + ROW_SV]).then_inc(vT_loaded, 16)
                sp.dma_start(a_q[:], pT[i + ROW_SQ]).then_inc(at_loaded, 16)
                sp.wait_ge(pad_zero, 1)
                for u in range(2):
                    sp.dma_start(a_k[64 * u:64 * u + 64, u, :], pT[i + ROW_SK, 64 * u:64 * u + 64]).then_inc(at_loaded, 16)
                for b in range(4):
                    sp_block(sp, PAIR_AT + 2 * i + b // 2, b % 2)
            for T in range(2):
                sp.wait_ge(y_stored[T], 1 + 16 * 4)
            for s in range(2):
                sp.wait_ge(stored[s], 1 + 16 * PAIR_DN)
            end_phase(sp, 2)
            sp.dma_start(d_z[:], pT[ROW_DZ]).then_inc(dn_z, 16)
            for j, row in enumerate((ROW_DQ, ROW_DK, ROW_DV)):
                sp.dma_start(d_in[j][:, 3:], pT[row]).then_inc(dn_loaded, 16)

            def sp_head(i, last=False):
                sp_block(sp, PAIR_DN + 3 * i, 0)
                if not last:
                    sp.wait_ge(dn_conv, 12 * i + 12)
                    for j, row in enumerate((ROW_DQ, ROW_DK, ROW_DV)):
                        sp.dma_start(d_in[j][:, 3:], pT[i + 1 + row]).then_inc(dn_loaded, 16)
                for b in range(1, 6):
                    sp_block(sp, PAIR_DN + 3 * i + b // 2, b % 2)
                sp.wait_ge(dn_out, 2 * i + 2)
                sp.dma_start(yT[4 + i], d_o[:]).then_inc(dn_yst, 16)
                if not last:
                    sp.dma_start(d_z[:], pT[i + 1 + ROW_DZ]).then_inc(dn_z, 16)

            with sp.Fori(0, 3) as i:
                sp_head(i)
            sp_head(3, last=True)
            sp.wait_ge(dn_yst, 1 + 64)
            for s in range(2):
                sp.wait_ge(stored[s], 1 + 16 * PAIR_SG)
            end_phase(sp, 3)
            for r in range(2):
                sp.dma_start(g_v[:, 2 * r:2 * r + 2, :], pT[ROW_V[r]:ROW_V[r] + 2].rearrange("k p s -> p k s")).then_inc(g_load, 16)
            sp.dma_start(g_w[:], w_spT).then_inc(gw_load, 16)
            for r in range(2):
                sp.dma_start(g_u[:, 2 * r:2 * r + 2, :], pT[ROW_U[r]:ROW_U[r] + 2].rearrange("k p s -> p k s")).then_inc(gu_load, 16)
            for r in range(2):
                load_y(sp, r)
            for r in range(2):
                load_gate(sp, 0, 0, r)
            for b in range(8):
                sp_block(sp, PAIR_SG + b // 2, b % 2)
                if b >= 4:
                    sp.wait_ge(g_out, b - 3)
                    sp.dma_start(yT[b - 4], g_y[b % 2][:]).then_inc(g_store[b % 2], 16)
            for s in range(2):
                sp.wait_ge(g_store[s], 32)
            for s in range(2):
                sp.wait_ge(stored[s], 1 + 16 * PAIR_BR)
            end_phase(sp, 4)
            for i in range(2):
                for q in range(6):
                    n, s = PAIR_BR + 3 * i + q // 2, q % 2
                    load_weights(sp, n + 1, s)
                    for r in range(4):
                        if i == 0 and (q, r) in ((0, 0), (1, 0)):
                            for y in range(2):
                                load_y(sp, 2 + 2 * q + y)
                        if (i, q) != (0, 0) or r >= 2:
                            sp.wait_ge(bank_read[r % 2], 1 + 2 * PAIR_BR + 12 * i + 2 * q + r // 2)
                            load_gate(sp, i, q, r)
            end_phase(sp, 5)
            for r in range(4):
                sp.dma_start(x_fin[:, 2 * r:2 * r + 2, :], xT[2 * r:2 * r + 2].rearrange("k p s -> p k s")).then_inc(x_ld[r], 16)
            with sp.Fori(0, 4) as i:
                for s in range(2):
                    load_weights(sp, PAIR_OUT + i + 1, s)
            for k in range(KT):
                sp.wait_ge(x1_ready[k % 2], k // 2 + 1)
                sp.dma_start(x1T[k], mixed[:, k, :]).then_inc(x1_st, 16)
            sp.wait_ge(x1_st, 16 * KT)
            end_phase(sp, 6)
            with sp.Fori(PAIR_FF, N_PAIRS - 1) as n:
                for s in range(2):
                    load_weights(sp, n + 1, s)
            end_phase(sp, 7)
            for r in range(4):
                sp.dma_start(x_fin[:, 2 * r:2 * r + 2, :], x1T[2 * r:2 * r + 2].rearrange("k p s -> p k s")).then_inc(x_ld[r], 16)
            for k in range(KT):
                sp.wait_ge(out_ready[k % 2], k // 2 + 1)
                sp.dma_start(outT[k], x_fin[:, k, :]).then_inc(out_st, 16)
            sp.wait_ge(out_st, 16 * KT)

        @block.scalar
        def _(act):
            exp_ln_tables()
            norm_squares(act, 0, lambda k: x_sb[:, k, :], sq0, ready=lambda k: (x_in[k // 2], 16),
                         after=lambda k: split_hi(act, 0, k - 4, first=True) if k in (4, 5) else None)
            act.wait_ge(ones_set, 2)
            norm_root(act, 0, rstd0)
            for k in range(KT):
                act.wait_ge(h_ready, k + 1)
                nc.scalar.activation(act_hi[:, k, :], hbuf[k % 4][:], ACT.Copy).then_inc(hh_ready, 1)
            act.wait_ge(loaded, 32)
            nc.scalar.activation(wbd_parts[:], ident[:, None, :].broadcast_to([P, KT, P]), ACT.Copy, scale=0.0).then_inc(wbd_zero, 1)
            act.wait_ge(wbd_zero, 1)
            nc.scalar.activation(wbd_parts[:, :, 0:8], wbd[:], ACT.Copy).then_inc(small, 1)
            with act.Fori(0, N_SB - 1) as i:
                for s in range(2):
                    act_block(act, i, s, ACT.Identity)
            act.wait_ge(small, 3)
            nc.scalar.activation(bd_beta[:], bd[:, :, 0:4].rearrange("p n h -> p h n"), ACT.Sigmoid).then_inc(small, 1)
            act.wait_ge(small, 6)
            nc.scalar.activation(bt[2][:], bt[1][:], ACT.Exp).then_inc(small, 1)
            act.wait_ge(small, 7)
            nc.scalar.activation(bt[2][:], bt[2][:], ACT.Ln, bias=1.0).then_inc(small, 1)
            for h in range(4):
                last = nc.scalar.activation(bt[3][:, h, :], cols[:, V_ALOG + h:V_ALOG + h + 1].broadcast_to([P, NCH]), ACT.Exp)
            last.then_inc(small, 1)
            act_block(act, N_SB - 1, 0, ACT.Identity)
            act.wait_ge(small, 12)
            nc.scalar.activation(bt[4][:], bd_gc[:], ACT.Exp).then_inc(small, 1)
            act_block(act, N_SB - 1, 1, ACT.Identity)
            end_phase(act, 1)
            for tri, c in ((a_from, lo_incl), (a_ones, ones[:])):
                last = nc.scalar.activation(tri[:], c, ACT.Copy)
            last.then_inc(tri_ready, 1)
            exp_ln_tables()
            with act.Fori(0, 4) as i:
                b = Beside(PAIR_AT + 2 * i, AT_SLOTS, (ACT.Identity,) * 2)
                act_beside(act, b)
                act.wait_ge(pad_zero, 2)
                for hf in range(2):
                    act.wait_ge(at_vt, 2 * i + hf + 1)
                    src = z_bank[hf][:].rearrange("p (n c) -> p n c", c=P)
                    for u in range(2):
                        last = nc.scalar.activation(a_v[:, 4 * hf:4 * hf + 4, u, 64 * u:64 * u + 64], src[:, :, 64 * u:64 * u + 64], ACT.Copy)
                    last.then_inc(at_v, 1)

                def cols_of(x):
                    return slice(first_col(STEPS[x][0], STEPS[x][2]), HALF)

                def copy_z(x):
                    act.wait_ge(z_ready, 1 + NST * i + x + 1)
                    if x >= 4:
                        act.wait_ge(arg_ready, NST * i + x - 3)
                    nc.scalar.activation(a_z[x % 4][:, cols_of(x)], z_bank[x % 2][:, cols_of(x)], ACT.Copy, scale=0.125).then_inc(z_read, 1)

                def exp_arg(x):
                    T, u, j = STEPS[x]
                    act.wait_ge(arg_ready, NST * i + x + 1)
                    a = a_A[u][:, j, cols_of(x)]
                    nc.scalar.activation(a, a, ACT.Exp).then_inc(a_ready, 1)

                def exp_z(x):
                    e = a_e[x % 3][:, cols_of(x)]
                    act.wait_ge(na_ready, NST * i + x + 1)
                    nc.scalar.activation(e, e, ACT.Exp).then_inc(e_ready, 1)

                def ln_z(x):
                    e = a_e[x % 3][:, cols_of(x)]
                    act.wait_ge(e_ready, NST * i + x + 1)
                    nc.scalar.activation(e, e, ACT.Ln, bias=1.0).then_inc(l_ready, 1)

                def upper_sp(x):
                    act.wait_ge(sp_ready, NST * i + x + 1)
                    if x >= 2:
                        act.wait_ge(cum_ready, NST * i + x - 1)
                    nc.scalar.activation(a_sp_hi[x % 2][:, cols_of(x)], a_sp[x % 3][:, cols_of(x)], ACT.Copy).then_inc(sp_hi_ready, 1)

                def upper_R(x):
                    c = first_col(STEPS[x][0], STEPS[x][2])
                    act.wait_ge(r_sum, N_R * i + R_BEFORE[x] + 1)
                    if x >= 2:
                        act.wait_ge(cum_ready, NST * i + x)
                    nc.scalar.activation(a_R_hi[x % 2][:, c:HALF], a_R[x % 2][:, c:HALF], ACT.Copy).then_inc(r_hi, 1)

                def out_av(T):
                    act.wait_ge(av_done, 4 * i + 2 * T + 2)
                    act.wait_ge(y_stored[T], 1 + 16 * i)
                    nc.scalar.activation(a_y[T][:], o_bank[:], ACT.Copy).then_inc(av_read, 1)
                    act.wait_ge(av_read, 1 + 2 * i + T + 1)
                    act.dma_start(yT[8 + i, :, HALF * T:HALF * T + HALF], a_y[T][:]).then_inc(y_stored[T], 16)

                copy_z(0)
                for x in range(NST + LAG):
                    if 1 <= x < NST + 1:
                        upper_sp(x - 1)
                    if x < NST:
                        exp_z(x)
                    if x + 1 < NST:
                        copy_z(x + 1)
                    if x < NST:
                        ln_z(x)
                    if 1 <= x < NST and not group_of(x - 1)[2]:
                        upper_R(x - 1)
                    if 2 <= x < NST + 2:
                        exp_arg(x - 2)
                    act_beside(act, b)
                    if x >= 4 and group_of(x - 4)[2] and STEPS[x - 4][1] == 1:
                        out_av(STEPS[x - 4][0])
                out_av(1)
            end_phase(act, 2)
            with act.Fori(0, 4) as i:
                b = Beside(PAIR_DN + 3 * i, DN_SLOTS, DN_FUNCS)

                def beside():
                    act_beside(act, b)

                beside()
                beside()
                act.wait_ge(dn_z, 16 * i + 16)
                nc.scalar.activation(d_z[:], d_z[:], ACT.Silu).then_inc(dn_silu, 1)
                for j, sq in enumerate((d_eg, d_dt, None)):
                    if j:
                        beside()
                    act.wait_ge(dn_conv, 12 * i + 4 * j + 4)
                    nc.scalar.activation(d_cv[j][:], d_cv[j][:], ACT.Silu).then_inc(dn_silu, 1)
                    if sq is not None:
                        act.wait_ge(dn_silu, 4 * i + j + 2)
                        nc.scalar.activation(sq[:].rearrange("p n c -> p (n c)"), d_cv[j][:], ACT.Square).then_inc(dn_sq, 1)
                exp_ln_tables()
                r = d_wt[:].rearrange("p n c -> p (n c)")

                def inverse_root(use, scale):
                    for g in range(2):
                        act.wait_ge(dn_prod[g], DN_USES * i + use)
                        nc.scalar.activation(r[:, HALF * g:HALF * g + HALF], d_bank[g][:], ACT.Ln, scale=scale, bias=eps).then_inc(dn_taken[g], 1)
                    for g in range(2):
                        act.wait_ge(dn_taken[g], 1 + DN_USES * i + use)
                    nc.scalar.activation(r, r, ACT.Exp, scale=-0.5).then_inc(dn_root, 1)

                for j in range(2):
                    act.wait_ge(dn_chain, 1 + 4 * i + 3 * j)
                    inverse_root(j + 1, 1.0)
                    beside()
                for x, name in enumerate(DN_STAGES):
                    for g in range(2):
                        c = slice(4 * g, 4 * g + 4)
                        p3 = d_bank[g][:].rearrange("p (n c) -> p n c", c=P)
                        if name == "rowg":
                            act.wait_ge(dn_prod[g], DN_USES * i + 3 + x)
                            act.wait_ge(dn_taken[g], 1 + DN_USES * i + 2 + x)
                            nc.scalar.activation(d_eg[:, c, :], p3, ACT.Exp).then_inc(dn_eg[g], 1)
                            act.wait_ge(dn_min[g], i + 1)
                            nc.scalar.activation(d_tail[:, c], d_tail[:, c], ACT.Exp).then_inc(dn_eg[g], 1)
                            nc.scalar.activation(d_dt[:, c, :], d_dt[:, c, :], ACT.Exp).then_inc(dn_eg[g], 1)
                        if name[0] in "xt" or name == "w":
                            act.wait_ge(dn_prod[g], DN_USES * i + 3 + x)
                            dst = d_X if name[0] == "x" else d_T if name[0] == "t" else d_wt
                            nc.scalar.activation(dst[:, c, :], p3, ACT.Copy, scale=-1.0 if name == "w" else 1.0).then_inc(dn_taken[g], 1)
                        beside()
                for n in range(NCH):
                    beside()
                    beside()
                    if n % 4 == 3:
                        act.wait_ge(dn_scan_mm, 16 * i + 2 * n + 2)
                        nc.scalar.activation(d_o[:, HALF * (n // 4):HALF * (n // 4) + HALF], d_bank[1][:], ACT.Copy).then_inc(dn_o, 1)
                act.wait_ge(dn_o, 2 * i + 2)
                nc.scalar.activation(d_X[:].rearrange("p n c -> p (n c)"), d_o[:], ACT.Square).then_inc(dn_sq, 1)
                for g in range(2):
                    beside()
                inverse_root(DN_USES, 1.0 / P)
            end_phase(act, 3)
            b8 = Beside(PAIR_SG, SG_SLOTS, (ACT.Identity,) * 4)
            act_beside(act, b8)
            act_beside(act, b8)
            for b in range(4):
                for hf in range(2):
                    x = 2 * b + hf
                    act.wait_ge(g_chain, 2 + x + 1)
                    if x >= 2:
                        act.wait_ge(g_pe, 2 + x - 1)
                    nc.scalar.activation(g_sq[x % 2][:], g_v[:, b, HALF * hf:HALF * hf + HALF], ACT.Square).then_inc(g_act, 1)
                    act_beside(act, b8)
            act.wait_ge(g_pe, 10)
            for hf in range(2):
                nc.scalar.activation(g_rstd[:, HALF * hf:HALF * hf + HALF], d_bank[hf][:], ACT.Ln, scale=1.0 / BW, bias=eps).then_inc(g_chain, 1)
            act.wait_ge(g_chain, 12)
            nc.scalar.activation(g_rstd[:], g_rstd[:], ACT.Exp, scale=-0.5).then_inc(g_chain, 1)
            act_beside(act, b8)
            for b in range(4):
                for hf in range(2):
                    act.wait_ge(g_pe, 10 + 4 * b + hf + 1)
                    if b:
                        act.wait_ge(g_pe, 10 + 4 * b)
                    nc.scalar.activation(g_vt[:, 4 * hf:4 * hf + 4, :], z_bank[hf][:].rearrange("p (n c) -> p n c", c=P), ACT.Copy).then_inc(g_act, 1)
                act_beside(act, b8)
                split_y_hi(act, b)
                act_beside(act, b8)
            for hf in range(2):
                gate_sigmoid(act, 0, hf)
            end_phase(act, 4)
            for i in range(2):
                for q in range(6):
                    n, s = PAIR_BR + 3 * i + q // 2, q % 2
                    for r in range(4):
                        dd, hf = divmod(r, 2)
                        if (i, q) != (0, 0) or dd:
                            gate_sigmoid(act, 12 * i + 2 * q + dd, hf)
                        if i == 0 and q < 2 and r >= 2:
                            for y in range(2):
                                split_y_hi(act, 4 * q + 2 * r + y)
                    split_hi(act, n + 1, s)
                    if q % 3 == 2:
                        for dd in range(2):
                            d = 4 * i + 2 * (q // 3) + dd
                            act.wait_ge(m_added, 16 * i + 8 * (q // 3) + 6 + 2 * dd)
                            settle(act)
                            nc.scalar.activation(tile_of(act_hi, d), m_acc[:, dd, :], ACT.Copy).then_inc(mh_ready, 1)
            end_phase(act, 5)
            exp_ln_tables()
            with act.Fori(0, 4) as i:
                for s in range(2):
                    n = PAIR_OUT + i
                    for hf in range(2):
                        wait_half(act, n, s, hf, 2 * n + s + HALF_BRANCH)
                        settle(act)
                        nc.scalar.activation(tile_of(mixed, 2 * i + s)[:, HALF * hf:HALF * hf + HALF], g_bank[hf][:], ACT.Copy).then_inc(bank_read[hf], 1)
                    split_hi(act, n + 1, s)
                    act.wait_ge(w_added, 2 * i + s + 1)
                    for hf in range(2):
                        act.wait_ge(bank_read[hf], 1 + 2 * n + s + 1 + MIX_BRANCH)
                    settle(act)
                    nc.scalar.activation(n_sq[s][:], tile_of(mixed, 2 * i + s), ACT.Square).then_inc(w_sq, 1)
            norm_root(act, 1, n_rstd)
            norm_squares(act, 2, lambda k: mixed[:, k, :], n_sq, ready=lambda k: (x1_ready[k % 2], k // 2 + 1))
            norm_root(act, 2, n_rstd)
            for k in range(KT):
                act.wait_ge(h_ready, KT + k + 1)
                nc.scalar.activation(act_hi[:, k, :], n_h[k % 4][:], ACT.Copy).then_inc(hh_ready, 1)
            end_phase(act, 6)
            def ff_hi(blk, hf, count):
                act.wait_ge(f_sqr, count)
                settle(act)
                nc.scalar.activation(tile_of(f_hi, blk)[:, HALF * hf:HALF * hf + HALF], f_t[hf][:], ACT.Copy).then_inc(f_hr, 1)

            def ff_group(g, last=False):
                with act.Fori(0, 4) as i:
                    for s in range(2):
                        n = PAIR_FF + 8 * g + i
                        for hf in range(2):
                            c = 16 * g + 4 * i + 2 * s + hf
                            wait_half(act, n, s, hf, 2 * n + s + HALF_BRANCH)
                            act.wait_ge(f_lr, 1 + 16 * g + 4 * i + 2 * s)
                            nc.scalar.activation(f_t[hf][:], g_bank[hf][:], ACT.Relu).then_inc(bank_read[hf], 1)
                            ff_hi(2 * i + s, hf, c + 1)
                        split_hi(act, n + 1, s)
                def sum_squares(i, s):
                    for hf in range(2):
                        act.wait_ge(bank_read[hf], 1 + 2 * (PAIR_FF + 8 * g + 4 + i) + s + 1 + MIX_BRANCH)
                        act.wait_ge(w_added, 10 + 4 * i + 2 * s + hf)
                        settle(act)
                        nc.scalar.activation(f_sq[hf][:], tile_of(mixed, 2 * i + s)[:, HALF * hf:HALF * hf + HALF], ACT.Square).then_inc(w_sq, 1)

                with act.Fori(0, 3 if last else 4) as i:
                    for s in range(2):
                        split_hi(act, PAIR_FF + 8 * g + 4 + i + 1, s)
                        if last:
                            sum_squares(i, s)
                if last:
                    for s in range(2):
                        sum_squares(3, s)

            with act.Fori(0, 3) as g:
                ff_group(g)
            ff_group(3, last=True)
            end_phase(act, 7)
            norm_root(act, 3, n_rstd)

        @block.tensor
        def _(pe):
            pe.wait_ge(ones_set, 1)
            norm_products(pe, 0, sq0)
            pe.wait_ge(loaded, 32)
            for hf in range(2):
                product_half(pe, 0, 0, hf, act_hi, act_lo, 0, ready=lambda k: (hl_ready[k % 2], k // 2 + 1))
            pe_block(pe, 0, 1, act_hi, act_lo, 0)
            with pe.Fori(1, N_SB - 2) as i:
                for s in range(2):
                    pe_block(pe, i, s, act_hi, act_lo, 0)
            pe.wait_ge(small, 2)
            for hf in range(2):
                t = slice(HALF * hf, HALF * hf + HALF)
                for k in range(KT):
                    nc.tensor.matmul(z_bank[hf][:], wbd_parts[:, k, :], act_hi[:, k, t], start=(k == 0), stop=False)
                    last = nc.tensor.matmul(z_bank[hf][:], wbd_parts[:, k, :], act_lo[:, k, t], start=False, stop=(k == KT - 1))
                last.then_inc(bd_mm, 1)
            for s in range(2):
                pe_block(pe, N_SB - 2, s, act_hi, act_lo, 0)
            pe.wait_ge(bdT_ready, 2)
            for n in range(NCH):
                for part in range(2):
                    last = nc.tensor.matmul(c_bank[:, 8 * n:8 * n + 8], bdT[:, P * n:P * n + P], ident[0:16, 8 * part:8 * part + 8],
                                            start=(part == 0), stop=(part == 1))
            last.then_inc(bd_mm, 1)
            pe_block(pe, N_SB - 1, 0, act_hi, act_lo, 0)
            pe.wait_ge(small, 11)
            nc.tensor.matmul(z_bank[1][:, 0:32], up_incl, bd_g[:].rearrange("p h n -> p (h n)"), start=True, stop=True).then_inc(bd_mm, 1)
            pe_block(pe, N_SB - 1, 1, act_hi, act_lo, 0)
            leave_phase(pe)
            pe.wait_ge(tri_ready, 1)
            with pe.Fori(0, 4) as i:
                b = Beside(PAIR_AT + 2 * i, AT_SLOTS, (ACT.Identity,) * 2)
                pe_beside(pe, b)
                pe.wait_ge(vT_loaded, 16 * i + 16)
                for hf in range(2):
                    for n in range(4):
                        last = nc.tensor.transpose(z_bank[hf][:, P * n:P * n + P], a_vT[:, P * (4 * hf + n):P * (4 * hf + n) + P], ident)
                    last.then_inc(at_vt, 1)

                def scores(x):
                    T, u, j = STEPS[x]
                    c = first_col(T, j)
                    if x < 2:
                        pe.wait_ge(at_v, 2 * i + x + 1)
                    else:
                        pe.wait_ge(z_read, NST * i + x - 1)
                    nc.tensor.matmul(z_bank[x % 2][:, c:HALF], a_k[:, u, P * j:P * j + P], a_q[:, HALF * T + c:HALF * T + HALF],
                                     start=True, stop=True).then_inc(z_ready, 1)

                def sums_above(x):
                    T, u, j = STEPS[x]
                    c, c1 = first_col(T, j), first_col(T, j + 1)
                    first = group_of(x)[1]
                    pe.wait_ge(sp_lo_ready, NST * i + x + 1)
                    if x >= 2:
                        pe.wait_ge(arg_ready, NST * i + x - 1)
                    nc.tensor.matmul(cum_bank[x % 2][:, c:HALF], a_from[:], a_sp_hi[x % 2][:, c:HALF], start=True, stop=False)
                    mm = nc.tensor.matmul(cum_bank[x % 2][:, c:HALF], a_from[:], a_sp_lo[x % 2][:, c:HALF], start=False, stop=first)
                    if not first:
                        pe.wait_ge(r_ready, N_R * i + R_BEFORE[x])
                        nc.tensor.matmul(cum_bank[x % 2][:, c1:HALF], a_ones[:], a_R_hi[(x - 1) % 2][:, c1:HALF], start=False, stop=False)
                        mm = nc.tensor.matmul(cum_bank[x % 2][:, c1:HALF], a_ones[:], a_R_lo[(x - 1) % 2][:, c1:HALF], start=False, stop=True)
                    mm.then_inc(cum_ready, 1)

                def weighted_values(x):
                    T, u, _ = STEPS[x]
                    pe.wait_ge(a_ready, NST * i + x + 1)
                    pe.wait_ge(a_masked, N_DIAG * i + DIAGS[x])
                    if u == 0:
                        pe.wait_ge(av_read, 1 + 2 * i + T)
                    for j in range(4 * T + 4):
                        c = first_col(T, j)
                        last = nc.tensor.matmul(o_bank[:, c:HALF], a_v[:, j, u, :], a_A[u][:, j, c:HALF],
                                                start=(u == 0 and j == 0), stop=(u == 1 and j == 4 * T + 3))
                    last.then_inc(av_done, 1)

                pe.wait_ge(at_loaded, 48 * i + 48)
                scores(0)
                scores(1)
                for x in range(NST + LAG):
                    if x + 2 < NST:
                        scores(x + 2)
                    pe_beside(pe, b)
                    if 1 <= x < NST + 1:
                        sums_above(x - 1)
                    if x >= 3 and group_of(x - 3)[2]:
                        weighted_values(x - 3)
            leave_phase(pe)
            with pe.Fori(0, 4) as i:
                b = Beside(PAIR_DN + 3 * i, DN_SLOTS, DN_FUNCS)

                def beside():
                    pe_beside(pe, b)

                def chunk(t, n):
                    return t[:, P * n:P * n + P]

                for j in range(4):
                    beside()
                for j, sq in enumerate((d_eg, d_dt)):
                    pe.wait_ge(dn_sq, 3 * i + j + 1)
                    for g in range(2):
                        pe.wait_ge(dn_taken[g], 1 + DN_USES * i + j)
                        nc.tensor.matmul(d_bank[g][:], ones[:], sq[:].rearrange("p n c -> p (n c)")[:, HALF * g:HALF * g + HALF],
                                         start=True, stop=True).then_inc(dn_prod[g], 1)
                    beside()
                for x, name in enumerate(DN_STAGES):
                    for g in range(2):
                        pe.wait_ge(dn_taken[g], 1 + DN_USES * i + 2 + x)
                        if name == "rowg":
                            pe.wait_ge(dn_chain, 1 + 4 * i + 2)
                        if name == "gram":
                            pe.wait_ge(dn_chain, 1 + 4 * i + 4)
                            pe.wait_ge(dn_silu, 4 * i + 4)
                        if name == "t0":
                            pe.wait_ge(dn_tt[g], i + 1)
                        if name[0] == "x":
                            pe.wait_ge(dn_b[g], (N_LEV - 1) * i + int(name[1:]))
                        for m in range(4):
                            n = 4 * g + m
                            o = d_bank[g][:, P * m:P * m + P]
                            if name == "rowg":
                                last = nc.tensor.matmul(o, d_gB[:, n, :], up_incl, start=True, stop=True)
                            elif name == "rowb":
                                last = nc.tensor.matmul(o, d_bB[:, n, :], ident, start=True, stop=True)
                            elif name == "gram":
                                last = nc.tensor.matmul(o, chunk(d_cv[1], n), chunk(d_cv[1], n), start=True, stop=True)
                            elif name == "qk":
                                last = nc.tensor.matmul(o, chunk(d_cv[1], n), chunk(d_cv[0], n), start=True, stop=True)
                            elif name == "kT":
                                last = nc.tensor.transpose(o, chunk(d_cv[1], n), ident)
                            elif name == "vT":
                                last = nc.tensor.transpose(o, chunk(d_cv[2], n), ident)
                            elif name[0] == "t":
                                last = nc.tensor.transpose(o, d_TT[:, n, :], ident)
                            elif name[0] == "x":
                                last = nc.tensor.matmul(o, d_B[:, n, :], d_T[:, n, :], start=True, stop=True)
                            elif name[0] == "y":
                                last = nc.tensor.matmul(o, d_X[:, n, :], d_TT[:, n, :], start=True, stop=True)
                            else:
                                last = nc.tensor.matmul(o, d_kb[:, n, :], d_TT[:, n, :], start=True, stop=True)
                        last.then_inc(dn_prod[g], 1)
                        beside()
                for g in range(2):
                    pe.wait_ge(dn_taken[g], 1 + DN_USES * i + 2 + NDS)
                pe.wait_ge(dn_q, 2 * i + 2)
                for n in range(NCH):
                    if n == 4:
                        pe.wait_ge(dn_o, 2 * i + 1)
                    o = d_bank[1][:, P * (n % 4):P * (n % 4) + P]
                    pe.wait_ge(dn_scan_ev, 17 * i + 1 + 2 * n)
                    nc.tensor.matmul(o, d_S[:], d_cv[0][:, P * n:P * n + P], start=True, stop=False)
                    nc.tensor.matmul(d_bank[0][:, 0:P], d_TT[:, n, :], d_vb[:, n, :], start=True, stop=False)
                    nc.tensor.matmul(d_bank[0][:, 0:P], d_wt[:, n, :], d_S[:], start=False, stop=True).then_inc(dn_scan_mm, 1)
                    beside()
                    pe.wait_ge(dn_scan_ev, 17 * i + 2 + 2 * n)
                    nc.tensor.matmul(o, d_vn[:], d_qk[:, n, :], start=False, stop=True)
                    nc.tensor.matmul(d_bank[0][:, P:2 * P], d_kt[:, n, :], d_vn[:], start=True, stop=True).then_inc(dn_scan_mm, 1)
                    beside()
                pe.wait_ge(dn_sq, 3 * i + 3)
                pe.wait_ge(dn_scan_ev, 17 * i + 17)
                for g in range(2):
                    nc.tensor.matmul(d_bank[g][:], ones[:], d_X[:].rearrange("p n c -> p (n c)")[:, HALF * g:HALF * g + HALF],
                                     start=True, stop=True).then_inc(dn_prod[g], 1)
                    beside()
            leave_phase(pe)
            b8 = Beside(PAIR_SG, SG_SLOTS, (ACT.Identity,) * 4)
            pe_beside(pe, b8)
            pe.wait_ge(g_load, 32)
            for hf in range(2):
                for b in range(4):
                    last = nc.tensor.matmul(d_bank[hf][:], ones[:], g_v[:, b, HALF * hf:HALF * hf + HALF], start=(b == 0), stop=(b == 3))
                last.then_inc(g_pe, 1)
            pe_beside(pe, b8)
            pe.wait_ge(g_chain, 2)
            for b in range(4):
                for hf in range(2):
                    pe.wait_ge(g_act, 2 * b + hf + 1)
                    nc.tensor.matmul(d_bank[hf][:], ones[:], g_sq[hf][:], start=(b == 0), stop=(b == 3)).then_inc(g_pe, 1)
                    pe_beside(pe, b8)
            pe_beside(pe, b8)
            pe.wait_ge(g_masked, 1)
            for b in range(4):
                pe.wait_ge(g_chain, 13 + 4 * b + 2)
                for hf in range(2):
                    if b:
                        pe.wait_ge(g_act, 8 + 2 * b)
                    for m in range(4):
                        n = 4 * hf + m
                        last = nc.tensor.transpose(z_bank[hf][:, P * m:P * m + P], g_n[:, P * n:P * n + P], ident)
                    last.then_inc(g_pe, 1)
                pe_beside(pe, b8)
                pe.wait_ge(g_act, 8 + 2 * b + 2)
                for hf in range(2):
                    if b:
                        pe.wait_ge(g_out, b)
                    for m in range(4):
                        for e in range(2):
                            last = nc.tensor.matmul(d_bank[hf][64 * e:64 * e + 64, P * m:P * m + P],
                                                    g_vt[:, 4 * hf + m, 64 * e:64 * e + 64], g_w[:, 2 * b + e, :], start=True, stop=True)
                    last.then_inc(g_pe, 1)
                pe_beside(pe, b8)
            leave_phase(pe)
            for i in range(2):
                for q in range(6):
                    n, s = PAIR_BR + 3 * i + q // 2, q % 2
                    pe.wait_ge(lo_ready[s], n + 1)
                    for r in range(4):
                        dd, hf = divmod(r, 2)
                        t = slice(HALF * hf, HALF * hf + HALF)
                        pe.wait_ge(bank_read[hf], 1 + 2 * PAIR_BR + 12 * i + 2 * q + dd)
                        for k in range(4):
                            kk, y = 4 * dd + k, 4 * (q % 3) + k
                            if r == 0:
                                pe.wait_ge(yl_ready, y + 1)
                            nc.tensor.matmul(g_bank[hf][:], w_hi[s][:, kk, :], y_upper(y)[:, t], start=(k == 0), stop=False)
                            nc.tensor.matmul(g_bank[hf][:], w_hi[s][:, kk, :], y_lower(y)[:, t], start=False, stop=False)
                            last = nc.tensor.matmul(g_bank[hf][:], w_lo[s][:, kk, :], y_upper(y)[:, t], start=False, stop=(k == 3))
                        last.then_inc(half_ready if r < 3 else blk_done[s], 1)
            leave_phase(pe)
            with pe.Fori(0, 4) as i:
                for s in range(2):
                    n = PAIR_OUT + i
                    for hf in range(2):
                        product_half(pe, n, s, hf, act_hi, act_lo, 2 * n + s + MIX_BRANCH,
                                     ready=(lambda k: (ml_ready, 1 + k + 1)) if s == 0 else None)
            loop_sums(pe, 1, 10)
            norm_products(pe, 2, n_sq)
            leave_phase(pe)

            def ff_group(g):
                with pe.Fori(0, 4) as i:
                    for s in range(2):
                        n = PAIR_FF + 8 * g + i
                        for hf in range(2):
                            product_half(pe, n, s, hf, act_hi, act_lo, 2 * n + s + MIX_BRANCH,
                                         ready=(lambda k: (hl_ready[k % 2], 4 + k // 2 + 1)) if s == 0 else None)
                with pe.Fori(0, 4) as i:
                    for s in range(2):
                        n = PAIR_FF + 8 * g + 4 + i
                        for hf in range(2):
                            product_half(pe, n, s, hf, f_hi, f_lo, 2 * n + s + MIX_BRANCH,
                                         ready=(lambda k: (f_lr, 1 + 16 * g + 2 * k + 2)) if s == 0 else None)

            with pe.Fori(0, 4) as g:
                ff_group(g)
            leave_phase(pe)
            loop_sums(pe, 3, 11 + 16)

        @block.vector
        def _(dve):
            for s in range(2):
                split_lo(dve, 0, s)
            dve.wait_ge(cols_loaded, 16)
            dve.wait_ge(rstd_ready, 1)
            normalised(dve, 0, x_sb, V_NORM, rstd0, hbuf)
            dve.wait_ge(loaded, 32)
            dve.wait_ge(small, 1)
            nc.vector.tensor_tensor(wbd_parts[:, :, 8:16], wbd[:], wbd_parts[:, :, 0:8].bitcast(f32), ALU.subtract).then_inc(small, 1)
            with dve.Fori(0, N_SB - 2) as i:
                for s in range(2):
                    split_lo(dve, i + 1, s)
            for hf in range(2):
                dve.wait_ge(bd_mm, hf + 1)
                nc.vector.tensor_copy(bdT[:, HALF * hf:HALF * hf + HALF], z_bank[hf][0:16, :]).then_inc(bdT_ready, 1)
            for s in range(2):
                split_lo(dve, N_SB - 1, s)
            dve.wait_ge(bd_mm, 3)
            nc.vector.tensor_tensor(bd[:], c_bank[:, 0:64].rearrange("p (n c) -> p n c", c=8),
                                    cols[:, None, V_BBD:V_BBD + 8].broadcast_to([P, NCH, 8]), ALU.add).then_inc(small, 1)
            dve.wait_ge(small, 4)
            nc.vector.tensor_tensor(bt[0][:], bd[:, :, 4:8].rearrange("p n h -> p h n"),
                                    cols[:, V_DTB:V_DTB + 4, None].broadcast_to([P, 4, NCH]), ALU.add).then_inc(small, 1)
            dve.wait_ge(small, 5)
            nc.vector.scalar_tensor_tensor(bt[1][:], bt[0][:], -1.0, bt[0][:], ALU.mult, ALU.min).then_inc(small, 1)
            dve.wait_ge(small, 9)
            nc.vector.scalar_tensor_tensor(bt[0][:], bt[0][:], 0.0, bt[2][:], ALU.max, ALU.add).then_inc(small, 1)
            dve.wait_ge(small, 10)
            nc.vector.scalar_tensor_tensor(bd_g[:], bt[0][:], -1.0, bt[3][:], ALU.mult, ALU.mult).then_inc(small, 1)
            split_lo(dve, N_SB, 0)
            dve.wait_ge(bd_mm, 4)
            nc.vector.tensor_copy(bd_gc[:].rearrange("p h n -> p (h n)"), z_bank[1][:, 0:32]).then_inc(small, 1)
            dve.wait_ge(small, 13)
            nc.vector.tensor_tensor(bd_egc[:], bt[4][:], bd_beta[:], ALU.mult).then_inc(small, 1)
            split_lo(dve, N_SB, 1)
            end_phase(dve, 1)
            with dve.Fori(0, 4) as i:
                b = Beside(PAIR_AT + 2 * i, AT_SLOTS, (ACT.Identity,) * 2)

                def cols_of(x):
                    return slice(first_col(STEPS[x][0], STEPS[x][2]), HALF)

                def minus_abs(x):
                    t, z = cols_of(x), a_z[x % 4]
                    dve.wait_ge(z_read, NST * i + x + 1)
                    nc.vector.scalar_tensor_tensor(a_e[x % 3][:, t], z[:, t], -1.0, z[:, t], ALU.mult, ALU.min).then_inc(na_ready, 1)

                def softplus(x):
                    T, u, j = STEPS[x]
                    c, t, sp = first_col(T, j), cols_of(x), a_sp[x % 3]
                    dve.wait_ge(l_ready, NST * i + x + 1)
                    if x >= 3:
                        dve.wait_ge(sp_lo_ready, NST * i + x - 2)
                        dve.wait_ge(r_ready, N_R * i + R_BEFORE[x - 2])
                    diag = is_diag(T, j)
                    nc.vector.scalar_tensor_tensor(sp[:, t], a_z[x % 4][:, t], 0.0, a_e[x % 3][:, t],
                                                   ALU.max, ALU.add).then_inc(sp_raw if diag else sp_ready, 1)
                    if diag:
                        dve.wait_ge(sp_raw, N_DIAG * i + DIAGS[x])
                        nc.vector.tensor_tensor(sp[:, c:c + P], sp[:, c:c + P], up_strict, ALU.mult).then_inc(sp_ready, 1)

                def lower_sp(x):
                    t = cols_of(x)
                    dve.wait_ge(sp_hi_ready, NST * i + x + 1)
                    if x >= 2:
                        dve.wait_ge(cum_ready, NST * i + x - 1)
                    nc.vector.tensor_tensor(a_sp_lo[x % 2][:, t], a_sp[x % 3][:, t], a_sp_hi[x % 2][:, t].bitcast(f32),
                                            ALU.subtract).then_inc(sp_lo_ready, 1)

                def argument(x):
                    T, u, j = STEPS[x]
                    t = cols_of(x)
                    dve.wait_ge(cum_ready, NST * i + x + 1)
                    if group_of(x)[1] and T == 1:
                        dve.wait_ge(av_done, 4 * i + u + 1)
                    nc.vector.tensor_tensor(a_A[u][:, j, t], a_z[x % 4][:, t], cum_bank[x % 2][:, t], ALU.subtract).then_inc(arg_ready, 1)

                dve_beside(dve, b)
                minus_abs(0)
                for x in range(NST + LAG):
                    if 1 <= x < NST + 1:
                        lower_sp(x - 1)
                    if 2 <= x < NST + 2:
                        argument(x - 2)
                    if x + 1 < NST:
                        minus_abs(x + 1)
                    if x < NST:
                        softplus(x)
                    dve_beside(dve, b)
            end_phase(dve, 2)
            for j in range(3):
                nc.vector.memset(d_in[j][:, 0:3], 0.0).then_inc(dn_dve, 1)
            dve.wait_ge(dn_dve, 3)
            with dve.Fori(0, 4) as i:
                b = Beside(PAIR_DN + 3 * i, DN_SLOTS, DN_FUNCS)

                def beside():
                    dve_beside(dve, b)

                beside()
                dve.wait_ge(dn_loaded, 48 * i + 48)
                for j in range(3):
                    w = V_CONV + 16 * j
                    if j == 2:
                        dve.wait_ge(dn_yst, 1 + 16 * i)
                    nc.vector.tensor_scalar(d_cv[j][:], d_in[j][:, 3:3 + S], cols[:, ds(w + 4 * i + 3, 1)], None, ALU.mult).then_inc(dn_conv, 1)
                    for tap in range(2, -1, -1):
                        dve.wait_ge(dn_conv, 12 * i + 4 * j + 3 - tap)
                        nc.vector.scalar_tensor_tensor(d_cv[j][:], d_in[j][:, tap:tap + S], cols[:, ds(w + 4 * i + tap, 1)], d_cv[j][:],
                                                       ALU.mult, ALU.add).then_inc(dn_conv, 1)
                    beside()
                nc.vector.tensor_copy(d_gB[:], bd_g[:, ds(i, 1), :].rearrange("p h n -> p (h n)")[:, :, None].broadcast_to([P, NCH, P])).then_inc(dn_chain, 1)
                nc.vector.tensor_copy(d_bB[:], bd_beta[:, ds(i, 1), :].rearrange("p h n -> p (h n)")[:, :, None].broadcast_to([P, NCH, P])).then_inc(dn_chain, 1)
                r = d_wt[:].rearrange("p n c -> p (n c)")
                for j in range(2):
                    dve.wait_ge(dn_root, 3 * i + j + 1)
                    nc.vector.scalar_tensor_tensor(d_cv[j][:], d_cv[j][:], P ** -0.5 if j == 0 else 1.0, r, ALU.mult, ALU.mult).then_inc(dn_chain, 1)
                    beside()
                dve.wait_ge(dn_chain, 1 + 4 * i + 4)

                def per_row(t, c):
                    return t[:, ds(i, 1), c].rearrange("p h n -> p (h n)")[:, :, None].broadcast_to([P, 4, P])

                def mask(m):
                    return m[:, None, :].broadcast_to([P, 4, P])

                def chained(ins):
                    local[0] += 1
                    ins.then_inc(dn_dve, 1)
                    dve.wait_ge(dn_dve, 3 + DVE_CHAIN * i + local[0])

                local = [0]
                for x, name in enumerate(DN_STAGES):
                    for g in range(2):
                        c = slice(4 * g, 4 * g + 4)
                        p3 = d_bank[g][:].rearrange("p (n c) -> p n c", c=P)
                        if name in ("rowg", "rowb", "gram", "qk", "kT", "vT") or name[0] == "y":
                            dve.wait_ge(dn_prod[g], DN_USES * i + 3 + x)
                        taken = DN_USES * i + 3 + x
                        if name == "rowg":
                            dve.wait_ge(dn_eg[g], 3 * i + 1)
                            nc.vector.tensor_tensor(d_dt[:, c, :], p3, per_row(bd_gc, c), ALU.subtract).then_inc(dn_taken[g], 1)
                            dve.wait_ge(dn_taken[g], 1 + taken)
                            chained(nc.vector.tensor_copy(d_tail[:, c], d_dt[:, c, P - 1]))
                            nc.vector.tensor_scalar(d_dt[:, c, :], d_dt[:, c, :], 0.0, None, ALU.min).then_inc(dn_min[g], 1)
                        elif name == "rowb":
                            dve.wait_ge(dn_eg[g], 3 * i + 3)
                            chained(nc.vector.tensor_tensor(d_dt[:, c, :], d_dt[:, c, :], mask(up_incl), ALU.mult))
                            nc.vector.tensor_tensor(d_at[:, c, :], p3, d_dt[:, c, :], ALU.mult).then_inc(dn_taken[g], 1)
                            dve.wait_ge(dn_taken[g], 1 + taken)
                            chained(nc.vector.tensor_tensor(d_at[:, c, :], d_at[:, c, :], mask(up_strict), ALU.mult))
                        elif name == "gram":
                            nc.vector.tensor_tensor(d_at[:, c, :], p3, d_at[:, c, :], ALU.mult).then_inc(dn_taken[g], 1)
                        elif name == "qk":
                            nc.vector.tensor_tensor(d_qk[:, c, :], p3, d_dt[:, c, :], ALU.mult).then_inc(dn_taken[g], 1)
                        elif name == "kT":
                            nc.vector.tensor_tensor(d_kb[:, c, :], p3, per_row(bd_egc, c), ALU.mult)
                            nc.vector.tensor_tensor(d_kt[:, c, :], p3, d_tail[:, c, None].broadcast_to([P, 4, P]), ALU.mult).then_inc(dn_taken[g], 1)
                        elif name == "vT":
                            nc.vector.tensor_tensor(d_vb[:, c, :], p3, per_row(bd_beta, c), ALU.mult).then_inc(dn_taken[g], 1)
                            chained(nc.vector.tensor_tensor(d_TT[:, c, :], d_at[:, c, :], mask(consts[:, C_LEV, :]), ALU.mult))
                            nc.vector.scalar_tensor_tensor(d_TT[:, c, :], d_TT[:, c, :], -1.0, mask(ident), ALU.mult, ALU.add).then_inc(dn_tt[g], 1)
                        if name[0] == "y":
                            nc.vector.tensor_tensor(d_TT[:, c, :], d_TT[:, c, :], p3, ALU.subtract).then_inc(dn_taken[g], 1)
                        beside()
                assert local[0] == DVE_CHAIN
                nc.vector.memset(d_S[:], 0.0).then_inc(dn_scan_ev, 1)
                for n in range(NCH):
                    dve.wait_ge(dn_scan_mm, 16 * i + 2 * n + 1)
                    nc.vector.tensor_copy(d_vn[:], d_bank[0][:, 0:P]).then_inc(dn_scan_ev, 1)
                    beside()
                    dve.wait_ge(dn_scan_mm, 16 * i + 2 * n + 2)
                    dve.wait_ge(dn_scan_ev, 17 * i + 2 * n + 2)
                    nc.vector.scalar_tensor_tensor(d_S[:], d_S[:], d_eg[:, n, P - 1:P], d_bank[0][:, P:2 * P],
                                                   ALU.mult, ALU.add).then_inc(dn_scan_ev, 1)
                    beside()
                for g in range(2):
                    beside()
                dve.wait_ge(dn_root, 3 * i + 3)
                nc.vector.scalar_tensor_tensor(d_o[:], d_o[:], cols[:, V_DNG:V_DNG + 1], r, ALU.mult, ALU.mult).then_inc(dn_out, 1)
                dve.wait_ge(dn_out, 2 * i + 1)
                dve.wait_ge(dn_silu, 4 * i + 4)
                nc.vector.tensor_tensor(d_o[:], d_o[:], d_z[:], ALU.mult).then_inc(dn_out, 1)
            end_phase(dve, 3)
            b8 = Beside(PAIR_SG, SG_SLOTS, (ACT.Identity,) * 4)
            dve_beside(dve, b8)
            for hf in range(2):
                dve.wait_ge(g_pe, hf + 1)
                nc.vector.tensor_scalar(g_mean[:, HALF * hf:HALF * hf + HALF], d_bank[hf][:], 1.0 / BW, None, ALU.mult).then_inc(g_chain, 1)
            dve_beside(dve, b8)
            dve.wait_ge(g_chain, 2)
            for b in range(4):
                for hf in range(2):
                    v = g_v[:, b, HALF * hf:HALF * hf + HALF]
                    nc.vector.tensor_tensor(v, v, g_mean[:, HALF * hf:HALF * hf + HALF], ALU.subtract).then_inc(g_chain, 1)
                    dve_beside(dve, b8)
            dve_beside(dve, b8)
            dve.wait_ge(gu_load, 32)
            for b in range(4):
                dve.wait_ge(g_chain, 13 + 4 * b)
                nc.vector.scalar_tensor_tensor(g_n[:], g_v[:, b, :], cols[:, V_LNG + b:V_LNG + b + 1], g_rstd[:], ALU.mult, ALU.mult).then_inc(g_chain, 1)
                dve.wait_ge(g_chain, 14 + 4 * b)
                nc.vector.tensor_scalar(g_n[:], g_n[:], cols[:, V_LNB + b:V_LNB + b + 1], None, ALU.add).then_inc(g_chain, 1)
                dve_beside(dve, b8)
                y = g_y[b % 2]
                if b >= 2:
                    dve.wait_ge(g_store[b % 2], 16)
                for hf in range(2):
                    t = slice(HALF * hf, HALF * hf + HALF)
                    dve.wait_ge(g_pe, 10 + 4 * b + 2 + hf + 1)
                    bias = cols[:, None, V_BSP + P * b:V_BSP + P * b + P].broadcast_to([P, 4, P])
                    nc.vector.tensor_tensor(y[:, t].rearrange("p (n c) -> p n c", c=P), d_bank[hf][:].rearrange("p (n c) -> p n c", c=P),
                                            bias, ALU.add).then_inc(g_chain, 1)
                dve.wait_ge(g_chain, 17 + 4 * b)
                nc.vector.tensor_tensor(y[:], y[:], g_u[:, b, :], ALU.mult).then_inc(g_out, 1)
                split_y_lo(dve, b)
                dve_beside(dve, b8)
            end_phase(dve, 4)
            for i in range(2):
                for q in range(6):
                    n, s = PAIR_BR + 3 * i + q // 2, q % 2
                    for r in range(4):
                        dd, hf = divmod(r, 2)
                        acc = m_acc[:, dd, HALF * hf:HALF * hf + HALF]
                        if r < 3:
                            dve.wait_ge(half_ready, 2 * PAIR_BR + 18 * i + 3 * q + r + 1)
                        else:
                            dve.wait_ge(blk_done[s], n + 1)
                        uses = 12 * i + 2 * q + dd
                        dve.wait_ge(gate_sig[hf], uses + 1)
                        first = q % 3 == 0
                        added = 16 * i + 8 * (q // 3) + 4 * (q % 3 - 1) + r
                        if first:
                            dve.wait_ge(ml_ready, 1 + 4 * i + 2 * (q // 3))
                        else:
                            dve.wait_ge(m_added, added)
                        nc.vector.tensor_tensor(acc if first else m_t[:], g_bank[hf][:], gate[hf][:], ALU.mult).then_inc(bank_read[hf], 1)
                        if not first:
                            dve.wait_ge(bank_read[hf], 1 + 2 * PAIR_BR + uses + 1)
                            nc.vector.tensor_tensor(acc, acc, m_t[:], ALU.add).then_inc(m_added, 1)
                        if i == 0 and q < 2 and r >= 2:
                            for y in range(2):
                                split_y_lo(dve, 4 * q + 2 * r + y)
                    split_lo(dve, n + 1, s)
                    if q % 3 == 2:
                        for dd in range(2):
                            d = 4 * i + 2 * (q // 3) + dd
                            dve.wait_ge(mh_ready, d + 1)
                            nc.vector.tensor_tensor(tile_of(act_lo, d), m_acc[:, dd, :], tile_of(act_hi, d).bitcast(f32), ALU.subtract).then_inc(ml_ready, 1)
            end_phase(dve, 5)
            nc.vector.memset(sum_sq[:], 0.0).then_inc(w_added, 1)
            with dve.Fori(0, 4) as i:
                for s in range(2):
                    split_lo(dve, PAIR_OUT + i + 1, s)
                    dve.wait_ge(w_sq, 2 * i + s + 1)
                    dve.wait_ge(w_added, 2 * i + s + 2)
                    nc.vector.tensor_tensor(sum_sq[:], sum_sq[:], n_sq[s][:], ALU.add).then_inc(w_added, 1)
            dve.wait_ge(rstd_ready, 2)
            for k in range(KT):
                nc.vector.scalar_tensor_tensor(mixed[:, k, :], mixed[:, k, :], cols[:, V_NORM + 8 + k:V_NORM + 9 + k], n_rstd[:],
                                               ALU.mult, ALU.mult).then_inc(n_chain, 1)
                if k % 2 == 0:
                    add_residual(nc.vector, k)
            dve.wait_ge(rstd_ready, 3)
            normalised(dve, 2, mixed, V_NORM + 16, n_rstd, n_h)
            end_phase(dve, 6)

            def ff_group(g, first=False, last=False):
                with dve.Fori(0, 4) as i:
                    for s in range(2):
                        n = PAIR_FF + 8 * g + i
                        for hf in range(2):
                            c = 16 * g + 4 * i + 2 * s + hf
                            t = slice(HALF * hf, HALF * hf + HALF)
                            dve.wait_ge(bank_read[hf], 1 + 2 * n + s + 1 + MIX_BRANCH)
                            nc.vector.tensor_tensor(f_t[hf][:], f_t[hf][:], f_t[hf][:], ALU.mult).then_inc(f_sqr, 1)
                            dve.wait_ge(f_hr, c + 1)
                            nc.vector.tensor_tensor(tile_of(f_lo, 2 * i + s)[:, t], f_t[hf][:], tile_of(f_hi, 2 * i + s)[:, t].bitcast(f32),
                                                    ALU.subtract).then_inc(f_lr, 1)
                        split_lo(dve, n + 1, s)
                def add_pair(i, split):
                    for s in range(2):
                        n = PAIR_FF + 8 * g + 4 + i
                        for hf in range(2):
                            acc = tile_of(mixed, 2 * i + s)[:, HALF * hf:HALF * hf + HALF]
                            wait_half(dve, n, s, hf, 2 * n + s + HALF_BRANCH)
                            if first:
                                nc.vector.tensor_copy(acc, g_bank[hf][:]).then_inc(bank_read[hf], 1)
                            else:
                                nc.vector.tensor_tensor(acc, acc, g_bank[hf][:], ALU.add).then_inc(bank_read[hf], 1)
                        if split:
                            split_lo(dve, n + 1, s)
                        if last:
                            for hf in range(2):
                                c, t = 4 * i + 2 * s + hf, slice(HALF * hf, HALF * hf + HALF)
                                dve.wait_ge(w_sq, 8 + c + 1)
                                dve.wait_ge(w_added, 11 + c)
                                nc.vector.tensor_tensor(sum_sq[:, t], sum_sq[:, t], f_sq[hf][:], ALU.add).then_inc(w_added, 1)

                if last:
                    nc.vector.memset(sum_sq[:], 0.0).then_inc(w_added, 1)
                with dve.Fori(0, 3 if last else 4) as i:
                    add_pair(i, True)
                if last:
                    add_pair(3, False)

            ff_group(0, first=True)
            with dve.Fori(1, 3) as g:
                ff_group(g)
            ff_group(3, last=True)
            end_phase(dve, 7)
            dve.wait_ge(rstd_ready, 4)
            for k in range(KT):
                nc.vector.scalar_tensor_tensor(mixed[:, k, :], mixed[:, k, :], cols[:, V_NORM + 24 + k:V_NORM + 25 + k], n_rstd[:],
                                               ALU.mult, ALU.mult).then_inc(n_chain, 1)
                if k % 2 == 0:
                    add_output(nc.vector, k)

        @block.gpsimd
        def _(pool):
            nc.gpsimd.memset(ones[:], 1.0).then_inc(ones_set, 1)
            nc.gpsimd.memset(eps, EPS).then_inc(ones_set, 1)
            for k in range(1, KT, 2):
                lower_part(nc.gpsimd, 0, k, hbuf)
            end_phase(pool, 1)
            nc.gpsimd.memset(a_k[:], 0.0).then_inc(pad_zero, 1)
            nc.gpsimd.memset(a_v[:], 0.0).then_inc(pad_zero, 1)
            with pool.Fori(0, 4) as i:
                for x in range(NST + 2):
                    if x >= 2 and is_diag(STEPS[x - 2][0], STEPS[x - 2][2]):
                        T, u, j = STEPS[x - 2]
                        c = first_col(T, j)
                        pool.wait_ge(a_ready, NST * i + x - 1)
                        nc.gpsimd.tensor_tensor(a_A[u][:, j, c:c + P], a_A[u][:, j, c:c + P], up_strict, ALU.mult).then_inc(a_masked, 1)
                    if 1 <= x < NST and not group_of(x - 1)[2]:
                        c = first_col(STEPS[x - 1][0], STEPS[x - 1][2])
                        pool.wait_ge(r_hi, N_R * i + R_BEFORE[x])
                        if x >= 3:
                            pool.wait_ge(cum_ready, NST * i + x - 1)
                        nc.gpsimd.tensor_tensor(a_R_lo[(x - 1) % 2][:, c:HALF], a_R[(x - 1) % 2][:, c:HALF],
                                                a_R_hi[(x - 1) % 2][:, c:HALF].bitcast(f32), ALU.subtract).then_inc(r_ready, 1)
                    if x < NST and not group_of(x)[2]:
                        c = first_col(STEPS[x][0], STEPS[x][2])
                        pool.wait_ge(sp_ready, NST * i + x + 1)
                        if group_of(x)[1]:
                            if x:
                                pool.wait_ge(r_ready, N_R * i + R_BEFORE[x])
                            settle(pool)
                            for R in a_R:
                                nc.gpsimd.memset(R[:, 0:c], 0.0)
                            nc.gpsimd.tensor_copy(a_R[x % 2][:, c:HALF], a_sp[x % 3][:, c:HALF]).then_inc(r_sum, 1)
                        else:
                            pool.wait_ge(r_sum, N_R * i + R_BEFORE[x])
                            if R_BEFORE[x] >= 2:
                                pool.wait_ge(r_ready, N_R * i + R_BEFORE[x] - 1)
                            nc.gpsimd.tensor_tensor(a_R[x % 2][:, c:HALF], a_R[(x - 1) % 2][:, c:HALF], a_sp[x % 3][:, c:HALF], ALU.add).then_inc(r_sum, 1)
            end_phase(pool, 2)
            with pool.Fori(0, 4) as i:
                for lev in range(1, N_LEV):
                    for g in range(2):
                        c = slice(4 * g, 4 * g + 4)
                        if lev == 1:
                            pool.wait_ge(dn_taken[g], 1 + DN_USES * i + 3 + DN_STAGES.index("gram"))
                        else:
                            pool.wait_ge(dn_prod[g], DN_USES * i + 3 + DN_STAGES.index(f"x{lev - 1}"))
                        nc.gpsimd.tensor_tensor(d_B[:, c, :], d_at[:, c, :], consts[:, None, C_LEV + lev, :].broadcast_to([P, 4, P]),
                                                ALU.mult).then_inc(dn_b[g], 1)
                    if lev == 1:
                        for g in range(2):
                            c = slice(4 * g, 4 * g + 4)
                            q3 = d_cv[0][:, HALF * g:HALF * g + HALF].rearrange("p (n c) -> p n c", c=P)
                            pool.wait_ge(dn_prod[g], DN_USES * i + 3 + DN_STAGES.index("qk"))
                            nc.gpsimd.tensor_tensor(q3, q3, d_eg[:, c, :], ALU.mult).then_inc(dn_q, 1)
            end_phase(pool, 3)
            pool.wait_ge(gw_load, 16)
            nc.gpsimd.tensor_tensor(g_w[:], g_w[:], up_incl[:, None, :].broadcast_to([P, 8, P]), ALU.mult).then_inc(g_masked, 1)
            end_phase(pool, 4)
            end_phase(pool, 5)
            for k in range(1, KT, 2):
                add_residual(nc.gpsimd, k)
            for k in range(1, KT, 2):
                lower_part(nc.gpsimd, 2, k, n_h)
            end_phase(pool, 6)
            end_phase(pool, 7)
            for k in range(1, KT, 2):
                add_output(nc.gpsimd, k)


def kernel(x, norm_g, w_in, b_in, sgu_ln_g, sgu_ln_b, w_spatial, b_spatial, conv_w, a_log, dt_bias, dn_norm_g,
           w_branch, w_out, w_ff1, w_ff2):
    import concourse.bacc as bacc
    from concourse.bass_utils import run_bass_kernel_spmd as run

    f = lambda a: np.asarray(a)
    x, w_in, b_in = f(x), f(w_in)[0], f(b_in)[0]
    w_branch, w_out, w_ff1, w_ff2 = f(w_branch)[0], f(w_out)[0], f(w_ff1)[0], f(w_ff2)[0]

    def tiles(w):
        r, c = w.shape
        return w.reshape(r // P, P, c // P, P).transpose(2, 1, 0, 3).reshape(c // P, P, r)

    starts = [c + P * t for c in (COL_SQ, COL_SQ + 512, COL_SQ + 1024,
                                  COL_DQ, COL_DQ + 512, COL_DQ + 1024, COL_DQ + 1536) for t in range(4)]
    for h in range(4):
        starts += [c + 256 * h + P * t for c in (COL_GATE, COL_GATE + 1024, COL_AU) for t in range(2)]
    starts += [COL_GATE + 2048 + P * t for t in range(8)]
    stream = [tiles(w_in[:, c:c + P]) for c in starts]
    for i in range(2):
        for q in range(6):
            c = 512 * i + 256 * (q // 3)
            stream.append(tiles(w_branch[BRANCHES[q % 3]][:, c:c + 256]).transpose(1, 0, 2).reshape(1, P, KT * P))
    stream.append(tiles(w_out))
    for g in range(4):
        stream.append(tiles(w_ff1[:, 1024 * g:1024 * g + 1024]))
        stream.append(tiles(w_ff2[1024 * g:1024 * g + 1024]))
    w_stream = np.ascontiguousarray(np.concatenate(stream).reshape(N_PAIRS, 2, P, KT * P))

    def by_partition(a):
        return a.reshape(-1, P).T

    def on_all(a):
        return np.broadcast_to(a.reshape(1, -1), (P, a.size))

    bsp = np.repeat(f(b_spatial)[0].reshape(4, 2, P), 64, axis=1)
    cw = f(conv_w)[0].reshape(4, 12, P).transpose(2, 1, 0).reshape(P, 48)
    cols = np.concatenate([
        by_partition(f(norm_g)[0]), np.stack([b_in[c:c + P] for c in starts], 1),
        by_partition(f(sgu_ln_g)[0]), by_partition(f(sgu_ln_b)[0]), cw, by_partition(f(dn_norm_g)[0]),
        on_all(f(a_log)[0]), on_all(f(dt_bias)[0]), on_all(b_in[COL_BETA:COL_BETA + 8]),
        bsp.transpose(1, 0, 2).reshape(P, 4 * P)], axis=1)

    p, c = np.arange(P)[:, None], np.arange(P)[None, :]
    levels = [(c >> (v + 1) == p >> (v + 1)) & ((c >> v) % 2 == 1) & ((p >> v) % 2 == 0) for v in range(N_LEV)]
    consts = np.stack([p == c, p <= c, p < c, p >= c, *levels], axis=1).astype(np.float32)

    arrays = {
        "xT": np.ascontiguousarray(x[0].T.reshape(KT, P, S)),
        "w_stream": w_stream,
        "w_bd": np.ascontiguousarray(w_in[:, COL_BETA:COL_BETA + 8].reshape(KT, P, 8).transpose(1, 0, 2)),
        "w_spT": np.ascontiguousarray(f(w_spatial)[0].transpose(2, 0, 1)),
        "cols_in": np.ascontiguousarray(cols),
        "consts_in": consts,
    }
    nc = bacc.Bacc("TRN2", target_bir_lowering=False, num_devices=1)
    f32 = mybir.dt.float32
    args = [nc.dram_tensor(n, a.shape, f32, kind="ExternalInput").ap() for n, a in arrays.items()]
    out = nc.dram_tensor("outT", (KT, P, S), f32, kind="ExternalOutput").ap()
    hybrid_decoder_layer(nc, *args, out)
    r = run(nc, [arrays], core_ids=[0])
    y = r.results[0]["outT"].reshape(D, S)
    return np.ascontiguousarray(y.T)[None]
```
